# Optimizing a Trainium2 kernel written in Bass

```python
import jax, jax.numpy as jnp
from jax import lax
import numpy as np

D_MODEL = 2048
BATCH = 1
SEQ = 256
DEPTH = 1

CHUNK = 64
N_MEM = 256
RMS_EPS = 1e-6

RW_HEADS = 16
RW_HEAD_DIM = 64
RW_WIDTH = RW_HEADS * RW_HEAD_DIM
RW_DECAY_LORA = 64
RW_AAA_LORA = 64
RW_GATE_LORA = 160
RW_GN_EPS = 64e-5
RW_COLS = 3 * RW_WIDTH + RW_DECAY_LORA + RW_AAA_LORA + RW_GATE_LORA

GDN_QK_HEADS = 4
GDN_V_HEADS = 8
GDN_HEAD_DIM = 128
GDN_QK_WIDTH = GDN_QK_HEADS * GDN_HEAD_DIM
GDN_V_WIDTH = GDN_V_HEADS * GDN_HEAD_DIM
GDN_CONV = 4
GDN_CONV_CH = 2 * GDN_QK_WIDTH + GDN_V_WIDTH
GDN_COLS = GDN_CONV_CH + GDN_V_WIDTH + 2 * GDN_V_HEADS

N_BRANCH = 2
BRANCH_WIDTH = 1024
GATE_COLS = N_BRANCH * D_MODEL
IN_COLS = RW_COLS + GDN_COLS + GATE_COLS

MEM_HEADS = 4
MEM_HEAD_DIM = D_MODEL // MEM_HEADS

D_FF = 5632

kernel_name = "rwkv7_gdn_macaron_hybrid"

def _split(t, sizes):
    return jnp.split(t, [int(s) for s in np.cumsum(sizes)[:-1]], axis=-1)

def _rmsnorm(x, g, eps=RMS_EPS):
    xf = x.astype(jnp.float32)
    y = xf * lax.rsqrt(jnp.mean(xf * xf, axis=-1, keepdims=True) + eps)
    return (y * g.astype(jnp.float32)).astype(x.dtype)

def _l2norm(x, eps=1e-6):
    xf = x.astype(jnp.float32)
    return xf * lax.rsqrt(jnp.sum(xf * xf, axis=-1, keepdims=True) + eps)

def _swiglu_ffn(x, norm_g, w_gate, w_up, w_down):
    h = _rmsnorm(x, norm_g)
    return (jax.nn.silu(h @ w_gate) * (h @ w_up)) @ w_down

def _token_shift(x):
    return jnp.pad(x, ((0, 0), (1, 0), (0, 0)))[:, :-1]

def _causal_depthwise_conv(x, w):
    K, C = w.shape
    return lax.conv_general_dilated(
        x, w[:, None, :], window_strides=(1,), padding=[(K - 1, 0)],
        dimension_numbers=("NWC", "WIO", "NWC"), feature_group_count=C)

def _rwkv7_recurrence(r, w, k, v, a, b):
    B_, T, H, N = r.shape

    def step(S, inp):
        r_t, w_t, k_t, v_t, a_t, b_t = inp
        sa = jnp.einsum("bhij,bhj->bhi", S, a_t)
        S = S * w_t[:, :, None, :] + sa[..., None] * b_t[:, :, None, :] + v_t[..., None] * k_t[:, :, None, :]
        return S, jnp.einsum("bhij,bhj->bhi", S, r_t)

    xs = tuple(jnp.moveaxis(t, 1, 0) for t in (r, w, k, v, a, b))
    _, y = lax.scan(step, jnp.zeros((B_, H, N, N), jnp.float32), xs)
    return jnp.moveaxis(y, 0, 1)

def _rwkv7_branch(cols, shift_mu, w0, w2, a0, a2, g2, k_k, k_a, r_k, ln_w, ln_b):
    B_, T, _ = cols.shape
    cols = cols + (_token_shift(cols) - cols) * shift_mu
    r, k, v, wl, al, gl = _split(cols, (RW_WIDTH, RW_WIDTH, RW_WIDTH, RW_DECAY_LORA, RW_AAA_LORA, RW_GATE_LORA))
    w_log = -jax.nn.softplus(-(w0 + jnp.tanh(wl) @ w2)) - 0.5
    a = jax.nn.sigmoid(a0 + al @ a2)
    g = jax.nn.sigmoid(gl) @ g2

    def heads(t):
        return t.reshape(B_, T, RW_HEADS, RW_HEAD_DIM).astype(jnp.float32)

    kk = _l2norm(heads(k * k_k))
    k = k * (1 + (a - 1) * k_a)
    r_h, k_h, v_h, a_h = heads(r), heads(k), heads(v), heads(a)
    decay = jnp.exp(-jnp.exp(heads(w_log)))
    y = _rwkv7_recurrence(r_h, decay, k_h, v_h, -kk, kk * a_h)
    mu = jnp.mean(y, axis=-1, keepdims=True)
    var = jnp.mean(jnp.square(y - mu), axis=-1, keepdims=True)
    y = ((y - mu) * lax.rsqrt(var + RW_GN_EPS)).reshape(B_, T, RW_WIDTH)
    y = y * ln_w.astype(jnp.float32) + ln_b.astype(jnp.float32)
    bonus = jnp.sum(r_h * k_h * r_k.astype(jnp.float32), axis=-1, keepdims=True) * v_h
    y = y + bonus.reshape(B_, T, RW_WIDTH)
    return (y * g.astype(jnp.float32)).astype(cols.dtype)

def _chunked_gated_delta_rule(q, k, v, g, beta):
    B_, T, H, Dk = q.shape
    Dv = v.shape[-1]
    nc = T // CHUNK

    def to_chunks(t):
        return t.reshape((B_, nc, CHUNK, H) + t.shape[3:]).swapaxes(2, 3)

    q, k, v, g, beta = map(to_chunks, (q, k, v, g, beta))
    gc = jnp.cumsum(g, axis=-1)
    idx = jnp.arange(CHUNK)
    lower = idx[:, None] >= idx[None, :]
    strict = idx[:, None] > idx[None, :]
    diff = gc[..., :, None] - gc[..., None, :]
    decay = jnp.where(lower, jnp.exp(jnp.where(lower, diff, 0.0)), 0.0)
    k_beta = k * beta[..., None]
    v_beta = v * beta[..., None]
    m = jnp.where(strict, jnp.einsum("bnhid,bnhjd->bnhij", k_beta, k) * decay, 0.0)
    tri = m + jnp.eye(CHUNK, dtype=m.dtype)
    u = lax.linalg.triangular_solve(tri, v_beta, left_side=True, lower=True, unit_diagonal=True)
    w = lax.linalg.triangular_solve(tri, k_beta * jnp.exp(gc)[..., None], left_side=True, lower=True, unit_diagonal=True)
    a_qk = jnp.where(lower, jnp.einsum("bnhid,bnhjd->bnhij", q, k) * decay, 0.0)

    def step(S, inp):
        q_c, k_c, u_c, w_c, a_c, gc_c = inp
        v_new = u_c - jnp.einsum("bhld,bhde->bhle", w_c, S)
        o = (jnp.einsum("bhld,bhde->bhle", q_c * jnp.exp(gc_c)[..., None], S)
             + jnp.einsum("bhij,bhje->bhie", a_c, v_new))
        g_last = gc_c[..., -1]
        S = (S * jnp.exp(g_last)[..., None, None]
             + jnp.einsum("bhld,bhle->bhde", k_c * jnp.exp(g_last[..., None] - gc_c)[..., None], v_new))
        return S, o

    xs = tuple(jnp.moveaxis(t, 1, 0) for t in (q, k, u, w, a_qk, gc))
    _, o = lax.scan(step, jnp.zeros((B_, H, Dk, Dv), jnp.float32), xs)
    return o.transpose(1, 0, 3, 2, 4).reshape(B_, T, H, Dv)

def _gdn_branch(cols, conv_w, a_log, dt_bias, norm_w):
    B_, T, _ = cols.shape
    qkv, z, b_raw, a_raw = _split(cols, (GDN_CONV_CH, GDN_V_WIDTH, GDN_V_HEADS, GDN_V_HEADS))
    qkv = jax.nn.silu(_causal_depthwise_conv(qkv.astype(jnp.float32), conv_w.astype(jnp.float32)))
    q, k, v = _split(qkv, (GDN_QK_WIDTH, GDN_QK_WIDTH, GDN_V_WIDTH))
    rep = GDN_V_HEADS // GDN_QK_HEADS
    q = jnp.repeat(_l2norm(q.reshape(B_, T, GDN_QK_HEADS, GDN_HEAD_DIM)), rep, axis=2) * (GDN_HEAD_DIM ** -0.5)
    k = jnp.repeat(_l2norm(k.reshape(B_, T, GDN_QK_HEADS, GDN_HEAD_DIM)), rep, axis=2)
    v = v.reshape(B_, T, GDN_V_HEADS, GDN_HEAD_DIM)
    beta = jax.nn.sigmoid(b_raw.astype(jnp.float32))
    g = -jnp.exp(a_log.astype(jnp.float32)) * jax.nn.softplus(a_raw.astype(jnp.float32) + dt_bias.astype(jnp.float32))
    o = _chunked_gated_delta_rule(q, k, v, g, beta)
    z = z.reshape(B_, T, GDN_V_HEADS, GDN_HEAD_DIM).astype(jnp.float32)
    o = o * lax.rsqrt(jnp.mean(o * o, axis=-1, keepdims=True) + RMS_EPS) * norm_w.astype(jnp.float32) * jax.nn.silu(z)
    return o.reshape(B_, T, GDN_V_WIDTH).astype(cols.dtype)

def _memory_cross_attention(h, mem, q_norm, kv_norm, w_mq, w_mk, w_mv, w_mo):
    B_, T, _ = h.shape
    hq = _rmsnorm(h, q_norm)
    mkv = _rmsnorm(mem, kv_norm)
    q = (hq @ w_mq).reshape(B_, T, MEM_HEADS, MEM_HEAD_DIM)
    k = (mkv @ w_mk).reshape(B_, -1, MEM_HEADS, MEM_HEAD_DIM)
    v = (mkv @ w_mv).reshape(B_, -1, MEM_HEADS, MEM_HEAD_DIM)
    s = jnp.einsum("bthd,bmhd->bhtm", q, k).astype(jnp.float32) * (MEM_HEAD_DIM ** -0.5)
    p = jax.nn.softmax(s, axis=-1).astype(v.dtype)
    o = jnp.einsum("bhtm,bmhd->bthd", p, v).reshape(B_, T, D_MODEL)
    return o @ w_mo

def setup_inputs(seed: int = 0) -> dict:
    key = jax.random.key(seed)
    ks = iter(jax.random.split(key, 48))
    L = DEPTH

    def nrm(shape, scale):
        return jax.random.normal(next(ks), shape, jnp.float32) * scale

    def gain(shape):
        return 1.0 + nrm(shape, 0.02)

    def unif(shape, lo, hi):
        return jax.random.uniform(next(ks), shape, jnp.float32, lo, hi)

    dt = jnp.exp(unif((L, GDN_V_HEADS), float(np.log(1e-3)), float(np.log(1e-1))))
    return {
        "x": nrm((BATCH, SEQ, D_MODEL), 1.0),
        "mem": nrm((BATCH, N_MEM, D_MODEL), 1.0),
        "ffn1_norm": gain((L, D_MODEL)),
        "ffn1_w_gate": nrm((L, D_MODEL, D_FF), D_MODEL ** -0.5),
        "ffn1_w_up": nrm((L, D_MODEL, D_FF), D_MODEL ** -0.5),
        "ffn1_w_down": nrm((L, D_FF, D_MODEL), D_FF ** -0.5),
        "mix_norm": gain((L, D_MODEL)),
        "w_in": nrm((L, D_MODEL, IN_COLS), D_MODEL ** -0.5),
        "rw_shift_mu": unif((L, RW_COLS), 0.0, 1.0),
        "rw_w0": unif((L, RW_WIDTH), -6.0, -1.0),
        "rw_w2": nrm((L, RW_DECAY_LORA, RW_WIDTH), 0.1 * RW_DECAY_LORA ** -0.5),
        "rw_a0": nrm((L, RW_WIDTH), 0.1),
        "rw_a2": nrm((L, RW_AAA_LORA, RW_WIDTH), 0.1 * RW_AAA_LORA ** -0.5),
        "rw_g2": nrm((L, RW_GATE_LORA, RW_WIDTH), RW_GATE_LORA ** -0.5),
        "rw_k_k": 0.85 + nrm((L, RW_WIDTH), 0.02),
        "rw_k_a": 1.0 + nrm((L, RW_WIDTH), 0.02),
        "rw_r_k": nrm((L, RW_HEADS, RW_HEAD_DIM), 0.1),
        "rw_ln_w": gain((L, RW_WIDTH)),
        "rw_ln_b": nrm((L, RW_WIDTH), 0.01),
        "gdn_conv_w": nrm((L, GDN_CONV, GDN_CONV_CH), GDN_CONV ** -0.5),
        "gdn_a_log": jnp.log(unif((L, GDN_V_HEADS), 1.0, 16.0)),
        "gdn_dt_bias": dt + jnp.log(-jnp.expm1(-dt)),
        "gdn_norm_w": gain((L, GDN_HEAD_DIM)),
        "w_lift": nrm((L, N_BRANCH, BRANCH_WIDTH, D_MODEL), BRANCH_WIDTH ** -0.5),
        "w_out": nrm((L, D_MODEL, D_MODEL), D_MODEL ** -0.5),
        "mem_q_norm": gain((L, D_MODEL)),
        "mem_kv_norm": gain((L, D_MODEL)),
        "w_mq": nrm((L, D_MODEL, D_MODEL), D_MODEL ** -0.5),
        "w_mk": nrm((L, D_MODEL, D_MODEL), D_MODEL ** -0.5),
        "w_mv": nrm((L, D_MODEL, D_MODEL), D_MODEL ** -0.5),
        "w_mo": nrm((L, D_MODEL, D_MODEL), D_MODEL ** -0.5),
        "ffn2_norm": gain((L, D_MODEL)),
        "ffn2_w_gate": nrm((L, D_MODEL, D_FF), D_MODEL ** -0.5),
        "ffn2_w_up": nrm((L, D_MODEL, D_FF), D_MODEL ** -0.5),
        "ffn2_w_down": nrm((L, D_FF, D_MODEL), D_FF ** -0.5),
        "final_norm": gain((D_MODEL,)),
    }

def reference(x, mem, ffn1_norm, ffn1_w_gate, ffn1_w_up, ffn1_w_down,
              mix_norm, w_in, rw_shift_mu, rw_w0, rw_w2, rw_a0, rw_a2, rw_g2,
              rw_k_k, rw_k_a, rw_r_k, rw_ln_w, rw_ln_b,
              gdn_conv_w, gdn_a_log, gdn_dt_bias, gdn_norm_w,
              w_lift, w_out,
              mem_q_norm, mem_kv_norm, w_mq, w_mk, w_mv, w_mo,
              ffn2_norm, ffn2_w_gate, ffn2_w_up, ffn2_w_down, final_norm):
    B_, T, _ = x.shape
    h = x
    for l in range(DEPTH):
        h = h + 0.5 * _swiglu_ffn(h, ffn1_norm[l], ffn1_w_gate[l], ffn1_w_up[l], ffn1_w_down[l])
        u = _rmsnorm(h, mix_norm[l])
        proj = u @ w_in[l]
        rw_cols, gdn_cols, gate_cols = _split(proj, (RW_COLS, GDN_COLS, GATE_COLS))
        y_rw = _rwkv7_branch(rw_cols, rw_shift_mu[l], rw_w0[l], rw_w2[l], rw_a0[l], rw_a2[l], rw_g2[l],
                             rw_k_k[l], rw_k_a[l], rw_r_k[l], rw_ln_w[l], rw_ln_b[l])
        y_gdn = _gdn_branch(gdn_cols, gdn_conv_w[l], gdn_a_log[l], gdn_dt_bias[l], gdn_norm_w[l])
        gates = jax.nn.sigmoid(gate_cols.reshape(B_, T, N_BRANCH, D_MODEL))
        merged = (gates[:, :, 0] * (y_rw @ w_lift[l, 0])
                  + gates[:, :, 1] * (y_gdn @ w_lift[l, 1]))
        h = h + merged @ w_out[l]
        h = h + _memory_cross_attention(h, mem, mem_q_norm[l], mem_kv_norm[l], w_mq[l], w_mk[l], w_mv[l], w_mo[l])
        h = h + 0.5 * _swiglu_ffn(h, ffn2_norm[l], ffn2_w_gate[l], ffn2_w_up[l], ffn2_w_down[l])
    return _rmsnorm(h, final_norm)


_drawn_inputs = setup_inputs


def setup_inputs(seed=0):
    import zlib

    import numpy as np

    out = dict(_drawn_inputs(seed))
    spreads = {}
    factors = {'ffn1_norm': 6.025,
     'mix_norm': 3.916,
     'rw_w2': 42.349,
     'rw_a0': 4.67,
     'rw_a2': 4.778,
     'rw_k_k': 200.0,
     'rw_k_a': 8.0,
     'rw_ln_w': 200.0,
     'rw_ln_b': 200.0,
     'gdn_norm_w': 36.435,
     'mem_q_norm': 8.0,
     'mem_kv_norm': 23.552,
     'ffn2_norm': 34.488,
     'final_norm': 24.489}
    for name, (base, spread) in spreads.items():
        noise = np.random.default_rng([zlib.crc32(name.encode()), seed]).standard_normal(out[name].shape)
        drawn = base * np.exp(spread * noise) if base else spread * noise
        out[name] = __import__('jax').numpy.asarray(drawn.astype(out[name].dtype))
    for name, factor in factors.items():
        out[name] = (out[name] * factor).astype(out[name].dtype)
    return out
```

```python
from contextlib import ExitStack

import concourse.bass as bass
from concourse import mybir

F32 = mybir.dt.float32
F32R = mybir.dt.float32r
ALU = mybir.AluOpType
ACT = mybir.ActivationFunctionType
AX_X = mybir.AxisListType.X
ds = bass.ds

P = 128
T = 256
TT = T // P
D = 2048
KT = D // P
F = 5632
FT = F // P
CW = 512
SK = 2
RING = 4
NFC = F // CW
NDC = D // CW
RMS_EPS = 1e-6
C = 64
NCH = T // C

RW = 1024
RH = 64
RW_GN_EPS = 64e-5
LORA_D, LORA_A, LORA_G = 64, 64, 160
LORA = LORA_D + LORA_A + LORA_G
RW_COLS = 3 * RW + LORA
GH = 128
GHV = 8
GQ = 512
GV = 1024
CONV = 4
GDN0 = RW_COLS
Z0 = GDN0 + 2 * GQ + GV
BA0 = Z0 + GV
GATE0 = BA0 + 2 * GHV
AUXW = LORA + 2 * GHV
MH = 4
MHD = D // MH
MHK = MHD // P
HALVES = 2
EXP_HALF = 0.6065306597126334

PRM_LIST = [("ffn1_norm", KT), ("mix_norm", KT), ("mem_q_norm", KT), ("mem_kv_norm", KT), ("ffn2_norm", KT),
            ("mu_rkv", 3 * RW // P), ("mu_wa", 1), ("mu_g0", 1), ("mu_g1", 1), None,
            ("w0", RW // P), ("a0", RW // P), ("k_k", RW // P), ("k_a", RW // P), ("r_k", RW // P),
            ("ln_w", RW // P), ("ln_b", RW // P), ("conv", CONV * 16), ("gdn_norm", 1)]
PRM = {}
_at = 0
for _entry in PRM_LIST:
    if _entry is None:
        _at = P
    else:
        PRM[_entry[0]] = _at
        _at += _entry[1]
NPRM = _at


def plan():
    prods, turns = {}, {}
    state = dict(p=0, slot=0, t=0, s=0, freed=[0, 0])
    last = [None, None]

    def products(phase, n, nk, ups=None):
        out = []
        for c in range(n):
            k = nk[c % len(nk)]
            par = state["p"] % 2
            if ups is not None and c % 2 == 1:
                released = ("nat_ready", ups + c // 2 + 1)
            else:
                state["freed"][par] += 1
                released = (("pair_free0", "pair_free1")[par], state["freed"][par])
            out.append(dict(par=par, slot=state["slot"], ns=k // SK, free=last[par], released=released,
                            done=state["slot"] + k // SK))
            last[par] = released
            state["p"] += 1
            state["slot"] += k // SK
        prods[phase] = out

    def turned(phase, n, split=True):
        turns[phase] = (state["t"], state["s"])
        state["t"] += n
        if split:
            state["s"] += n

    def ffn(tag):
        turned(tag + "norm", NDC)
        turned(tag + "act", NFC)
        products(tag + "gu", 2 * NFC, [KT], ups=turns[tag + "act"][0])
        products(tag + "dn", NDC, [FT])

    ffn("f1")
    turned("mixnorm", NDC)
    products("aux", 1, [KT])
    for hf in range(HALVES):
        products(f"gdn{hf}", 3, [KT])
    for hf in range(HALVES):
        products(f"rw{hf}", 3, [KT])
    products("lift", 4 * NDC, [KT, KT, 8, 8])
    turned("merged", NDC)
    products("out", NDC, [KT])
    turned("memnorm", NDC)
    products("mkv", 2 * NDC, [KT])
    turned("mk", NDC, False)
    turned("qnorm", NDC)
    products("mq", NDC, [KT])
    turned("mq", NDC, False)
    products("mo", NDC, [KT])
    ffn("f2")
    return prods, turns


def build(nc, A, stop=None):
    prods, turns = plan()
    with ExitStack() as ctx:
        sems = {}

        def sem(name):
            if name not in sems:
                sems[name] = ctx.enter_context(nc.semaphore(name))
            return sems[name]

        base = -(-nc.sbuf_base // 64) * 64
        ctx.enter_context(nc.sbuf_tensor("slab", [P, 207 * 256], F32))

        def at(name, kib, shape, dt=F32):
            return nc.alloc_sbuf_tensor_at(name, [P] + shape, dt, offset=int(base + kib * 1024))

        h = at("h", 0, [TT, D])
        raw = at("raw", 16, [RING, SK, CW])
        whi = at("whi", 32, [RING, SK, CW], F32R)
        wlo = at("wlo", 48, [RING, SK, CW], F32R)
        xhi = at("xhi", 64, [KT, T], F32R)
        xlo = at("xlo", 80, [KT, T], F32R)
        ident = at("ident", 96, [P])
        ones = at("ones", 96.5, [P])
        headones = at("headones", 97, [P])
        m_up = at("m_up", 97.5, [C])
        m_upd = at("m_upd", 97.75, [C])
        m_upo = at("m_upo", 98, [C])
        m_inc = at("m_inc", 98.25, [C])
        eye = at("eye", 98.5, [C])
        prm = at("prm", 98.75, [NPRM])
        scanmask = at("scanmask", 99.75, [T])
        sel = at("sel", 100.75, [GHV, P])
        AR = 105
        hhi = at("hhi", AR, [FT, T], F32R)
        hlo = at("hlo", AR + 44, [FT, T], F32R)
        nat = at("nat", 193, [TT, CW])
        gs = at("gs", 197, [TT, CW])
        xf = at("xf", 201, [4, T])
        ss = at("ss", 205, [TT, NDC])
        ssum = at("ssum", 205.0625, [TT])
        rms = at("rms", 205.125, [TT])
        rstd = at("rstd", 205.1875, [TT])
        epsn = at("epsn", 205.25, [1])
        scal = at("scal", 205.5, [16 * 24])

        pp = ctx.enter_context(nc.psum_tensor("pp", [P, 4, CW], F32))
        pa = ctx.enter_context(nc.psum_tensor("pa", [P, 4, T], F32))
        pb = ctx.enter_context(nc.psum_tensor("pb", [P, 4, T], F32))

        def pair(par):
            return pp[:, 2 * par:2 * par + 2, :]

        LOADED = [sem(f"loaded{s}") for s in range(RING)]
        whi_ready, wlo_ready, slot_used = sem("whi_ready"), sem("wlo_ready"), sem("slot_used")
        nat_ready, turned, xf_ready = sem("nat_ready"), sem("turned"), sem("xf_ready")
        hi_ready, x_ready = sem("hi_ready"), sem("x_ready")
        sumsq_ready, ms_ready, rms_ready = sem("sumsq_ready"), sem("ms_ready"), sem("rms_ready")
        x_loaded, prm_clear, prm_loaded = sem("x_loaded"), sem("prm_clear"), sem("prm_loaded")
        consts_ready, prm_turned, prm_ready, eps_ready = sem("consts_ready"), sem("prm_turned"), sem("prm_ready"), sem("eps_ready")
        stored = sem("stored")

        two_pieces = [prods[k][0]["slot"] for k in ("aux", "gdn0", "gdn1")]

        def slot_of(base_slot, j, i=0):
            n = base_slot + j
            twice = sum(min(max((n - first) // RING + 1, 0), 2) for first in two_pieces)
            return n % RING, n + 16 * i, 16 * (n // RING + 1 + twice) + 64 * i

        def wait_pair(eng, need):
            if need is not None:
                eng.wait_ge(sem(need[0]), need[1])

        def load_slot(sp, src, base_slot, j, i=0, width=CW):
            s, n, _ = slot_of(base_slot, j, i)
            if not (isinstance(n, int) and n < RING):
                sp.wait_ge(wlo_ready, n - RING + 1)
            dst = raw[:, s, :, :] if width == CW else raw[:, s, :, 0:width]
            sp.dma_start(dst, src).then_inc(LOADED[s], 16)

        def split_hi(act, base_slot, j, i=0, width=CW):
            s, n, ld = slot_of(base_slot, j, i)
            act.wait_ge(LOADED[s], ld)
            if not (isinstance(n, int) and n < RING):
                act.wait_ge(slot_used, n - RING + 1)
            nc.scalar.activation(whi[:, s, :, 0:width], raw[:, s, :, 0:width], ACT.Copy).then_inc(whi_ready, 1)

        def split_lo(dve, base_slot, j, i=0, width=CW):
            s, n, _ = slot_of(base_slot, j, i)
            dve.wait_ge(whi_ready, n + 1)
            nc.vector.tensor_tensor(wlo[:, s, :, 0:width], raw[:, s, :, 0:width],
                                    whi[:, s, :, 0:width].bitcast(F32), ALU.subtract).then_inc(wlo_ready, 1)

        def multiply(pe, pr, free, acts, i=0, width=CW, k0=0):
            wait_pair(pe, free)
            a_hi, a_lo = acts
            for j in range(pr["ns"]):
                s, n, _ = slot_of(pr["slot"], j, i)
                pe.wait_ge(wlo_ready, n + 1)
                for kk in range(SK):
                    k = j * SK + kk
                    first, final = k == 0, k == pr["ns"] * SK - 1
                    for tt in range(TT):
                        tok = slice(tt * P, (tt + 1) * P)
                        out = pp[:, 2 * pr["par"] + tt, 0:width]
                        w_hi, w_lo = whi[:, s, kk, 0:width], wlo[:, s, kk, 0:width]
                        nc.tensor.matmul(out, a_hi[:, k0 + k, tok], w_hi, start=first, stop=False)
                        nc.tensor.matmul(out, a_lo[:, k0 + k, tok], w_hi, start=False, stop=False)
                        mm = nc.tensor.matmul(out, a_hi[:, k0 + k, tok], w_lo, start=False, stop=final)
                mm.then_inc(slot_used, 1)

        def turn(pe, t, src_ready=None):
            if src_ready is None:
                pe.wait_ge(nat_ready, t + 1)
            else:
                pe.wait_ge(*src_ready)
            if not (isinstance(t, int) and t == 0):
                pe.wait_ge(xf_ready, t)
            for kk in range(4):
                for tt in range(TT):
                    mm = nc.tensor.transpose(pa[:, kk, tt * P:(tt + 1) * P], nat[:, tt, kk * P:(kk + 1) * P], ident[:, :])
            mm.then_inc(turned, 1)

        def take(dve, t, s, gain=None):
            dve.wait_ge(turned, t + 1)
            if not (isinstance(s, int) and s == 0):
                dve.wait_ge(hi_ready, s)
                dve.wait_ge(x_ready, s)
            if gain is None:
                nc.vector.tensor_copy(xf[:, :, :], pa[:, :, :]).then_inc(xf_ready, 1)
            else:
                for kk in range(4):
                    op = nc.vector.tensor_scalar(xf[:, kk, :], pa[:, kk, :], prm[:, gain + kk:gain + kk + 1], None, ALU.mult)
                op.then_inc(xf_ready, 1)

        def x_hi(act, t, dst):
            act.wait_ge(xf_ready, t + 1)
            nc.scalar.activation(dst, xf[:, :, :], ACT.Copy).then_inc(hi_ready, 1)

        def x_lo(dve, s, dst_hi, dst_lo):
            dve.wait_ge(hi_ready, s + 1)
            nc.vector.tensor_tensor(dst_lo, xf[:, :, :], dst_hi.bitcast(F32), ALU.subtract).then_inc(x_ready, 1)

        def sumsq(act, src, q, c):
            if NDC * q + c > 0:
                act.wait_ge(sumsq_ready, NDC * q + c)
            for tt in range(TT):
                op = nc.scalar.activation(gs[:, tt, :], src[:, tt, c * CW:(c + 1) * CW], ACT.Square,
                                          accum_out=ss[:, tt, c:c + 1])
            op.then_inc(sumsq_ready, 1)

        def norm_root(act, q):
            act.wait_ge(ms_ready, q + 1)
            nc.scalar.activation(rms[:, :], ssum[:, :], ACT.Sqrt, bias=epsn[:, 0:1], scale=1.0 / D).then_inc(rms_ready, 1)

        def norm_scale(dve, q):
            dve.wait_ge(sumsq_ready, NDC * (q + 1))
            nc.vector.tensor_reduce(ssum[:, :], ss[:, :, :], AX_X, ALU.add).then_inc(ms_ready, 1)
            dve.wait_ge(rms_ready, q + 1)
            link(dve, nc.vector.reciprocal(rstd[:, :], rms[:, :]))

        def norm_chunk(dve, src, c, t):
            if t > 0:
                dve.wait_ge(turned, t)
            for tt in range(TT):
                op = nc.vector.tensor_scalar(nat[:, tt, :], src[:, tt, c * CW:(c + 1) * CW], rstd[:, tt:tt + 1], None, ALU.mult)
            op.then_inc(nat_ready, 1)

        def norm_dve(dve, q, src, tag, gain):
            t, s = turns[tag]
            norm_scale(dve, q)
            for c in range(NDC):
                norm_chunk(dve, src, c, t + c)
                take(dve, t + c, s + c, PRM[gain] + 4 * c)
                x_lo(dve, s + c, xhi[:, 4 * c:4 * c + 4, :], xlo[:, 4 * c:4 * c + 4, :])

        def norm_act(act, q, tag):
            t, s = turns[tag]
            norm_root(act, q)
            for c in range(NDC):
                x_hi(act, t + c, xhi[:, 4 * c:4 * c + 4, :])

        def norm_pe(pe, tag):
            for c in range(NDC):
                turn(pe, turns[tag][0] + c)

        chain = {}

        def link(eng, ins):
            name = {dve_engine: "dve_chain", act_engine: "act_chain", pool_engine: "pool_chain"}[type(eng)]
            chain[name] = chain.get(name, 0) + 1
            ins.then_inc(sem(name), 1)
            eng.wait_ge(sem(name), chain[name])

        dve_engine, act_engine, pool_engine = type(nc.vector), type(nc.scalar), type(nc.gpsimd)

        def ffn_load(sp, tag, w_gate, w_up, w_down):
            gu, dn = prods[tag + "gu"], prods[tag + "dn"]

            def chunk(i):
                for m, w in enumerate((w_gate, w_up)):
                    for j in range(KT // SK):
                        src = w[j * SK * P:(j + 1) * SK * P, ds(i * CW, CW)].rearrange("(k p) n -> p k n", p=P)
                        load_slot(sp, src, gu[m]["slot"], j, i)

            chunk(0)
            with sp.Fori(1, NFC) as i:
                chunk(i)
            for c in range(NDC):
                for j in range(FT // SK):
                    src = w_down[j * SK * P:(j + 1) * SK * P, c * CW:(c + 1) * CW].rearrange("(k p) n -> p k n", p=P)
                    load_slot(sp, src, dn[c]["slot"], j)

        def ffn_pe(pe, tag):
            gu, dn = prods[tag + "gu"], prods[tag + "dn"]
            t0, s0 = turns[tag + "act"]

            def chunk(i, first):
                gate_free = gu[0]["free"] if first else (gu[0]["released"][0], gu[0]["released"][1] + i - 1)
                up_free = gu[1]["free"] if first else ("nat_ready", t0 + i)
                multiply(pe, gu[0], gate_free, (xhi, xlo), i)
                if not first:
                    turn(pe, t0 + i - 1)
                multiply(pe, gu[1], up_free, (xhi, xlo), i)

            pe.wait_ge(x_ready, turns[tag + "norm"][1] + NDC)
            chunk(0, True)
            with pe.Fori(1, NFC) as i:
                chunk(i, False)
            turn(pe, t0 + NFC - 1)
            pe.wait_ge(x_ready, s0 + NFC)
            for c in range(NDC):
                multiply(pe, dn[c], dn[c]["free"], (hhi, hlo))

        def ffn_act(act, tag):
            gu, dn = prods[tag + "gu"], prods[tag + "dn"]
            t0, s0 = turns[tag + "act"]

            def chunk(i, first):
                for j in range(RING if first else 0, KT // SK):
                    split_hi(act, gu[0]["slot"], j, i)
                for j in range(KT // SK):
                    split_hi(act, gu[1]["slot"], j, i)
                    if j == 4:
                        if not first:
                            x_hi(act, t0 + i - 1, hhi[:, ds(4 * i - 4, 4), :])
                        act.wait_ge(slot_used, gu[0]["done"] + 16 * i)
                        act.wait_ge(nat_ready, t0 + i)
                        nc.scalar.activation(gs[:, :, :], pair(gu[0]["par"]), ACT.Silu).then_inc(sem(gu[0]["released"][0]), 1)

            chunk(0, True)
            with act.Fori(1, NFC) as i:
                chunk(i, False)
            for j in range(RING):
                split_hi(act, dn[0]["slot"], j)
            x_hi(act, t0 + NFC - 1, hhi[:, 4 * NFC - 4:4 * NFC, :])
            for c in range(NDC):
                for j in range(RING if c == 0 else 0, FT // SK):
                    split_hi(act, dn[c]["slot"], j)
                    if c > 0 and j == 5:
                        act.wait_ge(sem(dn[c - 1]["released"][0]), dn[c - 1]["released"][1])
                        sumsq(act, h, 1 if tag == "f1" else 5, c - 1)

        def ffn_dve(dve, tag):
            gu, dn = prods[tag + "gu"], prods[tag + "dn"]
            t0, s0 = turns[tag + "act"]

            def gated(i):
                dve.wait_ge(slot_used, gu[1]["done"] + 16 * i)
                dve.wait_ge(sem(gu[0]["released"][0]), gu[0]["released"][1] + i)
                dve.wait_ge(turned, t0 + i)
                nc.vector.tensor_tensor(nat[:, :, :], gs[:, :, :], pair(gu[1]["par"]), ALU.mult).then_inc(nat_ready, 1)

            def chunk(i, first):
                for j in range(RING if first else 0, KT // SK):
                    split_lo(dve, gu[0]["slot"], j, i)
                    if j == 4 and not first:
                        gated(i - 1)
                for j in range(KT // SK):
                    split_lo(dve, gu[1]["slot"], j, i)
                    if j == 2 and not first:
                        take(dve, t0 + i - 1, s0 + i - 1)
                    if j == 6 and not first:
                        x_lo(dve, s0 + i - 1, hhi[:, ds(4 * i - 4, 4), :], hlo[:, ds(4 * i - 4, 4), :])

            chunk(0, True)
            with dve.Fori(1, NFC) as i:
                chunk(i, False)
            for j in range(RING):
                split_lo(dve, dn[0]["slot"], j)
            gated(NFC - 1)
            take(dve, t0 + NFC - 1, s0 + NFC - 1)
            x_lo(dve, s0 + NFC - 1, hhi[:, 4 * NFC - 4:4 * NFC, :], hlo[:, 4 * NFC - 4:4 * NFC, :])
            for c in range(NDC):
                for j in range(RING if c == 0 else 0, FT // SK):
                    split_lo(dve, dn[c]["slot"], j)
                    if c > 0 and j == 4:
                        residual(dve, dn[c - 1], c - 1, 0.5)

        def residual(dve, pr, c, scale):
            dve.wait_ge(slot_used, pr["done"])
            hc = h[:, :, c * CW:(c + 1) * CW]
            nc.vector.scalar_tensor_tensor(hc, pair(pr["par"]), scale, hc, ALU.mult, ALU.add).then_inc(sem(pr["released"][0]), 1)

        auxt = at("auxt", AR, [3, T + 1])
        lora = at("lora", AR + 3.25, [3, T])
        beta_t = at("beta_t", AR + 6.25, [T])
        gc_t = at("gc_t", AR + 7.25, [T])
        sp_a = at("sp_a", AR + 8.25, [T])
        sp_b = at("sp_b", AR + 9.25, [T])
        qkp = at("qkp", AR + 10.25, [4, T + CONV - 1])
        vp = at("vp", AR + 14.5, [4, T + CONV - 1])
        zg = at("zg", AR + 18.75, [TT, CW])
        qk = at("qk", AR + 22.75, [4, T])
        vg = at("vg", AR + 26.75, [4, T])
        kb = at("kb", AR + 30.75, [4, T])
        qe = at("qe", AR + 34.75, [4, T])
        eg = at("eg", AR + 38.75, [4, T])
        bb = at("bb", AR + 42.75, [4, T])
        kn = at("kn", AR + 46.75, [TT, 2 * P])
        vb = at("vb", AR + 48.75, [TT, CW])
        dec = at("dec", AR + 52.75, [8, C])
        att = at("att", AR + 54.75, [8, C])
        ut_g = at("ut_g", AR + 56.75, [8, C])
        s_g = at("s_g", AR + 58.75, [4, GH])
        r_g = at("r_g", AR + 60.75, [4, GH])
        vn_g = at("vn_g", AR + 62.75, [4, GH])
        vs_g = at("vs_g", AR + 64.75, [4, GH])
        o_g = at("o_g", AR + 66.75, [TT, CW])
        sq_g = at("sq_g", AR + 70.75, [4, T])
        ri_g = at("ri_g", AR + 74.75, [4, T])
        inv_g = [at(f"inv_g{k}", AR + kib, [8, C]) for k, kib in enumerate((10.25, 12.25, 14.25, 16.25, 78.75, 80.75))]
        w2z = at("w2z", AR + 6.25, [CW])
        a2z = at("a2z", AR + 8.25, [CW])
        g2a = at("g2a", AR + 10.25, [CW])
        g2b = at("g2b", AR + 12.25, [CW])
        rkv = [at(f"rkv{m}", AR + kib, [4, T + 1]) for m, kib in enumerate((14.25, 18.5, 22.75))]
        az = at("az", AR + 27, [4, 2, T])
        rz = at("rz", AR + 35, [4, 2, T])
        bt = at("bt", AR + 43, [4, T])
        kt = at("kt", AR + 47, [4, T])
        gt = at("gt", AR + 51, [4, T])
        tmp = [at(f"tmp{m}", AR + 55 + 4 * m, [4, T]) for m in range(8)]
        bn = at("bn", AR + 55, [TT, CW])
        kn_r = at("kn_r", AR + 59, [TT, CW])
        vn_r = at("vn_r", AR + 63, [TT, CW])
        ut_r = at("ut_r", AR + 67, [TT, 8, C])
        ak = at("ak", AR + 71, [TT, 8, C])
        rb = at("rb", AR + 75, [TT, 8, C])
        rk = at("rk", AR + 79, [TT, 8, C])
        r_r = at("r_r", AR + 14.25, [8, C])
        sa_r = at("sa_r", AR + 16.25, [8, C])
        y_r = at("y_r", AR + 18.5, [TT, CW])
        bonus = at("bonus", AR + 22.75, [4, T])
        s_r = at("s_r", AR, [2, 4, C])
        inv_r = [at(f"inv_r{k}", AR + kib, [8, C]) for k, kib in enumerate((83, 85, 6.25, 8.25, 10.25, 12.25))]
        yf = at("yf", AR, [16, T])
        yhi = at("yhi", AR + 16, [16, T], F32R)
        ylo = at("ylo", AR + 32, [16, T], F32R)
        mhi = at("mhi", AR + 48, [KT, T], F32R)
        mlo = at("mlo", AR + 64, [KT, T], F32R)
        ga = at("ga", AR + 80, [TT, CW])
        gb = at("gb", AR + 84, [TT, CW])
        msb = at("msb", AR, [TT, D])
        qt = at("qt", AR, [KT, T])
        kt_m = at("kt_m", AR + 16, [KT, T])
        v_m = at("v_m", AR + 32, [TT, D])
        pr_m = at("pr_m", AR + 80, [2, TT, T])
        pt_m = at("pt_m", AR + 84, [2, TT, T])

        gc_n = scal[:, 0:16].rearrange("p (t g) -> p t g", t=TT)
        be_n = scal[:, 16:32].rearrange("p (t g) -> p t g", t=TT)
        nbe_n = scal[:, 32:48].rearrange("p (t g) -> p t g", t=TT)
        dtb, nal = scal[0:GHV, 48:49], scal[0:GHV, 49:50]
        eps_q, eps_k, eps_gn, one_c = scal[:, 50:51], scal[:, 51:52], scal[:, 52:53], scal[:, 53:54]
        msum = scal[:, 64:80]
        mroot = scal[:, 80:96]
        msum2 = scal[:, 96:112]
        mroot2 = scal[:, 112:128]
        pc = scal[:, 128:144].rearrange("p (d c) -> p d c", d=4)
        mx = scal[:, 144:152].rearrange("p (g t) -> p g t", g=MH)
        nmx = scal[:, 152:160].rearrange("p (g t) -> p g t", g=MH)
        den = scal[:, 160:168].rearrange("p (g t) -> p g t", g=MH)
        rden = scal[:, 168:176].rearrange("p (g t) -> p g t", g=MH)

        y_turned = nc.dram_tensor("y_turned", (16, P, T), F32, kind="Internal").ap()

        bank = [pa[:, 0:2, :], pa[:, 2:4, :], pb[:, 0:2, :], pb[:, 2:4, :]]
        units = [b.rearrange("p a (u c) -> p (a u) c", c=C) for b in bank]
        heads4 = [b.rearrange("p a (u c) -> p (a u) c", c=GH) for b in bank]

        def over_units(mask):
            return mask[:, :].unsqueeze(1).to_broadcast([P, 8, C])

        INV_MM, INV_DVE, INV_ACT = 10, 9, 7

        def copy(act, dst, src):
            return nc.scalar.activation(dst, src, ACT.Copy)

        def invert_pe(pe, v, buf):
            a, b, c, d, e, f = buf
            mm_done, by_dve, by_act = sem("inv_mm"), sem("inv_dve"), sem("inv_act")
            dv, ac = INV_DVE * v, INV_ACT * v

            def blocks(out, lhs, rhs):
                for u in range(8):
                    for cp in range(2):
                        r = slice(cp * C, (cp + 1) * C)
                        right = rhs[r, u, :] if rhs is not eye else eye[r, :]
                        mm = nc.tensor.matmul(out[r, u, :], lhs[r, u, :], right, start=True, stop=True)
                return mm

            pe.wait_ge(sem("inv_in"), v + 1)
            blocks(units[0], a, eye).then_inc(mm_done, 1)
            pe.wait_ge(by_act, ac + 1)
            blocks(units[1], b, a)
            blocks(units[2], a, b).then_inc(mm_done, 1)
            pe.wait_ge(by_dve, dv + 2)
            pe.wait_ge(by_act, ac + 2)
            blocks(units[0], d, c)
            blocks(units[3], c, d)
            blocks(units[1], d, e).then_inc(mm_done, 1)
            pe.wait_ge(by_dve, dv + 4)
            pe.wait_ge(by_act, ac + 3)
            blocks(units[2], a, b)
            blocks(units[0], b, e).then_inc(mm_done, 1)
            pe.wait_ge(by_dve, dv + 5)
            pe.wait_ge(by_act, ac + 4)
            blocks(units[1], c, e).then_inc(mm_done, 1)
            pe.wait_ge(by_dve, dv + 6)
            blocks(units[2], e, eye).then_inc(mm_done, 1)
            pe.wait_ge(by_act, ac + 5)
            blocks(units[0], d, f)
            blocks(units[3], f, d).then_inc(mm_done, 1)
            pe.wait_ge(by_dve, dv + 7)
            pe.wait_ge(by_act, ac + 6)
            blocks(units[2], a, b).then_inc(mm_done, 1)
            pe.wait_ge(by_act, ac + 7)
            blocks(units[1], c, e).then_inc(mm_done, 1)
            pe.wait_ge(by_dve, dv + 8)
            blocks(units[0], b, d).then_inc(mm_done, 1)

        def invert_act(act, v, buf):
            a, b, c, d, e, f = buf
            for step, dst, u in ((1, b, 0), (2, d, 2), (3, b, 3), (4, c, 2), (6, d, 2), (7, b, 3), (8, c, 2)):
                act.wait_ge(sem("inv_mm"), INV_MM * v + step)
                copy(act, dst[:, :, :], units[u]).then_inc(sem("inv_act"), 1)

        def invert_dve(dve, v, buf, out):
            a, b, c, d, e, f = buf

            def step(n, ins_of):
                dve.wait_ge(sem("inv_mm"), INV_MM * v + n)
                ins_of().then_inc(sem("inv_dve"), 1)

            v_ = nc.vector
            v_.tensor_tensor(e[:, :, :], a[:, :, :], over_units(eye), ALU.add).then_inc(sem("inv_dve"), 1)
            step(2, lambda: v_.tensor_copy(c[:, :, :], units[1]))
            step(3, lambda: v_.tensor_copy(a[:, :, :], units[0]))
            step(3, lambda: v_.tensor_tensor(e[:, :, :], e[:, :, :], units[1], ALU.add))
            step(4, lambda: v_.tensor_tensor(e[:, :, :], e[:, :, :], units[0], ALU.add))
            step(5, lambda: v_.tensor_tensor(e[:, :, :], e[:, :, :], units[1], ALU.add))
            step(7, lambda: v_.tensor_copy(a[:, :, :], units[0]))
            step(9, lambda: v_.tensor_tensor(d[:, :, :], e[:, :, :], units[1], ALU.add))
            step(10, lambda: v_.tensor_tensor(out, d[:, :, :], units[0], ALU.add))
            dve.wait_ge(sem("inv_dve"), INV_DVE * (v + 1))

        def mix_nat(dve, pr, m):
            dve.wait_ge(slot_used, pr["done"])
            if m > 0:
                dve.wait_ge(sem("mix_turned"), m)
            nc.vector.tensor_copy(nat[:, :, :], pair(pr["par"])).then_inc(sem(pr["released"][0]), 1)

        def mix_turn(pe, pr, m):
            pe.wait_ge(sem(pr["released"][0]), pr["released"][1])
            if m > 0:
                pe.wait_ge(sem("mix_take"), m)
            for kk in range(4):
                for tt in range(TT):
                    mm = nc.tensor.transpose(pa[:, kk, tt * P:(tt + 1) * P], nat[:, tt, kk * P:(kk + 1) * P], ident[:, :])
            mm.then_inc(sem("mix_turned"), 1)

        def mix_take(dve, dst, m):
            dve.wait_ge(sem("mix_turned"), m + 1)
            nc.vector.tensor_copy(dst, pa[:, :, :]).then_inc(sem("mix_take"), 1)
            dve.wait_ge(sem("mix_take"), m + 1)

        AUX = prods["aux"][0]

        def aux_pe(pe):
            multiply(pe, AUX, AUX["free"], (xhi, xlo), width=AUXW)
            pe.wait_ge(sem(AUX["released"][0]), AUX["released"][1])
            for tt in range(TT):
                tok = slice(tt * P, (tt + 1) * P)
                nc.tensor.transpose(pa[:, 0, tok], nat[:, tt, 0:P], ident[:, :])
                nc.tensor.transpose(pa[:, 1, tok], nat[:, tt, P:2 * P], ident[:, :])
                nc.tensor.transpose(pa[0:32, 2, tok], nat[:, tt, 2 * P:LORA], ident[:, :])
                nc.tensor.transpose(pa[0:GHV, 3, tok], nat[:, tt, LORA:LORA + GHV], ident[:, :])
                mm = nc.tensor.transpose(pb[0:GHV, 0, tok], nat[:, tt, LORA + GHV:AUXW], ident[:, :])
            mm.then_inc(sem("aux_turned"), 1)
            pe.wait_ge(sem("gc_ready"), 1)
            for tt in range(TT):
                tok = slice(tt * P, (tt + 1) * P)
                nc.tensor.transpose(pb[:, 2, 8 * tt:8 * tt + 8], gc_t[0:GHV, tok], ident[0:GHV, 0:GHV])
                mm = nc.tensor.transpose(pb[:, 2, 16 + 8 * tt:24 + 8 * tt], beta_t[0:GHV, tok], ident[0:GHV, 0:GHV])
            mm.then_inc(sem("scalars_turned"), 1)

        def aux_dve(dve):
            v_ = nc.vector
            for cell, value in ((eps_q, RMS_EPS * GH), (eps_k, RMS_EPS), (eps_gn, RW_GN_EPS), (one_c, 1.0)):
                link(dve, v_.memset(cell, value))
            dve.wait_ge(slot_used, AUX["done"])
            v_.tensor_copy(nat[:, :, 0:AUXW], pair(AUX["par"])[:, :, 0:AUXW]).then_inc(sem(AUX["released"][0]), 1)
            link(dve, v_.memset(auxt[:, :, :], 0.0))
            dve.wait_ge(sem("aux_turned"), 1)
            v_.tensor_copy(auxt[:, 0:2, 1:T + 1], pa[:, 0:2, :])
            link(dve, v_.tensor_copy(auxt[0:32, 2, 1:T + 1], pa[0:32, 2, :]))
            link(dve, v_.tensor_tensor(lora[:, :, :], auxt[:, :, 0:T], auxt[:, :, 1:T + 1], ALU.subtract))
            for m, name in enumerate(("mu_wa", "mu_g0", "mu_g1")):
                op = v_.scalar_tensor_tensor(lora[:, m, :], lora[:, m, :], prm[:, PRM[name]:PRM[name] + 1],
                                             auxt[:, m, 1:T + 1], ALU.mult, ALU.add)
            op.then_inc(sem("lora_mixed"), 1)
            dve.wait_ge(sem("gdn_loaded"), 32)
            v_.tensor_copy(beta_t[0:GHV, :], pa[0:GHV, 3, :]).then_inc(sem("beta_raw"), 1)
            link(dve, v_.tensor_scalar(sp_a[0:GHV, :], pb[0:GHV, 0, :], dtb, None, ALU.add))
            link(dve, v_.tensor_scalar(gc_t[0:GHV, :], sp_a[0:GHV, :], -1.0, None, ALU.mult))
            v_.tensor_tensor(sp_b[0:GHV, :], sp_a[0:GHV, :], gc_t[0:GHV, :], ALU.max).then_inc(sem("abs_ready"), 1)
            dve.wait_ge(sem("ln_ready"), 1)
            link(dve, v_.scalar_tensor_tensor(sp_a[0:GHV, :], sp_a[0:GHV, :], 0.0, sp_b[0:GHV, :], ALU.max, ALU.add))
            link(dve, v_.tensor_scalar(nal, nal, -1.0, None, ALU.mult))
            link(dve, v_.tensor_scalar(sp_a[0:GHV, :], sp_a[0:GHV, :], nal, None, ALU.mult))
            v_.tensor_tensor_scan(gc_t[0:GHV, :], scanmask[0:GHV, :], sp_a[0:GHV, :], 0.0, ALU.mult, ALU.add).then_inc(sem("gc_ready"), 1)
            dve.wait_ge(sem("scalars_turned"), 1)
            v_.tensor_copy(scal[:, 0:32], pb[:, 2, 0:32]).then_inc(sem("scalars_ready"), 1)
            dve.wait_ge(sem("exp_gc"), 1)
            link(dve, v_.scalar_tensor_tensor(scal[:, 32:48], scal[:, 32:48], -1.0, scal[:, 16:32], ALU.mult, ALU.mult))

        def aux_act(act):
            act.wait_ge(sem("lora_mixed"), 1)
            nc.scalar.activation(lora[0:LORA_D, 0, :], lora[0:LORA_D, 0, :], ACT.Tanh)
            nc.scalar.activation(lora[:, 1:3, :], lora[:, 1:3, :], ACT.Sigmoid)
            act.wait_ge(sem("beta_raw"), 1)
            link(act, nc.scalar.activation(beta_t[0:GHV, :], beta_t[0:GHV, :], ACT.Sigmoid))
            act.wait_ge(sem("gdn_loaded"), 32)
            link(act, nc.scalar.activation(nal, nal, ACT.Exp))
            act.wait_ge(sem("abs_ready"), 1)
            link(act, nc.scalar.activation(sp_b[0:GHV, :], sp_b[0:GHV, :], ACT.Exp, scale=-1.0))
            nc.scalar.activation(sp_b[0:GHV, :], sp_b[0:GHV, :], ACT.Ln, bias=one_c[0:GHV, :]).then_inc(sem("ln_ready"), 1)
            act.wait_ge(sem("scalars_ready"), 1)
            nc.scalar.activation(scal[:, 32:48], scal[:, 0:16], ACT.Exp).then_inc(sem("exp_gc"), 1)

        def gdn_pe(pe, hf):
            g = prods[f"gdn{hf}"]
            n = hf + 1
            multiply(pe, g[0], g[0]["free"], (xhi, xlo))
            multiply(pe, g[1], g[1]["free"], (xhi, xlo))
            mix_turn(pe, g[0], 2 * hf)
            multiply(pe, g[2], g[2]["free"], (xhi, xlo))
            mix_turn(pe, g[1], 2 * hf + 1)
            pe.wait_ge(sem("g_sq"), n)
            for kk in range(4):
                mm = nc.tensor.matmul(pb[:, kk, :], ones[:, :], sq_g[:, kk, :], start=True, stop=True)
            mm.then_inc(sem("g_norms"), 1)
            pe.wait_ge(sem("mix_take"), 2 * n)
            pe.wait_ge(sem("g_rooted"), n)
            for hl in range(4):
                hv = 4 * hf + hl
                nc.tensor.matmul(pa[:, hl, :], sel[0:GHV, hv, :], gc_t[0:GHV, :], start=True, stop=True)
                mm = nc.tensor.matmul(pb[:, hl, :], sel[0:GHV, hv, :], beta_t[0:GHV, :], start=True, stop=True)
            mm.then_inc(sem("g_rows"), 1)
            pe.wait_ge(sem("g_qk"), n)
            pe.wait_ge(sem("g_dec"), n)
            pe.wait_ge(sem("g_vact"), n)
            for tt in range(TT):
                tok = slice(tt * P, (tt + 1) * P)
                for kk in range(2):
                    nc.tensor.transpose(bank[2][:, tt, kk * P:(kk + 1) * P], qk[:, 2 + kk, tok], ident[:, :])
                for kk in range(4):
                    mm = nc.tensor.transpose(bank[tt][:, kk // 2, (kk % 2) * P:(kk % 2 + 1) * P], vg[:, kk, tok], ident[:, :])
            mm.then_inc(sem("g_naturals"), 1)
            pe.wait_ge(sem("g_kb"), n)
            for u in range(8):
                tt, hl = u // 4, u % 4
                for cp in range(2):
                    r = slice(cp * C, (cp + 1) * C)
                    tok = slice(tt * P + cp * C, tt * P + (cp + 1) * C)
                    nc.tensor.matmul(units[2][r, u, :], qk[:, 2 + hl // 2, tok], kb[:, hl, tok], start=True, stop=True)
                    mm = nc.tensor.matmul(units[3][r, u, :], qk[:, 2 + hl // 2, tok], qk[:, hl // 2, tok], start=True, stop=True)
            mm.then_inc(sem("g_mats"), 1)
            invert_pe(pe, hf, inv_g)
            pe.wait_ge(sem("inv_dve"), INV_DVE * n)
            for c in range(NCH):
                tt, cp = c // 2, c % 2
                r = slice(cp * C, (cp + 1) * C)
                tok = slice(c * C, (c + 1) * C)
                m = NCH * hf + c
                pe.wait_ge(sem("g_state"), m + hf + 1)
                for hl in range(4):
                    mm = nc.tensor.matmul(heads4[0][r, hl, :], qk[:, 2 + hl // 2, tok], s_g[:, hl, :], start=True, stop=True)
                mm.then_inc(sem("g_ks"), 1)
                pe.wait_ge(sem("g_r"), m + 1)
                for hl in range(4):
                    mm = nc.tensor.matmul(heads4[1][r, hl, :], ut_g[r, 4 * tt + hl, :], r_g[r, hl, :], start=True, stop=True)
                mm.then_inc(sem("g_vnew"), 1)
                pe.wait_ge(sem("g_vn"), m + 1)
                if m > 0:
                    pe.wait_ge(sem("g_o"), m)
                for hl in range(4):
                    nc.tensor.matmul(heads4[2][r, hl, :], qe[:, hl, tok], s_g[:, hl, :], start=True, stop=False)
                    mm = nc.tensor.matmul(heads4[2][r, hl, :], att[r, 4 * tt + hl, :], vn_g[r, hl, :], start=False, stop=True)
                mm.then_inc(sem("g_omm"), 1)
                for hl in range(4):
                    mm = nc.tensor.matmul(heads4[3][:, hl, :], kn[r, tt, (hl // 2) * P:(hl // 2 + 1) * P], vs_g[r, hl, :],
                                          start=True, stop=True)
                mm.then_inc(sem("g_ds"), 1)
            pe.wait_ge(sem("g_out"), n)
            for kk in range(4):
                for tt in range(TT):
                    mm = nc.tensor.transpose(pa[:, kk, tt * P:(tt + 1) * P], nat[:, tt, kk * P:(kk + 1) * P], ident[:, :])
            mm.then_inc(sem("g_out_turned"), 1)

        def gdn_act(act, hf):
            g = prods[f"gdn{hf}"]
            n = hf + 1
            for m in range(3):
                for j in range(RING if m == 0 else 0, KT // SK):
                    split_hi(act, g[m]["slot"], j)
            act.wait_ge(slot_used, g[2]["done"])
            nc.scalar.activation(zg[:, :, :], pair(g[2]["par"]), ACT.Silu).then_inc(sem(g[2]["released"][0]), 1)
            act.wait_ge(sem("g_conv"), 2 * hf + 1)
            link(act, nc.scalar.activation(qk[:, :, :], qk[:, :, :], ACT.Silu))
            nc.scalar.activation(sq_g[:, :, :], qk[:, :, :], ACT.Square).then_inc(sem("g_sq"), 1)
            act.wait_ge(sem("g_conv"), 2 * n)
            nc.scalar.activation(vg[:, :, :], vg[:, :, :], ACT.Silu).then_inc(sem("g_vact"), 1)
            act.wait_ge(sem("g_norms"), n)
            nc.scalar.activation(ri_g[:, 0:2, :], pb[:, 0:2, :], ACT.Sqrt, bias=eps_q, scale=float(GH))
            nc.scalar.activation(ri_g[:, 2:4, :], pb[:, 2:4, :], ACT.Sqrt, bias=eps_k).then_inc(sem("g_rooted"), 1)
            act.wait_ge(sem("g_rows"), n)
            nc.scalar.activation(eg[:, :, :], pa[:, :, :], ACT.Exp)
            copy(act, bb[:, :, :], pb[:, :, :]).then_inc(sem("g_eg"), 1)
            act.wait_ge(sem("g_diff"), n)
            nc.scalar.activation(dec[:, :, :], dec[:, :, :], ACT.Exp).then_inc(sem("g_decexp"), 1)
            invert_act(act, hf, inv_g)
            for c in range(NCH):
                tt, cp = c // 2, c % 2
                r = slice(cp * C, (cp + 1) * C)
                act.wait_ge(sem("g_omm"), NCH * hf + c + 1)
                op = copy(act, o_g[r, tt, :], heads4[2][r, :, :].rearrange("p h d -> p (h d)"))
                op.then_inc(sem("g_o"), 1)
            act.wait_ge(sem("g_o"), NCH * n)
            nc.scalar.activation(sq_g[:, :, :].rearrange("p a t -> p (a t)"), o_g[:, :, :].rearrange("p t d -> p (t d)"),
                                 ACT.Square).then_inc(sem("g_osq"), 1)
            act.wait_ge(sem("g_oms"), n)
            nc.scalar.activation(mroot[:, 0:8], msum[:, 0:8], ACT.Sqrt, bias=eps_k, scale=1.0 / GH).then_inc(sem("g_oroot"), 1)

        def gdn_dve(dve, hf):
            g = prods[f"gdn{hf}"]
            n = hf + 1
            v_ = nc.vector
            for j in range(RING, KT // SK):
                split_lo(dve, g[0]["slot"], j)
            for j in range(KT // SK):
                split_lo(dve, g[1]["slot"], j)
                if j == 4:
                    mix_nat(dve, g[0], 2 * hf)
            link(dve, v_.memset(qkp[:, :, :], 0.0))
            link(dve, v_.memset(vp[:, :, :], 0.0))
            for j in range(KT // SK):
                split_lo(dve, g[2]["slot"], j)
                if j == 4:
                    mix_take(dve, qkp[:, :, CONV - 1:], 2 * hf)
                    mix_nat(dve, g[1], 2 * hf + 1)
            mix_take(dve, vp[:, :, CONV - 1:], 2 * hf + 1)

            def conv(dst, src, tiles):
                for kk, tile in enumerate(tiles):
                    for tap in range(CONV):
                        w = prm[:, PRM["conv"] + 16 * tap + tile:PRM["conv"] + 16 * tap + tile + 1]
                        x = src[:, kk, tap:tap + T]
                        if tap == 0:
                            link(dve, v_.tensor_scalar(dst[:, kk, :], x, w, None, ALU.mult))
                        elif tap < CONV - 1:
                            link(dve, v_.scalar_tensor_tensor(dst[:, kk, :], x, w, dst[:, kk, :], ALU.mult, ALU.add))
                        else:
                            op = v_.scalar_tensor_tensor(dst[:, kk, :], x, w, dst[:, kk, :], ALU.mult, ALU.add)
                op.then_inc(sem("g_conv"), 1)

            conv(qk, qkp, [2 * hf, 2 * hf + 1, 4 + 2 * hf, 5 + 2 * hf])
            conv(vg, vp, [8 + 4 * hf + k for k in range(4)])
            dve.wait_ge(sem("g_conv"), 2 * n)
            dve.wait_ge(sem("g_rooted"), n)
            link(dve, v_.reciprocal(ri_g[:, :, :], ri_g[:, :, :]))
            v_.tensor_tensor(qk[:, :, :], qk[:, :, :], ri_g[:, :, :], ALU.mult).then_inc(sem("g_qk"), 1)
            dve.wait_ge(sem("g_eg"), n)
            for tt in range(TT):
                for cp in range(2):
                    r = slice(cp * C, (cp + 1) * C)
                    tok = slice(tt * P + cp * C, tt * P + (cp + 1) * C)
                    own = gc_n[r, tt, 4 * hf:4 * hf + 4].unsqueeze(2).to_broadcast([C, 4, C])
                    op = v_.tensor_tensor(dec[r, 4 * tt:4 * tt + 4, :], pa[r, :, tok], own, ALU.subtract)
            link(dve, op)
            v_.tensor_scalar(dec[:, :, :], dec[:, :, :], 0.0, None, ALU.min).then_inc(sem("g_diff"), 1)
            dve.wait_ge(sem("g_decexp"), n)
            v_.tensor_tensor(dec[:, :, :], dec[:, :, :], over_units(m_inc), ALU.mult).then_inc(sem("g_dec"), 1)
            dve.wait_ge(sem("g_qk"), n)
            for hl in range(4):
                v_.tensor_tensor(kb[:, hl, :], qk[:, 2 + hl // 2, :], bb[:, hl, :], ALU.mult)
                v_.tensor_tensor(qe[:, hl, :], qk[:, hl // 2, :], eg[:, hl, :], ALU.mult)
            dve.wait_ge(sem("g_naturals"), n)
            v_.tensor_copy(kn[:, :, :], bank[2])
            for tt in range(TT):
                own = be_n[:, tt, 4 * hf:4 * hf + 4].unsqueeze(2).to_broadcast([P, 4, GH])
                op = v_.tensor_tensor(vb[:, tt, :].rearrange("p (h d) -> p h d", h=4), heads4[tt], own, ALU.mult)
            op.then_inc(sem("g_kb"), 1)
            dve.wait_ge(sem("g_mats"), n)
            dve.wait_ge(sem("g_dec"), n)
            v_.tensor_tensor(att[:, :, :], units[3], dec[:, :, :], ALU.mult)
            link(dve, v_.scalar_tensor_tensor(inv_g[1][:, :, :], units[2], -1.0, dec[:, :, :], ALU.mult, ALU.mult))
            v_.tensor_tensor(inv_g[5][:, :, :], inv_g[1][:, :, :], over_units(m_upo), ALU.mult)
            v_.tensor_tensor(inv_g[0][:, :, :], inv_g[1][:, :, :], over_units(m_upd), ALU.mult).then_inc(sem("inv_in"), 1)
            dve.wait_ge(sem("inv_in"), n)
            invert_dve(dve, hf, inv_g, ut_g[:, :, :])
            v_.memset(s_g[:, :, :], 0.0).then_inc(sem("g_state"), 1)
            for c in range(NCH):
                tt, cp = c // 2, c % 2
                r = slice(cp * C, (cp + 1) * C)
                m = NCH * hf + c
                own = nbe_n[r, tt, 4 * hf:4 * hf + 4].unsqueeze(2).to_broadcast([C, 4, GH])
                dve.wait_ge(sem("g_ks"), m + 1)
                link(dve, v_.tensor_tensor(r_g[r, :, :], heads4[0][r, :, :], own, ALU.mult))
                v_.tensor_tensor(r_g[r, :, :], r_g[r, :, :], vb[r, tt, :].rearrange("p (h d) -> p h d", h=4), ALU.add).then_inc(sem("g_r"), 1)
                dve.wait_ge(sem("g_vnew"), m + 1)
                v_.tensor_copy(vn_g[r, :, :], heads4[1][r, :, :])
                last = dec[r, 4 * tt:4 * tt + 4, C - 1:C].to_broadcast([C, 4, GH])
                v_.tensor_tensor(vs_g[r, :, :], heads4[1][r, :, :], last, ALU.mult).then_inc(sem("g_vn"), 1)
                dve.wait_ge(sem("g_ds"), m + 1)
                for hl in range(4):
                    end = (c + 1) * C - 1
                    op = v_.scalar_tensor_tensor(s_g[:, hl, :], s_g[:, hl, :], eg[:, hl, end:end + 1], heads4[3][:, hl, :],
                                                 ALU.mult, ALU.add)
                op.then_inc(sem("g_state"), 1)
            dve.wait_ge(sem("g_osq"), n)
            v_.tensor_reduce(msum[:, 0:8], sq_g[:, :, :].rearrange("p a (h d) -> p (a h) d", d=GH), AX_X, ALU.add).then_inc(sem("g_oms"), 1)
            dve.wait_ge(sem("g_oroot"), n)
            link(dve, v_.reciprocal(mroot2[:, 0:8], mroot[:, 0:8]))
            link(dve, v_.tensor_tensor(o_g[:, :, :].rearrange("p t (h d) -> p (t h) d", d=GH),
                                       o_g[:, :, :].rearrange("p t (h d) -> p (t h) d", d=GH),
                                       mroot2[:, 0:8].unsqueeze(2).to_broadcast([P, 8, GH]), ALU.mult))
            dve.wait_ge(sem(g[2]["released"][0]), g[2]["released"][1])
            dve.wait_ge(sem("mix_turned"), 2 * n)
            v_.tensor_tensor(nat[:, :, :], o_g[:, :, :], zg[:, :, :], ALU.mult).then_inc(sem("g_out"), 1)
            dve.wait_ge(sem("g_out_turned"), n)
            if hf > 0:
                dve.wait_ge(sem("y_stored"), 16 * hf)
            v_.tensor_scalar(xf[:, :, :], pa[:, :, :], prm[:, PRM["gdn_norm"]:PRM["gdn_norm"] + 1], None, ALU.mult).then_inc(sem("y_ready"), 1)
            dve.wait_ge(sem("y_ready"), n)

        def rw_pe(pe, hf):
            g = prods[f"rw{hf}"]
            n = hf + 1
            m0 = 2 * HALVES + 3 * hf
            multiply(pe, g[0], g[0]["free"], (xhi, xlo))
            multiply(pe, g[1], g[1]["free"], (xhi, xlo))
            if hf == 0:
                pe.wait_ge(sem("y_ready"), HALVES)
            mix_turn(pe, g[0], m0)
            multiply(pe, g[2], g[2]["free"], (xhi, xlo))
            mix_turn(pe, g[1], m0 + 1)
            mix_turn(pe, g[2], m0 + 2)
            pe.wait_ge(sem("mix_take"), m0 + 3)
            pe.wait_ge(sem("lora_loaded"), 64 * n)
            for dt in range(4):
                cols = slice(dt * P, (dt + 1) * P)
                nc.tensor.matmul(pa[:, dt, :], w2z[:, cols], lora[:, 0, :], start=True, stop=True)
                mm = nc.tensor.matmul(pb[:, dt, :], a2z[:, cols], lora[:, 0, :], start=True, stop=True)
            mm.then_inc(sem("r_lora"), 1)
            pe.wait_ge(sem("r_sig"), n)
            for dt in range(4):
                cols = slice(dt * P, (dt + 1) * P)
                nc.tensor.matmul(pa[:, dt, :], g2a[:, cols], lora[:, 1, :], start=True, stop=False)
                mm = nc.tensor.matmul(pa[:, dt, :], g2b[0:32, cols], lora[0:32, 2, :], start=False, stop=True)
            mm.then_inc(sem("r_g"), 1)
            pe.wait_ge(sem("r_kksq"), n)
            for dt in range(4):
                mm = nc.tensor.matmul(pb[:, dt, :], headones[:, :], gs_t[:, dt, :], start=True, stop=True)
            mm.then_inc(sem("r_kknorm"), 1)
            pe.wait_ge(sem("r_rkk"), n)
            pe.wait_ge(sem("r_gt"), n)
            for dt in range(4):
                mm = nc.tensor.matmul(pa[:, dt, :], headones[:, :], nat_t[:, dt, :], start=True, stop=True)
            mm.then_inc(sem("r_bonus"), 1)
            pe.wait_ge(sem("r_tilde"), n)
            for k, (src, banks, need) in enumerate(((bt, bank[2:4], None), (kt, bank[0:2], "r_bonus_out"), (tmp[2], bank[2:4], "r_nat"))):
                if need is not None:
                    pe.wait_ge(sem(need), n if need == "r_bonus_out" else 3 * hf + 1)
                for tt in range(TT):
                    for dt in range(4):
                        mm = nc.tensor.transpose(banks[tt][:, dt // 2, (dt % 2) * P:(dt % 2 + 1) * P],
                                                 src[:, dt, tt * P:(tt + 1) * P], ident[:, :])
                mm.then_inc(sem("r_nat_turned"), 1)
            for tt in range(TT):
                v = HALVES + TT * hf + tt
                if tt == 0:
                    pe.wait_ge(sem("r_nat"), 3 * n)
                else:
                    pe.wait_ge(sem("inv_dve"), INV_DVE * v)
                for u in range(8):
                    for cp in range(2):
                        r = slice(cp * C, (cp + 1) * C)
                        tok = slice(tt * P + cp * C, tt * P + (cp + 1) * C)
                        for k, (left, right) in enumerate(((bt, az), (bt, rz), (kt, az), (kt, rz))):
                            mm = nc.tensor.matmul(units[k][r, u, :], left[:, u // 2, tok], right[:, u // 2, u % 2, tok],
                                                  start=True, stop=True)
                mm.then_inc(sem("r_mats"), 1)
                invert_pe(pe, v, inv_r)
            pe.wait_ge(sem("inv_dve"), INV_DVE * (HALVES + TT * n))
            for c in range(NCH):
                tt, cp = c // 2, c % 2
                r = slice(cp * C, (cp + 1) * C)
                tok = slice(c * C, (c + 1) * C)
                m = NCH * hf + c
                s_in = s_r[:, c % 2, :, :]
                pe.wait_ge(sem("r_state"), m + hf + 1)
                for u in range(8):
                    nc.tensor.matmul(units[0][r, u, :], az[:, u // 2, u % 2, tok], s_in[:, u // 2, :], start=True, stop=False)
                    mm = nc.tensor.matmul(units[0][r, u, :], ak[r, tt, u, :], vn_r[r, tt, u * C:(u + 1) * C], start=False, stop=True)
                mm.then_inc(sem("r_rmm"), 1)
                pe.wait_ge(sem("r_r"), m + 1)
                for u in range(8):
                    mm = nc.tensor.matmul(units[1][r, u, :], ut_r[r, tt, u, :], r_r[r, u, :], start=True, stop=True)
                mm.then_inc(sem("r_samm"), 1)
                pe.wait_ge(sem("r_sa"), m + 1)
                for u in range(8):
                    out = heads_state[(u % 2) * C:(u % 2 + 1) * C, u // 2, :]
                    cols = slice(u * C, (u + 1) * C)
                    nc.tensor.matmul(out, bn[r, tt, cols], sa_r[r, u, :], start=True, stop=False)
                    mm = nc.tensor.matmul(out, kn_r[r, tt, cols], vn_r[r, tt, cols], start=False, stop=True)
                mm.then_inc(sem("r_ds"), 1)
                if m > 0:
                    pe.wait_ge(sem("r_y"), m)
                for u in range(8):
                    cols = slice(u * C, (u + 1) * C)
                    nc.tensor.matmul(units[2][r, u, :], rz[:, u // 2, u % 2, tok], s_in[:, u // 2, :], start=True, stop=False)
                    nc.tensor.matmul(units[2][r, u, :], rb[r, tt, u, :], sa_r[r, u, :], start=False, stop=False)
                    mm = nc.tensor.matmul(units[2][r, u, :], rk[r, tt, u, :], vn_r[r, tt, cols], start=False, stop=True)
                mm.then_inc(sem("r_ymm"), 1)
            pe.wait_ge(sem("r_out"), n)
            for kk in range(4):
                for tt in range(TT):
                    mm = nc.tensor.transpose(pa[:, kk, tt * P:(tt + 1) * P], nat[:, tt, kk * P:(kk + 1) * P], ident[:, :])
            mm.then_inc(sem("r_out_turned"), 1)

        def rw_act(act, hf):
            g = prods[f"rw{hf}"]
            n = hf + 1
            for m in range(3):
                for j in range(RING if m == 0 else 0, KT // SK):
                    split_hi(act, g[m]["slot"], j)
            act.wait_ge(sem("r_lora"), n)
            for dt in range(4):
                b = 4 * hf + dt
                nc.scalar.activation(tmp[3][:, dt, :], pa[:, dt, :], ACT.Sigmoid, bias=prm[:, PRM["w0"] + b:PRM["w0"] + b + 1])
            for dt in range(4):
                b = 4 * hf + dt
                op = nc.scalar.activation(tmp[4][:, dt, :], pb[:, dt, :], ACT.Sigmoid, bias=prm[:, PRM["a0"] + b:PRM["a0"] + b + 1])
            op.then_inc(sem("r_sig"), 1)
            act.wait_ge(sem("r_g"), n)
            copy(act, gt[:, :, :], pa[:, :, :]).then_inc(sem("r_gt"), 1)
            act.wait_ge(sem("r_kk0"), n)
            nc.scalar.activation(gs_t[:, :, :], xf[:, :, :], ACT.Square).then_inc(sem("r_kksq"), 1)
            act.wait_ge(sem("r_kknorm"), n)
            nc.scalar.activation(gs_t[:, :, :], pb[:, :, :], ACT.Sqrt, bias=eps_k).then_inc(sem("r_kkroot"), 1)
            act.wait_ge(sem("r_cum"), n)
            nc.scalar.activation(tmp[6][:, :, :], tmp[5][:, :, :], ACT.Exp)
            nc.scalar.activation(tmp[7][:, :, :], tmp[5][:, :, :], ACT.Exp, scale=-1.0).then_inc(sem("r_exp"), 1)
            act.wait_ge(sem("r_cumx"), n)
            nc.scalar.activation(tmp[5][:, :, :], tmp[5][:, :, :], ACT.Exp).then_inc(sem("r_expx"), 1)
            for tt in range(TT):
                invert_act(act, HALVES + TT * hf + tt, inv_r)
            for c in range(NCH):
                tt, cp = c // 2, c % 2
                r = slice(cp * C, (cp + 1) * C)
                m = NCH * hf + c
                act.wait_ge(sem("r_rmm"), m + 1)
                copy(act, r_r[r, :, :], units[0][r, :, :]).then_inc(sem("r_r"), 1)
                act.wait_ge(sem("r_samm"), m + 1)
                copy(act, sa_r[r, :, :], units[1][r, :, :]).then_inc(sem("r_sa"), 1)
                act.wait_ge(sem("r_ymm"), m + 1)
                copy(act, y_r[r, tt, :], units[2][r, :, :].rearrange("p u c -> p (u c)")).then_inc(sem("r_y"), 1)
            act.wait_ge(sem("r_cent"), n)
            nc.scalar.activation(gs[:, :, :], y_r[:, :, :], ACT.Square).then_inc(sem("r_centsq"), 1)
            act.wait_ge(sem("r_var"), n)
            nc.scalar.activation(mroot[:, :], msum[:, :], ACT.Sqrt, bias=eps_gn, scale=1.0 / RH).then_inc(sem("r_std"), 1)

        def rw_dve(dve, hf):
            g = prods[f"rw{hf}"]
            n = hf + 1
            m0 = 2 * HALVES + 3 * hf
            v_ = nc.vector

            def col(name, dt):
                k = PRM[name] + 4 * hf + dt
                return prm[:, k:k + 1]

            if hf == 0:
                link(dve, v_.memset(az[:, :, :, :], 0.0))
                link(dve, v_.memset(rz[:, :, :, :], 0.0))
            link(dve, v_.memset(w2z[:, :], 0.0))
            v_.memset(a2z[:, :], 0.0).then_inc(sem("lora_clear"), 1)
            for m in range(3):
                link(dve, v_.memset(rkv[m][:, :, 0:1], 0.0))
            for j in range(RING, KT // SK):
                split_lo(dve, g[0]["slot"], j)
            for j in range(KT // SK):
                split_lo(dve, g[1]["slot"], j)
                if j == 4:
                    dve.wait_ge(sem("g_out_turned" if hf == 0 else "r_out_turned"), HALVES if hf == 0 else hf)
                    mix_nat(dve, g[0], m0)
            for j in range(KT // SK):
                split_lo(dve, g[2]["slot"], j)
                if j == 4:
                    mix_take(dve, rkv[0][:, :, 1:T + 1], m0)
                    mix_nat(dve, g[1], m0 + 1)
            mix_take(dve, rkv[1][:, :, 1:T + 1], m0 + 1)
            mix_nat(dve, g[2], m0 + 2)
            mix_take(dve, rkv[2][:, :, 1:T + 1], m0 + 2)
            for m in range(3):
                link(dve, v_.tensor_tensor(tmp[m][:, :, :], rkv[m][:, :, 0:T], rkv[m][:, :, 1:T + 1], ALU.subtract))
                for dt in range(4):
                    k = PRM["mu_rkv"] + 8 * m + 4 * hf + dt
                    op = v_.scalar_tensor_tensor(tmp[m][:, dt, :], tmp[m][:, dt, :], prm[:, k:k + 1], rkv[m][:, dt, 1:T + 1],
                                                 ALU.mult, ALU.add)
                link(dve, op)
            r_, k_, v__, sg, a_, cum, ecum, encum = tmp
            dve.wait_ge(sem("y_stored"), 16 * (HALVES + hf))
            for dt in range(4):
                op = v_.tensor_scalar(xf[:, dt, :], k_[:, dt, :], col("k_k", dt), None, ALU.mult)
            op.then_inc(sem("r_kk0"), 1)
            dve.wait_ge(sem("r_sig"), n)
            link(dve, v_.tensor_scalar(sg[:, :, :], sg[:, :, :], -EXP_HALF, None, ALU.mult))
            for dt in range(4):
                op = v_.tensor_tensor_scan(cum[:, dt, :], scanmask[:, :], sg[:, dt, :], 0.0, ALU.mult, ALU.add)
            op.then_inc(sem("r_cum"), 1)
            dve.wait_ge(sem("r_exp"), n)
            v_.tensor_tensor(cum[:, :, :], cum[:, :, :], sg[:, :, :], ALU.subtract).then_inc(sem("r_cumx"), 1)
            dve.wait_ge(sem("r_cumx"), n)
            for dt in range(4):
                op = v_.tensor_scalar(sg[:, dt, :], a_[:, dt, :], 1.0, col("k_a", dt), ALU.subtract, ALU.mult)
            link(dve, op)
            link(dve, v_.scalar_tensor_tensor(k_[:, :, :], sg[:, :, :], 1.0, k_[:, :, :], ALU.add, ALU.mult))
            for dt in range(4):
                op = v_.scalar_tensor_tensor(nat_t[:, dt, :], r_[:, dt, :], col("r_k", dt), k_[:, dt, :], ALU.mult, ALU.mult)
            op.then_inc(sem("r_rkk"), 1)
            v_.tensor_copy(pc, ecum[:, :, :].rearrange("p d (c t) -> p d c t", t=C)[:, :, :, C - 1])
            v_.tensor_tensor(kt[:, :, :], k_[:, :, :], encum[:, :, :], ALU.mult)
            for e in range(2):
                half = slice(e * C, (e + 1) * C)
                v_.tensor_tensor(rz[half, :, e, :], r_[half, :, :], ecum[half, :, :], ALU.mult)
            dve.wait_ge(sem("r_kkroot"), n)
            link(dve, v_.reciprocal(gs_t[:, :, :], gs_t[:, :, :]))
            link(dve, v_.tensor_tensor(xf[:, :, :], xf[:, :, :], gs_t[:, :, :], ALU.mult))
            link(dve, v_.tensor_tensor(gs_t[:, :, :], xf[:, :, :], a_[:, :, :], ALU.mult))
            v_.tensor_tensor(bt[:, :, :], gs_t[:, :, :], encum[:, :, :], ALU.mult)
            dve.wait_ge(sem("r_expx"), n)
            for e in range(2):
                half = slice(e * C, (e + 1) * C)
                op = v_.scalar_tensor_tensor(az[half, :, e, :], xf[half, :, :], -1.0, cum[half, :, :], ALU.mult, ALU.mult)
            op.then_inc(sem("r_tilde"), 1)
            dve.wait_ge(sem("r_bonus"), n)
            v_.tensor_tensor(bonus[:, :, :], pa[:, :, :], v__[:, :, :], ALU.mult).then_inc(sem("r_bonus_out"), 1)
            dve.wait_ge(sem("r_tilde"), n)
            for k, (dst, lo, hi) in enumerate(((bn, 2, 4), (kn_r, 0, 2), (vn_r, 2, 4))):
                dve.wait_ge(sem("r_nat_turned"), 3 * hf + k + 1)
                src = (pa, pb)[lo // 2][:, :, :].rearrange("p a t -> p (a t)")
                v_.tensor_copy(dst[:, :, :].rearrange("p t d -> p (t d)"), src).then_inc(sem("r_nat"), 1)
            for tt in range(TT):
                v = HALVES + TT * hf + tt
                dve.wait_ge(sem("r_mats"), TT * hf + tt + 1)
                for dst, k, mask in ((inv_r[5][:, :, :], 0, m_upo), (rb[:, tt, :, :], 1, m_inc), (ak[:, tt, :, :], 2, m_up),
                                     (rk[:, tt, :, :], 3, m_inc)):
                    v_.tensor_tensor(dst, units[k], over_units(mask), ALU.mult)
                v_.tensor_tensor(inv_r[0][:, :, :], units[0], over_units(m_upd), ALU.mult).then_inc(sem("inv_in"), 1)
                dve.wait_ge(sem("inv_in"), v + 1)
                invert_dve(dve, v, inv_r, ut_r[:, tt, :, :])
            v_.memset(s_r[:, 0, :, :], 0.0).then_inc(sem("r_state"), 1)
            dve.wait_ge(sem("r_state"), (NCH + 1) * hf + 1)
            for c in range(NCH):
                m = NCH * hf + c
                dve.wait_ge(sem("r_ds"), m + 1)
                if m > 0 and c > 0:
                    dve.wait_ge(sem("r_ymm"), m)
                s_in, s_out = s_r[:, c % 2, :, :], s_r[:, (c + 1) % 2, :, :]
                link(dve, v_.tensor_tensor(s_out, s_in, heads_state, ALU.add))
                v_.tensor_tensor(s_out, s_out, pc[:, :, c:c + 1].to_broadcast([P, 4, C]), ALU.mult).then_inc(sem("r_state"), 1)
                dve.wait_ge(sem("r_state"), m + hf + 2)
            dve.wait_ge(sem("r_y"), NCH * n)
            yv = y_r[:, :, :].rearrange("p t (h c) -> p (t h) c", c=RH)
            link(dve, v_.tensor_reduce(msum2[:, :], yv, AX_X, ALU.add))
            link(dve, v_.tensor_scalar(mroot2[:, :], msum2[:, :], 1.0 / RH, None, ALU.mult))
            v_.tensor_tensor(yv, yv, mroot2[:, :].unsqueeze(2).to_broadcast([P, 16, RH]), ALU.subtract).then_inc(sem("r_cent"), 1)
            dve.wait_ge(sem("r_centsq"), n)
            v_.tensor_reduce(msum[:, :], gs[:, :, :].rearrange("p t (h c) -> p (t h) c", c=RH), AX_X, ALU.add).then_inc(sem("r_var"), 1)
            dve.wait_ge(sem("r_std"), n)
            link(dve, v_.reciprocal(msum2[:, :], mroot[:, :]))
            v_.tensor_tensor(nat[:, :, :].rearrange("p t (h c) -> p (t h) c", c=RH), yv,
                             msum2[:, :].unsqueeze(2).to_broadcast([P, 16, RH]), ALU.mult).then_inc(sem("r_out"), 1)
            dve.wait_ge(sem("r_out_turned"), n)
            for dt in range(4):
                op = v_.tensor_scalar(xf[:, dt, :], pa[:, dt, :], col("ln_w", dt), col("ln_b", dt), ALU.mult, ALU.add)
            link(dve, op)
            link(dve, v_.tensor_tensor(xf[:, :, :], xf[:, :, :], bonus[:, :, :], ALU.add))
            v_.tensor_tensor(xf[:, :, :], xf[:, :, :], gt[:, :, :], ALU.mult).then_inc(sem("y_ready"), 1)
            dve.wait_ge(sem("y_ready"), HALVES + n)

        gs_t = gs[:, :, :].rearrange("p a (b t) -> p (a b) t", t=T)
        nat_t = nat[:, :, :].rearrange("p a (b t) -> p (a b) t", t=T)
        heads_state = bank[3].rearrange("p a (u c) -> p (a u) c", c=C)[:, 0:4, :]

        def lift_pe(pe):
            L = prods["lift"]
            t0, s0 = turns["merged"]
            for c in range(NDC):
                multiply(pe, L[4 * c], L[4 * c]["free"], (xhi, xlo))
                if c > 0:
                    turn(pe, t0 + c - 1)
                multiply(pe, L[4 * c + 1], L[4 * c + 1]["free"], (xhi, xlo))
                if c == 0:
                    pe.wait_ge(sem("y_split"), 1)
                multiply(pe, L[4 * c + 2], L[4 * c + 2]["free"], (yhi, ylo))
                multiply(pe, L[4 * c + 3], L[4 * c + 3]["free"], (yhi, ylo), k0=8)
            turn(pe, t0 + NDC - 1)
            pe.wait_ge(x_ready, s0 + NDC)

        def lift_act(act):
            L = prods["lift"]
            t0, s0 = turns["merged"]
            for c in range(NDC):
                a_, b_, la, lb = L[4 * c:4 * c + 4]
                for j in range(RING if c == 0 else 0, a_["ns"]):
                    split_hi(act, a_["slot"], j)
                if c == 0:
                    act.wait_ge(sem("y_loaded"), 16)
                    copy(act, yhi[:, :, :], yf[:, :, :]).then_inc(sem("y_hi"), 1)
                for j in range(b_["ns"]):
                    split_hi(act, b_["slot"], j)
                    if j == 4:
                        act.wait_ge(slot_used, a_["done"])
                        act.wait_ge(nat_ready, t0 + c)
                        nc.scalar.activation(ga[:, :, :], pair(a_["par"]), ACT.Sigmoid).then_inc(sem(a_["released"][0]), 1)
                        if c > 0:
                            x_hi(act, t0 + c - 1, mhi[:, 4 * c - 4:4 * c, :])
                for j in range(la["ns"]):
                    split_hi(act, la["slot"], j)
                act.wait_ge(slot_used, b_["done"])
                nc.scalar.activation(gb[:, :, :], pair(b_["par"]), ACT.Sigmoid).then_inc(sem(b_["released"][0]), 1)
                for j in range(lb["ns"]):
                    split_hi(act, lb["slot"], j)
            for j in range(RING):
                split_hi(act, prods["out"][0]["slot"], j)
            x_hi(act, t0 + NDC - 1, mhi[:, 12:16, :])

        def lift_dve(dve):
            L = prods["lift"]
            t0, s0 = turns["merged"]
            v_ = nc.vector

            def merge(c):
                lb, b_ = L[4 * c + 3], L[4 * c + 1]
                dve.wait_ge(slot_used, lb["done"])
                dve.wait_ge(sem(b_["released"][0]), b_["released"][1])
                v_.tensor_tensor(gb[:, :, :], gb[:, :, :], pair(lb["par"]), ALU.mult).then_inc(sem(lb["released"][0]), 1)
                dve.wait_ge(sem(lb["released"][0]), lb["released"][1])
                if c > 0:
                    dve.wait_ge(turned, t0 + c)
                else:
                    dve.wait_ge(sem("r_out_turned"), HALVES)
                v_.tensor_tensor(nat[:, :, :], ga[:, :, :], gb[:, :, :], ALU.add).then_inc(nat_ready, 1)

            for c in range(NDC):
                a_, b_, la, lb = L[4 * c:4 * c + 4]
                for j in range(RING if c == 0 else 0, a_["ns"]):
                    split_lo(dve, a_["slot"], j)
                    if j == 4 and c > 0:
                        merge(c - 1)
                if c == 0:
                    dve.wait_ge(sem("y_hi"), 1)
                    v_.tensor_tensor(ylo[:, :, :], yf[:, :, :], yhi[:, :, :].bitcast(F32), ALU.subtract).then_inc(sem("y_split"), 1)
                for j in range(b_["ns"]):
                    split_lo(dve, b_["slot"], j)
                    if c > 0 and j == 2:
                        take(dve, t0 + c - 1, s0 + c - 1)
                    if c > 0 and j == 6:
                        x_lo(dve, s0 + c - 1, mhi[:, 4 * c - 4:4 * c, :], mlo[:, 4 * c - 4:4 * c, :])
                for j in range(la["ns"]):
                    split_lo(dve, la["slot"], j)
                for j in range(lb["ns"]):
                    split_lo(dve, lb["slot"], j)
                dve.wait_ge(slot_used, la["done"])
                dve.wait_ge(sem(a_["released"][0]), a_["released"][1])
                v_.tensor_tensor(ga[:, :, :], ga[:, :, :], pair(la["par"]), ALU.mult).then_inc(sem(la["released"][0]), 1)
                dve.wait_ge(sem(la["released"][0]), la["released"][1])
            for j in range(RING):
                split_lo(dve, prods["out"][0]["slot"], j)
            merge(NDC - 1)
            take(dve, t0 + NDC - 1, s0 + NDC - 1)
            x_lo(dve, s0 + NDC - 1, mhi[:, 12:16, :], mlo[:, 12:16, :])

        def attn_pe(pe):
            O, KV, Q, MO = prods["out"], prods["mkv"], prods["mq"], prods["mo"]
            tm, tk, tq, th = (turns[k][0] for k in ("memnorm", "mk", "qnorm", "mq"))
            for c in range(NDC):
                multiply(pe, O[c], O[c]["free"], (mhi, mlo))
                turn(pe, tm + c)
            pe.wait_ge(x_ready, turns["memnorm"][1] + NDC)
            for c in range(2 * NDC):
                multiply(pe, KV[c], KV[c]["free"], (xhi, xlo))
                if 1 <= c <= NDC:
                    turn(pe, tk + c - 1)
                if c > NDC:
                    turn(pe, tq + c - NDC - 1)
            turn(pe, tq + NDC - 1)
            pe.wait_ge(x_ready, turns["qnorm"][1] + NDC)
            for c in range(NDC):
                multiply(pe, Q[c], Q[c]["free"], (mhi, mlo))
                if c > 0:
                    turn(pe, th + c - 1)
            turn(pe, th + NDC - 1)
            pe.wait_ge(xf_ready, th + NDC)
            pe.wait_ge(sem(Q[NDC - 1]["released"][0]), Q[NDC - 1]["released"][1])
            for g in range(MH + 1):
                if g < MH:
                    if g >= 2:
                        pe.wait_ge(sem("p_exp"), g - 1)
                    sc = bank[2 + g % 2]
                    for tt in range(TT):
                        for kk in range(MHK):
                            mm = nc.tensor.matmul(sc[:, tt, :], qt[:, MHK * g + kk, tt * P:(tt + 1) * P], kt_m[:, MHK * g + kk, :],
                                                  start=(kk == 0), stop=(kk == MHK - 1))
                    mm.then_inc(sem("p_scores"), 1)
                if g > 0:
                    e = g - 1
                    pe.wait_ge(sem("p_norm"), e + 1)
                    for mt in range(TT):
                        for tt in range(TT):
                            mm = nc.tensor.transpose(bank[e % 2][:, mt, tt * P:(tt + 1) * P], pr_m[:, e % 2, tt, mt * P:(mt + 1) * P],
                                                     ident[:, :])
                    mm.then_inc(sem("p_turned"), 1)
                    pe.wait_ge(sem("p_t"), e + 1)
                    if e >= 2:
                        pe.wait_ge(sem("o_take"), e - 1)
                    out = pair(e % 2).rearrange("p a (b t) -> p (a b) t", t=T)
                    for kk in range(MHK):
                        for mt in range(TT):
                            mm = nc.tensor.matmul(out[:, kk, :], v_m[:, mt, e * MHD + kk * P:e * MHD + (kk + 1) * P],
                                                  pt_m[:, e % 2, mt, :], start=(mt == 0), stop=(mt == TT - 1))
                    mm.then_inc(sem("o_mm"), 1)
            pe.wait_ge(sem("o_ready"), MH)
            for c in range(NDC):
                multiply(pe, MO[c], MO[c]["free"], (xhi, xlo))

        def attn_act(act):
            O, KV, Q, MO = prods["out"], prods["mkv"], prods["mq"], prods["mo"]
            tm, tk, tq, th = (turns[k][0] for k in ("memnorm", "mk", "qnorm", "mq"))
            act.wait_ge(sem("mem_loaded"), 16 * TT)
            for c in range(NDC):
                sumsq(act, msb, 2, c)
            norm_root(act, 2)
            for c in range(NDC):
                for j in range(RING if c == 0 else 0, KT // SK):
                    split_hi(act, O[c]["slot"], j)
                    if c > 0 and j == 5:
                        act.wait_ge(sem(O[c - 1]["released"][0]), O[c - 1]["released"][1])
                        sumsq(act, h, 3, c - 1)
                        x_hi(act, tm + c - 1, xhi[:, 4 * c - 4:4 * c, :])
            for j in range(RING):
                split_hi(act, KV[0]["slot"], j)
            act.wait_ge(sem(O[3]["released"][0]), O[3]["released"][1])
            sumsq(act, h, 3, 3)
            x_hi(act, tm + 3, xhi[:, 12:16, :])
            for c in range(2 * NDC):
                for j in range(RING if c == 0 else 0, KT // SK):
                    split_hi(act, KV[c]["slot"], j)
                    if c == NDC and j == 5:
                        norm_root(act, 3)
                if c > NDC + 1:
                    x_hi(act, tq + c - NDC - 2, mhi[:, 4 * (c - NDC - 2):4 * (c - NDC - 1), :])
            for j in range(RING):
                split_hi(act, Q[0]["slot"], j)
            for k in (2, 3):
                x_hi(act, tq + k, mhi[:, 4 * k:4 * k + 4, :])
            for c in range(NDC):
                for j in range(RING if c == 0 else 0, KT // SK):
                    split_hi(act, Q[c]["slot"], j)
            for j in range(RING):
                split_hi(act, MO[0]["slot"], j)
            for g in range(MH + 1):
                if g < MH:
                    act.wait_ge(sem("p_max"), g + 1)
                    for tt in range(TT):
                        op = nc.scalar.activation(pr_m[:, g % 2, tt, :], bank[2 + g % 2][:, tt, :], ACT.Exp, bias=nmx[:, g, tt:tt + 1],
                                                  scale=MHD ** -0.5, accum_out=den[:, g, tt:tt + 1])
                    op.then_inc(sem("p_exp"), 1)
                if g > 0:
                    act.wait_ge(sem("o_take"), g)
                    e = g - 1
                    copy(act, xhi[:, MHK * e:MHK * (e + 1), :], xf[:, :, :]).then_inc(sem("o_hi"), 1)
            for c in range(NDC):
                for j in range(RING if c == 0 else 0, KT // SK):
                    split_hi(act, MO[c]["slot"], j)
                    if c > 0 and j == 5:
                        act.wait_ge(sem(MO[c - 1]["released"][0]), MO[c - 1]["released"][1])
                        sumsq(act, h, 4, c - 1)

        def attn_dve(dve):
            O, KV, Q, MO = prods["out"], prods["mkv"], prods["mq"], prods["mo"]
            (tm, sm), (tk, _), (tq, sq), (th, _) = (turns[k] for k in ("memnorm", "mk", "qnorm", "mq"))
            v_ = nc.vector
            norm_scale(dve, 2)
            norm_chunk(dve, msb, 0, tm)
            for c in range(NDC):
                for j in range(RING if c == 0 else 0, KT // SK):
                    split_lo(dve, O[c]["slot"], j)
                    if c > 0 and j == 4:
                        residual(dve, O[c - 1], c - 1, 1.0)
                        take(dve, tm + c - 1, sm + c - 1, PRM["mem_kv_norm"] + 4 * (c - 1))
                        norm_chunk(dve, msb, c, tm + c)
                    if c > 0 and j == 7:
                        x_lo(dve, sm + c - 1, xhi[:, 4 * c - 4:4 * c, :], xlo[:, 4 * c - 4:4 * c, :])
            for j in range(RING):
                split_lo(dve, KV[0]["slot"], j)
            residual(dve, O[3], 3, 1.0)
            take(dve, tm + 3, sm + 3, PRM["mem_kv_norm"] + 12)
            x_lo(dve, sm + 3, xhi[:, 12:16, :], xlo[:, 12:16, :])

            def k_nat(c):
                dve.wait_ge(slot_used, KV[c]["done"])
                dve.wait_ge(turned, tk + c)
                v_.tensor_copy(nat[:, :, :], pair(KV[c]["par"])).then_inc(nat_ready, 1)
                dve.wait_ge(nat_ready, tk + c + 1)
                dve.sem_inc(sem(KV[c]["released"][0]), 1)

            def plain(dst, t):
                dve.wait_ge(turned, t + 1)
                v_.tensor_copy(dst, pa[:, :, :]).then_inc(xf_ready, 1)

            def v_nat(c):
                dve.wait_ge(slot_used, KV[NDC + c]["done"])
                v_.tensor_copy(v_m[:, :, c * CW:(c + 1) * CW], pair(KV[NDC + c]["par"])).then_inc(sem(KV[NDC + c]["released"][0]), 1)

            for c in range(2 * NDC):
                for j in range(RING if c == 0 else 0, KT // SK):
                    split_lo(dve, KV[c]["slot"], j)
                    if j == 4 and 1 <= c <= NDC:
                        k_nat(c - 1)
                    if j == 4 and c > NDC:
                        v_nat(c - 1 - NDC)
                    if j == 1 and 2 <= c <= NDC + 1:
                        plain(kt_m[:, MHK * (c - 2):MHK * (c - 1), :], tk + c - 2)
                    if j == 5 and c == NDC:
                        norm_scale(dve, 3)
                    if j == 5 and c > NDC:
                        norm_chunk(dve, h, c - NDC - 1, tq + c - NDC - 1)
                    if j == 1 and c > NDC + 1:
                        take(dve, tq + c - NDC - 2, sq + c - NDC - 2, PRM["mem_q_norm"] + 4 * (c - NDC - 2))
                if c > NDC + 1:
                    e = c - NDC - 2
                    x_lo(dve, sq + e, mhi[:, 4 * e:4 * e + 4, :], mlo[:, 4 * e:4 * e + 4, :])
            for j in range(RING):
                split_lo(dve, Q[0]["slot"], j)
            v_nat(NDC - 1)
            take(dve, tq + 2, sq + 2, PRM["mem_q_norm"] + 8)
            norm_chunk(dve, h, 3, tq + 3)
            x_lo(dve, sq + 2, mhi[:, 8:12, :], mlo[:, 8:12, :])
            take(dve, tq + 3, sq + 3, PRM["mem_q_norm"] + 12)
            x_lo(dve, sq + 3, mhi[:, 12:16, :], mlo[:, 12:16, :])

            def q_nat(c):
                dve.wait_ge(slot_used, Q[c]["done"])
                dve.wait_ge(turned, th + c)
                v_.tensor_copy(nat[:, :, :], pair(Q[c]["par"])).then_inc(nat_ready, 1)
                dve.wait_ge(nat_ready, th + c + 1)
                dve.sem_inc(sem(Q[c]["released"][0]), 1)

            for c in range(NDC):
                for j in range(RING if c == 0 else 0, KT // SK):
                    split_lo(dve, Q[c]["slot"], j)
                    if j == 4 and c > 0:
                        q_nat(c - 1)
                    if j == 1 and c > 1:
                        plain(qt[:, MHK * (c - 2):MHK * (c - 1), :], th + c - 2)
            for j in range(RING):
                split_lo(dve, MO[0]["slot"], j)
            plain(qt[:, 8:12, :], th + 2)
            q_nat(3)
            plain(qt[:, 12:16, :], th + 3)
            for g in range(MH + 1):
                if g < MH:
                    dve.wait_ge(sem("p_scores"), g + 1)
                    link(dve, v_.tensor_reduce(mx[:, g, :], bank[2 + g % 2], AX_X, ALU.max))
                    v_.tensor_scalar(nmx[:, g, :], mx[:, g, :], -MHD ** -0.5, None, ALU.mult).then_inc(sem("p_max"), 1)
                    dve.wait_ge(sem("p_exp"), g + 1)
                    link(dve, v_.reciprocal(rden[:, g, :], den[:, g, :]))
                    for tt in range(TT):
                        op = v_.tensor_scalar(pr_m[:, g % 2, tt, :], pr_m[:, g % 2, tt, :], rden[:, g, tt:tt + 1], None, ALU.mult)
                    op.then_inc(sem("p_norm"), 1)
                    dve.wait_ge(sem("p_turned"), g + 1)
                    v_.tensor_copy(pt_m[:, g % 2, :, :], bank[g % 2]).then_inc(sem("p_t"), 1)
                if g > 0:
                    e = g - 1
                    dve.wait_ge(sem("o_mm"), e + 1)
                    if e > 0:
                        dve.wait_ge(sem("o_hi"), e)
                        dve.wait_ge(sem("o_ready"), e)
                    v_.tensor_copy(xf[:, :, :], pair(e % 2).rearrange("p a (b t) -> p (a b) t", t=T)).then_inc(sem("o_take"), 1)
                    dve.wait_ge(sem("o_hi"), e + 1)
                    v_.tensor_tensor(xlo[:, MHK * e:MHK * (e + 1), :], xf[:, :, :], xhi[:, MHK * e:MHK * (e + 1), :].bitcast(F32),
                                     ALU.subtract).then_inc(sem("o_ready"), 1)
            for c in range(NDC):
                for j in range(RING if c == 0 else 0, KT // SK):
                    split_lo(dve, MO[c]["slot"], j)
                    if c > 0 and j == 4:
                        residual(dve, MO[c - 1], c - 1, 1.0)

        fgain = at("fgain", 64, [D])

        def next_hi(act, phase):
            for j in range(RING):
                split_hi(act, prods[phase][0]["slot"], j)

        def next_lo(dve, phase):
            for j in range(RING):
                split_lo(dve, prods[phase][0]["slot"], j)

        def store_y(sp, tile, n):
            sp.wait_ge(sem("y_ready"), n)
            sp.dma_start(y_turned[tile:tile + 4].rearrange("k p t -> p k t"), xf[:, :, :]).then_inc(sem("y_stored"), 16)

        def last_sumsq(act, pr, q):
            act.wait_ge(sem(pr["released"][0]), pr["released"][1])
            sumsq(act, h, q, NDC - 1)

        block = ctx.enter_context(nc.Block())

        @block.gpsimd
        def _(pool):
            g = nc.gpsimd
            g.memset(nat[:, :, :], 0.0).then_inc(prm_clear, 1)
            pool.wait_ge(prm_clear, 1)
            link(pool, g.memset(epsn[:, :], RMS_EPS))
            link(pool, g.memset(ident[:, :], 0.0))
            link(pool, g.affine_select(out=ident[:, :], in_=ident[:, :], compare_op=ALU.not_equal, fill=1.0, base=0,
                                       pattern=[[-1, P]], channel_multiplier=1))
            link(pool, g.memset(ones[:, :], 1.0))
            link(pool, g.memset(headones[:, :], 0.0))
            link(pool, g.memset(eye[:, :], 0.0))
            for c in range(2):
                rows = slice(c * C, (c + 1) * C)
                link(pool, g.memset(headones[rows, rows], 1.0))
                link(pool, g.affine_select(out=eye[rows, :], in_=eye[rows, :], compare_op=ALU.not_equal, fill=1.0, base=0,
                                           pattern=[[-1, C]], channel_multiplier=1))
                for mask, op, pattern in ((m_inc, ALU.is_ge, [[1, C]]), (m_up, ALU.is_gt, [[1, C]]),
                                          (m_upo, ALU.is_gt, [[16, C // 16], [0, 16]])):
                    link(pool, g.affine_select(out=mask[rows, :], in_=ones[rows, 0:C], compare_op=op, fill=0.0, base=0,
                                               pattern=pattern, channel_multiplier=-1))
            link(pool, g.tensor_tensor(m_upd[:, :], m_up[:, :], m_upo[:, :], ALU.subtract))
            link(pool, g.memset(scanmask[:, :], 1.0))
            link(pool, g.memset(scanmask[:, :].rearrange("p (c t) -> p c t", t=C)[:, :, 0:1], 0.0))
            link(pool, g.memset(sel[0:GHV, :, :], 1.0))
            g.affine_select(out=sel[0:GHV, :, :], in_=sel[0:GHV, :, :], compare_op=ALU.is_equal, fill=0.0, base=0,
                            pattern=[[-1, GHV], [0, P]], channel_multiplier=1).then_inc(consts_ready, 1)
            pool.wait_ge(slot_used, prods["f2dn"][0]["slot"])
            g.dma_start(fgain[:, :], A["final_norm"].rearrange("(m d) -> m d", m=1).to_broadcast([P, D])).then_inc(sem("fgain_loaded"), 16)


        @block.sync
        def _(sp):
            for tt in range(TT):
                sp.dma_start(h[:, tt, :], A["x"][0, tt * P:(tt + 1) * P, :]).then_inc(x_loaded, 16)
            sp.wait_ge(prm_clear, 1)
            for name, src, m in prm_sources(A):
                r = PRM[name]
                sp.dma_start(nat[r % P:r % P + m, r // P, 0:src.shape[-1]], src).then_inc(prm_loaded, 16)
            for cell, name in ((dtb, "gdn_dt_bias"), (nal, "gdn_a_log")):
                sp.dma_start(cell, A[name][0].rearrange("(g m) -> g m", m=1)).then_inc(sem("gdn_loaded"), 16)
            ffn_load(sp, "f1", A["ffn1_w_gate"][0], A["ffn1_w_up"][0], A["ffn1_w_down"][0])

            def weights(w, cols, pr, rows0=0):
                for j in range(pr["ns"]):
                    rows = slice(rows0 + j * SK * P, rows0 + (j + 1) * SK * P)
                    load_slot(sp, w[rows, cols].rearrange("(k p) n -> p k n", p=P), pr["slot"], j)

            w_in = A["w_in"][0]
            for j in range(KT // SK):
                rows = slice(j * SK * P, (j + 1) * SK * P)
                s, n, _ = slot_of(AUX["slot"], j)
                sp.wait_ge(wlo_ready, n - RING + 1)
                for at_, c0, c1 in ((0, 3 * RW, RW_COLS), (LORA, BA0, GATE0)):
                    sp.dma_start(raw[:, s, :, at_:at_ + c1 - c0], w_in[rows, c0:c1].rearrange("(k p) n -> p k n", p=P)).then_inc(LOADED[s], 16)
            for hf in range(HALVES):
                g = prods[f"gdn{hf}"]
                for j in range(KT // SK):
                    rows = slice(j * SK * P, (j + 1) * SK * P)
                    s, n, _ = slot_of(g[0]["slot"], j)
                    sp.wait_ge(wlo_ready, n - RING + 1)
                    for at_, c0 in ((0, GDN0 + hf * 256), (256, GDN0 + GQ + hf * 256)):
                        sp.dma_start(raw[:, s, :, at_:at_ + 256], w_in[rows, c0:c0 + 256].rearrange("(k p) n -> p k n", p=P)).then_inc(LOADED[s], 16)
                for m, c0 in ((1, GDN0 + 2 * GQ), (2, Z0)):
                    weights(w_in, slice(c0 + hf * CW, c0 + (hf + 1) * CW), g[m])
                if hf > 0:
                    store_y(sp, 8 + 4 * (hf - 1), hf)
            for hf in range(HALVES):
                g = prods[f"rw{hf}"]
                for m in range(3):
                    weights(w_in, slice(m * RW + hf * CW, m * RW + (hf + 1) * CW), g[m])
                    if m == 0:
                        if hf == 0:
                            store_y(sp, 12, HALVES)
                        else:
                            store_y(sp, 0, HALVES + 1)
                        cols = slice(hf * CW, (hf + 1) * CW)
                        sp.wait_ge(sem("lora_clear"), hf + 1)
                        sp.dma_start(w2z[0:LORA_D, :], A["rw_w2"][0][:, cols]).then_inc(sem("lora_loaded"), 16)
                        sp.dma_start(a2z[LORA_D:P, :], A["rw_a2"][0][:, cols]).then_inc(sem("lora_loaded"), 16)
                        sp.dma_start(g2a[:, :], A["rw_g2"][0][0:P, cols]).then_inc(sem("lora_loaded"), 16)
                        sp.dma_start(g2b[0:32, :], A["rw_g2"][0][P:LORA_G, cols]).then_inc(sem("lora_loaded"), 16)
            for c in range(NDC):
                L = prods["lift"][4 * c:4 * c + 4]
                cols = slice(c * CW, (c + 1) * CW)
                weights(w_in, slice(GATE0 + c * CW, GATE0 + (c + 1) * CW), L[0])
                if c == 0:
                    store_y(sp, 4, HALVES + 2)
                    sp.wait_ge(sem("y_stored"), 16 * 2 * HALVES)
                    sp.dma_start(yf[:, :, :], y_turned.rearrange("k p t -> p k t")).then_inc(sem("y_loaded"), 16)
                weights(w_in, slice(GATE0 + D + c * CW, GATE0 + D + (c + 1) * CW), L[1])
                weights(A["w_lift"][0, 0], cols, L[2])
                weights(A["w_lift"][0, 1], cols, L[3])
            sp.wait_ge(slot_used, prods["lift"][-1]["done"])
            for tt in range(TT):
                sp.dma_start(msb[:, tt, :], A["mem"][0, tt * P:(tt + 1) * P, :]).then_inc(sem("mem_loaded"), 16)
            for phase, ws in (("out", ("w_out",)), ("mkv", ("w_mk", "w_mv")), ("mq", ("w_mq",)), ("mo", ("w_mo",))):
                for m, w in enumerate(ws):
                    for c in range(NDC):
                        weights(A[w][0], slice(c * CW, (c + 1) * CW), prods[phase][NDC * m + c])
            ffn_load(sp, "f2", A["ffn2_w_gate"][0], A["ffn2_w_up"][0], A["ffn2_w_down"][0])
            for c in range(NDC):
                sp.wait_ge(sem("out_ready"), c + 1)
                sp.dma_start(A["out"][0].rearrange("(t p) d -> p t d", p=P)[:, :, c * CW:(c + 1) * CW],
                             h[:, :, c * CW:(c + 1) * CW]).then_inc(stored, 16)
            sp.wait_ge(stored, 16 * NDC)

        @block.scalar
        def _(act):
            next_hi(act, "f1gu")
            act.wait_ge(x_loaded, 16 * TT)
            for c in range(NDC):
                sumsq(act, h, 0, c)
            act.wait_ge(consts_ready, 1)
            norm_act(act, 0, "f1norm")
            ffn_act(act, "f1")
            for j in range(RING):
                split_hi(act, AUX["slot"], j, width=AUXW)
            last_sumsq(act, prods["f1dn"][3], 1)
            norm_act(act, 1, "mixnorm")
            for j in range(RING, KT // SK):
                split_hi(act, AUX["slot"], j, width=AUXW)
            next_hi(act, "gdn0")
            aux_act(act)
            for hf in range(HALVES):
                gdn_act(act, hf)
                next_hi(act, "gdn1" if hf == 0 else "rw0")
            for hf in range(HALVES):
                rw_act(act, hf)
                next_hi(act, "rw1" if hf == 0 else "lift")
            lift_act(act)
            attn_act(act)
            next_hi(act, "f2gu")
            last_sumsq(act, prods["mo"][3], 4)
            norm_act(act, 4, "f2norm")
            ffn_act(act, "f2")
            last_sumsq(act, prods["f2dn"][3], 5)
            norm_root(act, 5)

        @block.vector
        def _(dve):
            dve.wait_ge(prm_turned, 1)
            nc.vector.tensor_copy(prm[:, 0:NPRM], pb[:, :, :].rearrange("p a b -> p (a b)")[:, 0:NPRM]).then_inc(prm_ready, 1)
            dve.wait_ge(prm_ready, 1)
            next_lo(dve, "f1gu")
            norm_dve(dve, 0, h, "f1norm", "ffn1_norm")
            ffn_dve(dve, "f1")
            for j in range(RING):
                split_lo(dve, AUX["slot"], j, width=AUXW)
            residual(dve, prods["f1dn"][3], 3, 0.5)
            norm_dve(dve, 1, h, "mixnorm", "mix_norm")
            for j in range(RING, KT // SK):
                split_lo(dve, AUX["slot"], j, width=AUXW)
            next_lo(dve, "gdn0")
            aux_dve(dve)
            for hf in range(HALVES):
                gdn_dve(dve, hf)
                next_lo(dve, "gdn1" if hf == 0 else "rw0")
            for hf in range(HALVES):
                rw_dve(dve, hf)
                next_lo(dve, "rw1" if hf == 0 else "lift")
            lift_dve(dve)
            attn_dve(dve)
            next_lo(dve, "f2gu")
            residual(dve, prods["mo"][3], 3, 1.0)
            norm_dve(dve, 4, h, "f2norm", "ffn2_norm")
            ffn_dve(dve, "f2")
            residual(dve, prods["f2dn"][3], 3, 0.5)
            norm_scale(dve, 5)
            dve.wait_ge(sem("fgain_loaded"), 16)
            for c in range(NDC):
                cols = slice(c * CW, (c + 1) * CW)
                for tt in range(TT):
                    op = nc.vector.scalar_tensor_tensor(h[:, tt, cols], h[:, tt, cols], rstd[:, tt:tt + 1], fgain[:, cols], ALU.mult, ALU.mult)
                op.then_inc(sem("out_ready"), 1)

        @block.tensor
        def _(pe):
            pe.wait_ge(consts_ready, 1)
            pe.wait_ge(prm_loaded, 16 * len(PRM))
            for g in range(2):
                mm = nc.tensor.transpose(pb[:, g // 2, g * P:(g + 1) * P], nat[:, g, 0:P], ident[:, :])
            mm.then_inc(prm_turned, 1)
            norm_pe(pe, "f1norm")
            ffn_pe(pe, "f1")
            norm_pe(pe, "mixnorm")
            pe.wait_ge(x_ready, turns["mixnorm"][1] + NDC)
            aux_pe(pe)
            for hf in range(HALVES):
                gdn_pe(pe, hf)
            for hf in range(HALVES):
                rw_pe(pe, hf)
            lift_pe(pe)
            attn_pe(pe)
            norm_pe(pe, "f2norm")
            ffn_pe(pe, "f2")


def prm_sources(A):
    def rows(v):
        return v.rearrange("(m p) -> m p", p=P)

    mu = A["rw_shift_mu"][0]
    wide = 3 * RW
    out = [("ffn1_norm", rows(A["ffn1_norm"][0]), KT), ("mix_norm", rows(A["mix_norm"][0]), KT),
           ("mem_q_norm", rows(A["mem_q_norm"][0]), KT), ("mem_kv_norm", rows(A["mem_kv_norm"][0]), KT),
           ("ffn2_norm", rows(A["ffn2_norm"][0]), KT), ("mu_rkv", rows(mu[0:wide]), wide // P),
           ("mu_wa", rows(mu[wide:wide + P]), 1), ("mu_g0", rows(mu[wide + P:wide + 2 * P]), 1),
           ("mu_g1", mu[wide + 2 * P:RW_COLS].rearrange("(m p) -> m p", m=1), 1)]
    for name in ("w0", "a0", "k_k", "k_a", "ln_w", "ln_b"):
        out.append((name, rows(A["rw_" + name][0]), RW // P))
    out.append(("r_k", A["rw_r_k"][0].rearrange("(m a) n -> m (a n)", a=2), RW // P))
    out.append(("conv", A["gdn_conv_w"][0].rearrange("k (m p) -> (k m) p", p=P), CONV * 16))
    out.append(("gdn_norm", A["gdn_norm_w"][0].rearrange("(m p) -> m p", m=1), 1))
    return out


_INS = ['x', 'mem', 'ffn1_norm', 'ffn1_w_gate', 'ffn1_w_up', 'ffn1_w_down', 'mix_norm', 'w_in', 'rw_shift_mu', 'rw_w0',
        'rw_w2', 'rw_a0', 'rw_a2', 'rw_g2', 'rw_k_k', 'rw_k_a', 'rw_r_k', 'rw_ln_w', 'rw_ln_b', 'gdn_conv_w',
        'gdn_a_log', 'gdn_dt_bias', 'gdn_norm_w', 'w_lift', 'w_out', 'mem_q_norm', 'mem_kv_norm', 'w_mq', 'w_mk',
        'w_mv', 'w_mo', 'ffn2_norm', 'ffn2_w_gate', 'ffn2_w_up', 'ffn2_w_down', 'final_norm']


def kernel(**inputs):
    import numpy as np
    import concourse.bacc as bacc
    from concourse.bass_utils import run_bass_kernel_spmd

    nc = bacc.Bacc("TRN2", target_bir_lowering=False, num_devices=1)
    arrays, aps = {}, {}
    for name in _INS:
        a = np.ascontiguousarray(inputs[name])
        arrays[f"in_{name}"] = a
        aps[name] = nc.dram_tensor(f"in_{name}", a.shape, mybir.dt.from_np(a.dtype), kind="ExternalInput").ap()
    aps["out"] = nc.dram_tensor("out", (1, T, D), F32, kind="ExternalOutput").ap()
    build(nc, aps)
    r = run_bass_kernel_spmd(nc, [arrays], core_ids=[0])
    return np.asarray(r.results[0]["out"])
```

```python
from contextlib import ExitStack

import concourse.bass as bass
from concourse import mybir

F32 = mybir.dt.float32
F32R = mybir.dt.float32r
ALU = mybir.AluOpType
ACT = mybir.ActivationFunctionType
AX_X = mybir.AxisListType.X
ds = bass.ds

P = 128
T = 256
TT = T // P
D = 2048
KT = D // P
F = 5632
FT = F // P
CW = 512
SK = 2
RING = 4
NFC = F // CW
NDC = D // CW
RMS_EPS = 1e-6
C = 64
NCH = T // C

RW = 1024
RH = 64
RW_GN_EPS = 64e-5
LORA_D, LORA_A, LORA_G = 64, 64, 160
LORA = LORA_D + LORA_A + LORA_G
RW_COLS = 3 * RW + LORA
GH = 128
GHV = 8
GQ = 512
GV = 1024
CONV = 4
GDN0 = RW_COLS
Z0 = GDN0 + 2 * GQ + GV
BA0 = Z0 + GV
GATE0 = BA0 + 2 * GHV
AUXW = LORA + 2 * GHV
MH = 4
MHD = D // MH
MHK = MHD // P
HALVES = 2
EXP_HALF = 0.6065306597126334

PRM_LIST = [("ffn1_norm", KT), ("mix_norm", KT), ("mem_q_norm", KT), ("mem_kv_norm", KT), ("ffn2_norm", KT),
            ("mu_rkv", 3 * RW // P), ("mu_wa", 1), ("mu_g0", 1), ("mu_g1", 1), None,
            ("w0", RW // P), ("a0", RW // P), ("k_k", RW // P), ("k_a", RW // P), ("r_k", RW // P),
            ("ln_w", RW // P), ("ln_b", RW // P), ("conv", CONV * 16), ("gdn_norm", 1)]
PRM = {}
_at = 0
for _entry in PRM_LIST:
    if _entry is None:
        _at = P
    else:
        PRM[_entry[0]] = _at
        _at += _entry[1]
NPRM = _at


def background():
    marks = []

    def mark(name, n):
        marks.append((name, n))

    def inversion(v, weights):
        for k in range(10):
            mark(f"inv{v}.{k + 1}", weights[k])

    for hf in range(HALVES):
        for name, n in zip(("conv", "norms", "rows", "naturals", "mats"), W_GDN[hf]):
            mark(f"gdn{hf}.{name}", n)
        inversion(hf, W_INV[hf])
        for c in range(NCH):
            for name, n in zip(("ks", "vnew", "state"), W_GCH[hf]):
                mark(f"gdn{hf}.{name}{c}", n)
        mark(f"gdn{hf}.out", W_GOUT[hf])
    for hf in range(HALVES):
        for name, n in zip(("lora", "g", "r", "k", "v", "shift", "kk", "tilde", "bonus", "nat"), W_RW[hf]):
            mark(f"rw{hf}.{name}", n)
        for tt in range(TT):
            mark(f"rw{hf}.mats{tt}", W_RMATS[hf])
            inversion(HALVES + TT * hf + tt, W_INV[HALVES + TT * hf + tt])
        for c in range(NCH):
            for name, n in zip(("r", "sa", "y"), W_RCH[hf]):
                mark(f"rw{hf}.{name}{c}", n)
        mark(f"rw{hf}.out", W_ROUT[hf])
    return marks


W_GDN = [[8, 2, 2, 2, 2], [8, 2, 2, 2, 2]]
W_INV = [[1] * 9 + [0]] * 2 + [[1] * 4 + [0] * 6] * 4
W_GCH = [[1, 0, 1], [1, 0, 1]]
W_GOUT = [2, 2]
W_RW = [[1, 1, 1, 1, 1, 2, 2, 3, 2, 1], [1, 1, 1, 1, 1, 2, 2, 3, 2, 1]]
W_RMATS = [1, 1]
W_RCH = [[0, 1, 0], [0, 0, 0]]
W_ROUT = [1, 0]


def plan():
    prods, turns = {}, {}
    state = dict(p=0, slot=0, t=0, s=0, freed=[0, 0])
    last = [None, None]

    def products(phase, n, nk, ups=None):
        out = []
        for c in range(n):
            k = nk[c % len(nk)]
            par = state["p"] % 2
            if ups is not None and c % 2 == 1:
                released = ("nat_ready", ups + c // 2 + 1)
            else:
                state["freed"][par] += 1
                released = (("pair_free0", "pair_free1")[par], state["freed"][par])
            out.append(dict(par=par, slot=state["slot"], ns=k // SK, free=last[par], released=released,
                            done=state["slot"] + k // SK))
            last[par] = released
            state["p"] += 1
            state["slot"] += k // SK
        prods[phase] = out

    def turned(phase, n, split=True):
        turns[phase] = (state["t"], state["s"])
        state["t"] += n
        if split:
            state["s"] += n

    def ffn(tag):
        turned(tag + "norm", NDC)
        turned(tag + "act", NFC)
        products(tag + "gu", 2 * NFC, [KT], ups=turns[tag + "act"][0])
        products(tag + "dn", NDC, [FT])

    ffn("f1")
    turned("mixnorm", NDC)
    products("aux", 1, [KT])
    for hf in range(HALVES):
        products(f"gdn{hf}", 3, [KT])
    for hf in range(HALVES):
        products(f"rw{hf}", 3, [KT])
    products("gates", 2 * NDC, [KT])
    products("lift", 2 * NDC, [8])
    turned("merged", NDC)
    products("out", NDC, [KT])
    turned("memnorm", NDC)
    products("mkv", 2 * NDC, [KT])
    turned("mk", NDC, False)
    turned("qnorm", NDC)
    products("mq", NDC, [KT])
    turned("mq", NDC, False)
    products("mo", NDC, [KT])
    ffn("f2")
    return prods, turns


def build(nc, A, stop=None):
    prods, turns = plan()
    with ExitStack() as ctx:
        sems = {}

        def sem(name):
            if name not in sems:
                sems[name] = ctx.enter_context(nc.semaphore(name))
            return sems[name]

        base = -(-nc.sbuf_base // 64) * 64
        ctx.enter_context(nc.sbuf_tensor("slab", [P, 207 * 256], F32))

        def at(name, kib, shape, dt=F32):
            return nc.alloc_sbuf_tensor_at(name, [P] + shape, dt, offset=int(base + kib * 1024))

        h = at("h", 0, [TT, D])
        raw = at("raw", 16, [RING, SK, CW])
        whi = at("whi", 32, [RING, SK, CW], F32R)
        wlo = at("wlo", 48, [RING, SK, CW], F32R)
        xhi = at("xhi", 64, [KT, T], F32R)
        xlo = at("xlo", 80, [KT, T], F32R)
        ident = at("ident", 96, [P])
        ones = at("ones", 96.5, [P])
        headones = at("headones", 97, [P])
        m_up = at("m_up", 97.5, [C])
        m_upd = at("m_upd", 97.75, [C])
        m_upo = at("m_upo", 98, [C])
        m_inc = at("m_inc", 98.25, [C])
        eye = at("eye", 98.5, [C])
        prm = at("prm", 98.75, [NPRM])
        scanmask = at("scanmask", 99.75, [T])
        sel = at("sel", 100.75, [GHV, P])
        AR = 105
        hhi = at("hhi", AR, [FT, T], F32R)
        hlo = at("hlo", AR + 44, [FT, T], F32R)
        nat = at("nat", 193, [TT, CW])
        gs = at("gs", 197, [TT, CW])
        xf = at("xf", 201, [4, T])
        ss = at("ss", 205, [TT, NDC])
        ssum = at("ssum", 205.0625, [TT])
        rms = at("rms", 205.125, [TT])
        rstd = at("rstd", 205.1875, [TT])
        epsn = at("epsn", 205.25, [1])
        scal = at("scal", 205.5, [16 * 24])

        pp = ctx.enter_context(nc.psum_tensor("pp", [P, 4, CW], F32))
        pa = ctx.enter_context(nc.psum_tensor("pa", [P, 4, T], F32))
        pb = ctx.enter_context(nc.psum_tensor("pb", [P, 4, T], F32))

        def pair(par):
            return pp[:, 2 * par:2 * par + 2, :]

        LOADED = [sem(f"loaded{s}") for s in range(RING)]
        whi_ready, wlo_ready, slot_used = sem("whi_ready"), sem("wlo_ready"), sem("slot_used")
        nat_ready, turned, xf_ready = sem("nat_ready"), sem("turned"), sem("xf_ready")
        hi_ready, x_ready = sem("hi_ready"), sem("x_ready")
        sumsq_ready, ms_ready, rms_ready = sem("sumsq_ready"), sem("ms_ready"), sem("rms_ready")
        x_loaded, prm_clear, prm_loaded = sem("x_loaded"), sem("prm_clear"), sem("prm_loaded")
        consts_ready, prm_turned, prm_ready, eps_ready = sem("consts_ready"), sem("prm_turned"), sem("prm_ready"), sem("eps_ready")
        stored = sem("stored")

        two_pieces = [prods[k][0]["slot"] for k in ("aux", "gdn0", "gdn1")]

        def slot_of(base_slot, j, i=0):
            n = base_slot + j
            twice = sum(min(max((n - first) // RING + 1, 0), 2) for first in two_pieces)
            return n % RING, n + 16 * i, 16 * (n // RING + 1 + twice) + 64 * i

        def wait_pair(eng, need):
            if need is not None:
                eng.wait_ge(sem(need[0]), need[1])

        def load_slot(sp, src, base_slot, j, i=0, width=CW):
            s, n, _ = slot_of(base_slot, j, i)
            if not (isinstance(n, int) and n < RING):
                sp.wait_ge(wlo_ready, n - RING + 1)
            dst = raw[:, s, :, :] if width == CW else raw[:, s, :, 0:width]
            sp.dma_start(dst, src).then_inc(LOADED[s], 16)

        def split_hi(act, base_slot, j, i=0, width=CW):
            s, n, ld = slot_of(base_slot, j, i)
            act.wait_ge(LOADED[s], ld)
            if not (isinstance(n, int) and n < RING):
                act.wait_ge(slot_used, n - RING + 1)
            nc.scalar.activation(whi[:, s, :, 0:width], raw[:, s, :, 0:width], ACT.Copy).then_inc(whi_ready, 1)

        def split_lo(dve, base_slot, j, i=0, width=CW):
            s, n, _ = slot_of(base_slot, j, i)
            dve.wait_ge(whi_ready, n + 1)
            nc.vector.tensor_tensor(wlo[:, s, :, 0:width], raw[:, s, :, 0:width],
                                    whi[:, s, :, 0:width].bitcast(F32), ALU.subtract).then_inc(wlo_ready, 1)

        def multiply(pe, pr, free, acts, i=0, width=CW, k0=0):
            wait_pair(pe, free)
            for j in range(pr["ns"]):
                multiply_slot(pe, pr, j, acts, i, width, k0)

        def multiply_slot(pe, pr, j, acts, i=0, width=CW, k0=0):
            a_hi, a_lo = acts
            s, n, _ = slot_of(pr["slot"], j, i)
            pe.wait_ge(wlo_ready, n + 1)
            for kk in range(SK):
                k = j * SK + kk
                first, final = k == 0, k == pr["ns"] * SK - 1
                for tt in range(TT):
                    tok = slice(tt * P, (tt + 1) * P)
                    out = pp[:, 2 * pr["par"] + tt, 0:width]
                    w_hi, w_lo = whi[:, s, kk, 0:width], wlo[:, s, kk, 0:width]
                    nc.tensor.matmul(out, a_hi[:, k0 + k, tok], w_hi, start=first, stop=False)
                    nc.tensor.matmul(out, a_lo[:, k0 + k, tok], w_hi, start=False, stop=False)
                    mm = nc.tensor.matmul(out, a_hi[:, k0 + k, tok], w_lo, start=False, stop=final)
            mm.then_inc(slot_used, 1)

        BG = [pr for phase in ("gdn1", "rw0", "rw1", "gates") for pr in prods[phase]]
        BG0, BGN = BG[0]["slot"], len(BG) * (KT // SK)
        upto, total = {}, 0
        for name, n in background():
            total = min(total + n, BGN)
            upto[name] = total
        upto["rest"] = BGN
        spooled_before = max(0, (upto["gdn1.out"] + 4 - 5) // (KT // SK))
        at_pe, at_act, at_dve = [0], [RING], [RING]
        LEAD = 4

        def bg_pe(pe, name):
            for n in range(at_pe[0], upto[name]):
                pr, j = BG[n // (KT // SK)], n % (KT // SK)
                if j == 0:
                    wait_pair(pe, pr["free"])
                multiply_slot(pe, pr, j, (xhi, xlo))
            at_pe[0] = max(at_pe[0], upto[name])

        def bg_act(act, name, spool):
            for n in range(at_act[0], min(upto[name] + LEAD, BGN)):
                q, j = n // (KT // SK), n % (KT // SK)
                split_hi(act, BG[q]["slot"], j)
                if j == 4 and q > 0:
                    spool_out(act, q - 1, spool)
            at_act[0] = max(at_act[0], min(upto[name] + LEAD, BGN))

        def spool_out(act, q, spool):
            pr = BG[q]
            act.wait_ge(slot_used, pr["done"])
            if q > 0:
                act.wait_ge(sem("spooled"), 16 * q)
            nc.scalar.activation(spool[:, :, :], pair(pr["par"]), ACT.Copy).then_inc(sem(pr["released"][0]), 1)
            act.wait_ge(sem(pr["released"][0]), pr["released"][1])
            act.dma_start(proj[q].rearrange("(t p) c -> p t c", p=P), spool[:, :, :]).then_inc(sem("spooled"), 16)

        def bg_dve(dve, name):
            for n in range(at_dve[0], min(upto[name] + LEAD, BGN)):
                split_lo(dve, BG[n // (KT // SK)]["slot"], n % (KT // SK))
            at_dve[0] = max(at_dve[0], min(upto[name] + LEAD, BGN))

        def turn(pe, t, src_ready=None):
            if src_ready is None:
                pe.wait_ge(nat_ready, t + 1)
            else:
                pe.wait_ge(*src_ready)
            if not (isinstance(t, int) and t == 0):
                pe.wait_ge(xf_ready, t)
            for kk in range(4):
                for tt in range(TT):
                    mm = nc.tensor.transpose(pa[:, kk, tt * P:(tt + 1) * P], nat[:, tt, kk * P:(kk + 1) * P], ident[:, :])
            mm.then_inc(turned, 1)

        def take(dve, t, s, gain=None):
            dve.wait_ge(turned, t + 1)
            if not (isinstance(s, int) and s == 0):
                dve.wait_ge(hi_ready, s)
                dve.wait_ge(x_ready, s)
            if gain is None:
                nc.vector.tensor_copy(xf[:, :, :], pa[:, :, :]).then_inc(xf_ready, 1)
            else:
                for kk in range(4):
                    op = nc.vector.tensor_scalar(xf[:, kk, :], pa[:, kk, :], prm[:, gain + kk:gain + kk + 1], None, ALU.mult)
                op.then_inc(xf_ready, 1)

        def x_hi(act, t, dst):
            act.wait_ge(xf_ready, t + 1)
            nc.scalar.activation(dst, xf[:, :, :], ACT.Copy).then_inc(hi_ready, 1)

        def x_lo(dve, s, dst_hi, dst_lo):
            dve.wait_ge(hi_ready, s + 1)
            nc.vector.tensor_tensor(dst_lo, xf[:, :, :], dst_hi.bitcast(F32), ALU.subtract).then_inc(x_ready, 1)

        def sumsq(act, src, q, c):
            if NDC * q + c > 0:
                act.wait_ge(sumsq_ready, NDC * q + c)
            for tt in range(TT):
                op = nc.scalar.activation(gs[:, tt, :], src[:, tt, c * CW:(c + 1) * CW], ACT.Square,
                                          accum_out=ss[:, tt, c:c + 1])
            op.then_inc(sumsq_ready, 1)

        def norm_root(act, q):
            act.wait_ge(ms_ready, q + 1)
            nc.scalar.activation(rms[:, :], ssum[:, :], ACT.Sqrt, bias=epsn[:, 0:1], scale=1.0 / D).then_inc(rms_ready, 1)

        def norm_scale(dve, q):
            dve.wait_ge(sumsq_ready, NDC * (q + 1))
            nc.vector.tensor_reduce(ssum[:, :], ss[:, :, :], AX_X, ALU.add).then_inc(ms_ready, 1)
            dve.wait_ge(rms_ready, q + 1)
            link(dve, nc.vector.reciprocal(rstd[:, :], rms[:, :]))

        def norm_chunk(dve, src, c, t):
            if t > 0:
                dve.wait_ge(turned, t)
            for tt in range(TT):
                op = nc.vector.tensor_scalar(nat[:, tt, :], src[:, tt, c * CW:(c + 1) * CW], rstd[:, tt:tt + 1], None, ALU.mult)
            op.then_inc(nat_ready, 1)

        def norm_dve(dve, q, src, tag, gain):
            t, s = turns[tag]
            norm_scale(dve, q)
            for c in range(NDC):
                norm_chunk(dve, src, c, t + c)
                take(dve, t + c, s + c, PRM[gain] + 4 * c)
                x_lo(dve, s + c, xhi[:, 4 * c:4 * c + 4, :], xlo[:, 4 * c:4 * c + 4, :])

        def norm_act(act, q, tag):
            t, s = turns[tag]
            norm_root(act, q)
            for c in range(NDC):
                x_hi(act, t + c, xhi[:, 4 * c:4 * c + 4, :])

        def norm_pe(pe, tag):
            for c in range(NDC):
                turn(pe, turns[tag][0] + c)

        chain = {}

        def link(eng, ins):
            name = {dve_engine: "dve_chain", act_engine: "act_chain", pool_engine: "pool_chain"}[type(eng)]
            chain[name] = chain.get(name, 0) + 1
            ins.then_inc(sem(name), 1)
            eng.wait_ge(sem(name), chain[name])

        dve_engine, act_engine, pool_engine = type(nc.vector), type(nc.scalar), type(nc.gpsimd)

        def ffn_load(sp, tag, w_gate, w_up, w_down):
            gu, dn = prods[tag + "gu"], prods[tag + "dn"]

            def chunk(i):
                for m, w in enumerate((w_gate, w_up)):
                    for j in range(KT // SK):
                        src = w[j * SK * P:(j + 1) * SK * P, ds(i * CW, CW)].rearrange("(k p) n -> p k n", p=P)
                        load_slot(sp, src, gu[m]["slot"], j, i)

            chunk(0)
            with sp.Fori(1, NFC) as i:
                chunk(i)
            for c in range(NDC):
                for j in range(FT // SK):
                    src = w_down[j * SK * P:(j + 1) * SK * P, c * CW:(c + 1) * CW].rearrange("(k p) n -> p k n", p=P)
                    load_slot(sp, src, dn[c]["slot"], j)

        def ffn_pe(pe, tag):
            gu, dn = prods[tag + "gu"], prods[tag + "dn"]
            t0, s0 = turns[tag + "act"]

            def chunk(i, first):
                gate_free = gu[0]["free"] if first else (gu[0]["released"][0], gu[0]["released"][1] + i - 1)
                up_free = gu[1]["free"] if first else ("nat_ready", t0 + i)
                multiply(pe, gu[0], gate_free, (xhi, xlo), i)
                if not first:
                    turn(pe, t0 + i - 1)
                multiply(pe, gu[1], up_free, (xhi, xlo), i)

            pe.wait_ge(x_ready, turns[tag + "norm"][1] + NDC)
            chunk(0, True)
            with pe.Fori(1, NFC) as i:
                chunk(i, False)
            turn(pe, t0 + NFC - 1)
            pe.wait_ge(x_ready, s0 + NFC)
            for c in range(NDC):
                multiply(pe, dn[c], dn[c]["free"], (hhi, hlo))

        def ffn_act(act, tag):
            gu, dn = prods[tag + "gu"], prods[tag + "dn"]
            t0, s0 = turns[tag + "act"]

            def chunk(i, first):
                for j in range(RING if first else 0, KT // SK):
                    split_hi(act, gu[0]["slot"], j, i)
                for j in range(KT // SK):
                    split_hi(act, gu[1]["slot"], j, i)
                    if j == 4:
                        if not first:
                            x_hi(act, t0 + i - 1, hhi[:, ds(4 * i - 4, 4), :])
                        act.wait_ge(slot_used, gu[0]["done"] + 16 * i)
                        act.wait_ge(nat_ready, t0 + i)
                        nc.scalar.activation(gs[:, :, :], pair(gu[0]["par"]), ACT.Silu).then_inc(sem(gu[0]["released"][0]), 1)

            chunk(0, True)
            with act.Fori(1, NFC) as i:
                chunk(i, False)
            for j in range(RING):
                split_hi(act, dn[0]["slot"], j)
            x_hi(act, t0 + NFC - 1, hhi[:, 4 * NFC - 4:4 * NFC, :])
            for c in range(NDC):
                for j in range(RING if c == 0 else 0, FT // SK):
                    split_hi(act, dn[c]["slot"], j)
                    if c > 0 and j == 5:
                        act.wait_ge(sem(dn[c - 1]["released"][0]), dn[c - 1]["released"][1])
                        sumsq(act, h, 1 if tag == "f1" else 5, c - 1)

        def ffn_dve(dve, tag):
            gu, dn = prods[tag + "gu"], prods[tag + "dn"]
            t0, s0 = turns[tag + "act"]

            def gated(i):
                dve.wait_ge(slot_used, gu[1]["done"] + 16 * i)
                dve.wait_ge(sem(gu[0]["released"][0]), gu[0]["released"][1] + i)
                dve.wait_ge(turned, t0 + i)
                nc.vector.tensor_tensor(nat[:, :, :], gs[:, :, :], pair(gu[1]["par"]), ALU.mult).then_inc(nat_ready, 1)

            def chunk(i, first):
                for j in range(RING if first else 0, KT // SK):
                    split_lo(dve, gu[0]["slot"], j, i)
                    if j == 4 and not first:
                        gated(i - 1)
                for j in range(KT // SK):
                    split_lo(dve, gu[1]["slot"], j, i)
                    if j == 2 and not first:
                        take(dve, t0 + i - 1, s0 + i - 1)
                    if j == 6 and not first:
                        x_lo(dve, s0 + i - 1, hhi[:, ds(4 * i - 4, 4), :], hlo[:, ds(4 * i - 4, 4), :])

            chunk(0, True)
            with dve.Fori(1, NFC) as i:
                chunk(i, False)
            for j in range(RING):
                split_lo(dve, dn[0]["slot"], j)
            gated(NFC - 1)
            take(dve, t0 + NFC - 1, s0 + NFC - 1)
            x_lo(dve, s0 + NFC - 1, hhi[:, 4 * NFC - 4:4 * NFC, :], hlo[:, 4 * NFC - 4:4 * NFC, :])
            for c in range(NDC):
                for j in range(RING if c == 0 else 0, FT // SK):
                    split_lo(dve, dn[c]["slot"], j)
                    if c > 0 and j == 4:
                        residual(dve, dn[c - 1], c - 1, 0.5)

        def residual(dve, pr, c, scale):
            dve.wait_ge(slot_used, pr["done"])
            hc = h[:, :, c * CW:(c + 1) * CW]
            nc.vector.scalar_tensor_tensor(hc, pair(pr["par"]), scale, hc, ALU.mult, ALU.add).then_inc(sem(pr["released"][0]), 1)

        auxt = at("auxt", AR, [3, T + 1])
        lora = at("lora", AR + 3.25, [3, T])
        beta_t = at("beta_t", AR + 6.25, [T])
        gc_t = at("gc_t", AR + 7.25, [T])
        sp_a = at("sp_a", AR + 8.25, [T])
        sp_b = at("sp_b", AR + 9.25, [T])
        qkp = at("qkp", AR + 10.25, [4, T + CONV - 1])
        vp = at("vp", AR + 14.5, [4, T + CONV - 1])
        zg = at("zg", AR + 18.75, [TT, CW])
        qk = at("qk", AR + 22.75, [4, T])
        vg = at("vg", AR + 26.75, [4, T])
        kb = at("kb", AR + 30.75, [4, T])
        qe = at("qe", AR + 34.75, [4, T])
        eg = at("eg", AR + 38.75, [4, T])
        bb = at("bb", AR + 42.75, [4, T])
        kn = at("kn", AR + 46.75, [TT, 2 * P])
        vb = at("vb", AR + 48.75, [TT, CW])
        dec = at("dec", AR + 52.75, [8, C])
        att = at("att", AR + 54.75, [8, C])
        ut_g = at("ut_g", AR + 56.75, [8, C])
        s_g = at("s_g", AR + 70.75, [2, 4, GH])
        r_g = at("r_g", AR + 60.75, [4, GH])
        vn_g = at("vn_g", AR + 62.75, [4, GH])
        vs_g = at("vs_g", AR + 64.75, [4, GH])
        o_g = at("o_g", AR + 66.75, [TT, CW])
        sq_g = at("sq_g", AR + 70.75, [4, T])
        so_g = at("so_g", AR + 74.75, [4, T])
        ri_g = at("ri_g", AR + 74.75, [4, T])
        inv_g = [at(f"inv_g{k}", AR + kib, [8, C]) for k, kib in enumerate((10.25, 12.25, 14.25, 16.25, 78.75, 80.75))]
        w2z = at("w2z", AR + 6.25, [CW])
        a2z = at("a2z", AR + 8.25, [CW])
        g2a = at("g2a", AR + 10.25, [CW])
        g2b = at("g2b", AR + 12.25, [CW])
        rkv = [at(f"rkv{m}", AR + kib, [4, T + 1]) for m, kib in enumerate((14.25, 18.5, 22.75))]
        az = at("az", AR + 27, [4, 2, T])
        rz = at("rz", AR + 35, [4, 2, T])
        bt = at("bt", AR + 43, [4, T])
        kt = at("kt", AR + 47, [4, T])
        gt = at("gt", AR + 51, [4, T])
        tmp = [at(f"tmp{m}", AR + 55 + 4 * m, [4, T]) for m in range(8)]
        bn = at("bn", AR + 55, [TT, CW])
        kn_r = at("kn_r", AR + 59, [TT, CW])
        vn_r = at("vn_r", AR + 63, [TT, CW])
        ut_r = at("ut_r", AR + 67, [TT, 8, C])
        ak = at("ak", AR + 71, [TT, 8, C])
        rb = at("rb", AR + 75, [TT, 8, C])
        rk = at("rk", AR + 79, [TT, 8, C])
        r_r = at("r_r", AR + 14.25, [8, C])
        sa_r = at("sa_r", AR + 16.25, [8, C])
        y_r = at("y_r", AR + 18.5, [TT, CW])
        bonus = at("bonus", AR + 22.75, [4, T])
        s_r = at("s_r", AR, [2, 4, C])
        inv_r = [at(f"inv_r{k}", AR + kib, [8, C]) for k, kib in enumerate((83, 85, 6.25, 8.25, 10.25, 12.25))]
        yf = at("yf", AR, [16, T])
        yhi = at("yhi", AR + 16, [16, T], F32R)
        ylo = at("ylo", AR + 32, [16, T], F32R)
        mhi = at("mhi", AR + 48, [KT, T], F32R)
        mlo = at("mlo", AR + 64, [KT, T], F32R)
        ga = at("ga", AR + 80, [TT, CW])
        gb = at("gb", AR + 84, [TT, CW])
        msb = at("msb", AR, [TT, D])
        qt = at("qt", AR, [KT, T])
        kt_m = at("kt_m", AR + 16, [KT, T])
        v_m = at("v_m", AR + 32, [TT, D])
        pr_m = at("pr_m", AR + 80, [2, TT, T])
        pt_m = at("pt_m", AR + 84, [2, TT, T])

        gc_n = scal[:, 0:16].rearrange("p (t g) -> p t g", t=TT)
        be_n = scal[:, 16:32].rearrange("p (t g) -> p t g", t=TT)
        nbe_n = scal[:, 32:48].rearrange("p (t g) -> p t g", t=TT)
        dtb, nal = scal[0:GHV, 48:49], scal[0:GHV, 49:50]
        eps_q, eps_k, eps_gn, one_c = scal[:, 50:51], scal[:, 51:52], scal[:, 52:53], scal[:, 53:54]
        msum = scal[:, 64:80]
        mroot = scal[:, 80:96]
        msum2 = scal[:, 96:112]
        mroot2 = scal[:, 112:128]
        pc = scal[:, 128:144].rearrange("p (d c) -> p d c", d=4)
        mx = scal[:, 144:152].rearrange("p (g t) -> p g t", g=MH)
        nmx = scal[:, 152:160].rearrange("p (g t) -> p g t", g=MH)
        den = scal[:, 160:168].rearrange("p (g t) -> p g t", g=MH)
        rden = scal[:, 168:176].rearrange("p (g t) -> p g t", g=MH)

        spool_g = at("spool_g", AR + 83, [TT, CW])
        spool_r = at("spool_r", 100.75, [TT, CW])
        proj = nc.dram_tensor("proj", (17, T, CW), F32, kind="Internal").ap()
        y_turned = nc.dram_tensor("y_turned", (16, P, T), F32, kind="Internal").ap()

        bank = [pa[:, 0:2, :], pa[:, 2:4, :], pb[:, 0:2, :], pb[:, 2:4, :]]
        units = [b.rearrange("p a (u c) -> p (a u) c", c=C) for b in bank]
        heads4 = [b.rearrange("p a (u c) -> p (a u) c", c=GH) for b in bank]

        def over_units(mask):
            return mask[:, :].unsqueeze(1).to_broadcast([P, 8, C])

        INV_MM, INV_DVE, INV_ACT = 10, 9, 7

        def copy(act, dst, src):
            return nc.scalar.activation(dst, src, ACT.Copy)

        def invert_pe(pe, v, buf):
            a, b, c, d, e, f = buf
            mm_done, by_dve, by_act = sem("inv_mm"), sem("inv_dve"), sem("inv_act")
            dv, ac = INV_DVE * v, INV_ACT * v

            def blocks(out, lhs, rhs):
                for u in range(8):
                    for cp in range(2):
                        r = slice(cp * C, (cp + 1) * C)
                        right = rhs[r, u, :] if rhs is not eye else eye[r, :]
                        mm = nc.tensor.matmul(out[r, u, :], lhs[r, u, :], right, start=True, stop=True)
                return mm

            def mark(k):
                bg_pe(pe, f"inv{v}.{k}")

            pe.wait_ge(sem("inv_in"), v + 1)
            blocks(units[0], a, eye).then_inc(mm_done, 1)
            mark(1)
            pe.wait_ge(by_act, ac + 1)
            blocks(units[1], b, a)
            blocks(units[2], a, b).then_inc(mm_done, 1)
            mark(2)
            pe.wait_ge(by_dve, dv + 2)
            pe.wait_ge(by_act, ac + 2)
            blocks(units[0], d, c)
            blocks(units[3], c, d)
            blocks(units[1], d, e).then_inc(mm_done, 1)
            mark(3)
            pe.wait_ge(by_dve, dv + 4)
            pe.wait_ge(by_act, ac + 3)
            blocks(units[2], a, b)
            blocks(units[0], b, e).then_inc(mm_done, 1)
            mark(4)
            pe.wait_ge(by_dve, dv + 5)
            pe.wait_ge(by_act, ac + 4)
            blocks(units[1], c, e).then_inc(mm_done, 1)
            mark(5)
            pe.wait_ge(by_dve, dv + 6)
            blocks(units[2], e, eye).then_inc(mm_done, 1)
            mark(6)
            pe.wait_ge(by_act, ac + 5)
            blocks(units[0], d, f)
            blocks(units[3], f, d).then_inc(mm_done, 1)
            mark(7)
            pe.wait_ge(by_dve, dv + 7)
            pe.wait_ge(by_act, ac + 6)
            blocks(units[2], a, b).then_inc(mm_done, 1)
            mark(8)
            pe.wait_ge(by_act, ac + 7)
            blocks(units[1], c, e).then_inc(mm_done, 1)
            mark(9)
            pe.wait_ge(by_dve, dv + 8)
            blocks(units[0], b, d).then_inc(mm_done, 1)
            mark(10)

        def invert_act(act, v, buf, spool):
            a, b, c, d, e, f = buf
            for step, dst, u in ((1, b, 0), (2, d, 2), (3, b, 3), (4, c, 2), (6, d, 2), (7, b, 3), (8, c, 2)):
                act.wait_ge(sem("inv_mm"), INV_MM * v + step)
                copy(act, dst[:, :, :], units[u]).then_inc(sem("inv_act"), 1)
                bg_act(act, f"inv{v}.{step if step not in (4, 8) else step + 1}", spool)
            bg_act(act, f"inv{v}.10", spool)

        def invert_dve(dve, v, buf, out):
            a, b, c, d, e, f = buf

            def step(n, ins_of):
                dve.wait_ge(sem("inv_mm"), INV_MM * v + n)
                ins_of().then_inc(sem("inv_dve"), 1)

            v_ = nc.vector
            v_.tensor_tensor(e[:, :, :], a[:, :, :], over_units(eye), ALU.add).then_inc(sem("inv_dve"), 1)
            bg_dve(dve, f"inv{v}.1")
            step(2, lambda: v_.tensor_copy(c[:, :, :], units[1]))
            bg_dve(dve, f"inv{v}.2")
            step(3, lambda: v_.tensor_copy(a[:, :, :], units[0]))
            step(3, lambda: v_.tensor_tensor(e[:, :, :], e[:, :, :], units[1], ALU.add))
            bg_dve(dve, f"inv{v}.3")
            step(4, lambda: v_.tensor_tensor(e[:, :, :], e[:, :, :], units[0], ALU.add))
            bg_dve(dve, f"inv{v}.4")
            step(5, lambda: v_.tensor_tensor(e[:, :, :], e[:, :, :], units[1], ALU.add))
            bg_dve(dve, f"inv{v}.6")
            step(7, lambda: v_.tensor_copy(a[:, :, :], units[0]))
            bg_dve(dve, f"inv{v}.8")
            step(9, lambda: v_.tensor_tensor(d[:, :, :], e[:, :, :], units[1], ALU.add))
            bg_dve(dve, f"inv{v}.9")
            step(10, lambda: v_.tensor_tensor(out, d[:, :, :], units[0], ALU.add))
            bg_dve(dve, f"inv{v}.10")
            dve.wait_ge(sem("inv_dve"), INV_DVE * (v + 1))

        def mix_nat(dve, pr, m):
            dve.wait_ge(slot_used, pr["done"])
            if m > 0:
                dve.wait_ge(sem("mix_turned"), m)
            nc.vector.tensor_copy(nat[:, :, :], pair(pr["par"])).then_inc(sem(pr["released"][0]), 1)

        def mix_turn(pe, m, src, ready):
            pe.wait_ge(*ready)
            if m > 0:
                pe.wait_ge(sem("mix_take"), m)
            for kk in range(4):
                for tt in range(TT):
                    mm = nc.tensor.transpose(pa[:, kk, tt * P:(tt + 1) * P], src[:, tt, kk * P:(kk + 1) * P], ident[:, :])
            mm.then_inc(sem("mix_turned"), 1)

        def mix_take(dve, dst, m):
            dve.wait_ge(sem("mix_turned"), m + 1)
            nc.vector.tensor_copy(dst, pa[:, :, :]).then_inc(sem("mix_take"), 1)
            dve.wait_ge(sem("mix_take"), m + 1)

        AUX = prods["aux"][0]

        def aux_pe(pe):
            multiply(pe, AUX, AUX["free"], (xhi, xlo), width=AUXW)
            pe.wait_ge(sem(AUX["released"][0]), AUX["released"][1])
            for tt in range(TT):
                tok = slice(tt * P, (tt + 1) * P)
                nc.tensor.transpose(pa[:, 0, tok], nat[:, tt, 0:P], ident[:, :])
                nc.tensor.transpose(pa[:, 1, tok], nat[:, tt, P:2 * P], ident[:, :])
                nc.tensor.transpose(pa[0:32, 2, tok], nat[:, tt, 2 * P:LORA], ident[:, :])
                nc.tensor.transpose(pa[0:GHV, 3, tok], nat[:, tt, LORA:LORA + GHV], ident[:, :])
                mm = nc.tensor.transpose(pb[0:GHV, 0, tok], nat[:, tt, LORA + GHV:AUXW], ident[:, :])
            mm.then_inc(sem("aux_turned"), 1)
            pe.wait_ge(sem("gc_ready"), 1)
            for tt in range(TT):
                tok = slice(tt * P, (tt + 1) * P)
                nc.tensor.transpose(pb[:, 2, 8 * tt:8 * tt + 8], gc_t[0:GHV, tok], ident[0:GHV, 0:GHV])
                mm = nc.tensor.transpose(pb[:, 2, 16 + 8 * tt:24 + 8 * tt], beta_t[0:GHV, tok], ident[0:GHV, 0:GHV])
            mm.then_inc(sem("scalars_turned"), 1)

        def aux_dve(dve):
            v_ = nc.vector
            for cell, value in ((eps_q, RMS_EPS * GH), (eps_k, RMS_EPS), (eps_gn, RW_GN_EPS), (one_c, 1.0)):
                link(dve, v_.memset(cell, value))
            dve.wait_ge(slot_used, AUX["done"])
            v_.tensor_copy(nat[:, :, 0:AUXW], pair(AUX["par"])[:, :, 0:AUXW]).then_inc(sem(AUX["released"][0]), 1)
            link(dve, v_.memset(auxt[:, :, :], 0.0))
            dve.wait_ge(sem("aux_turned"), 1)
            v_.tensor_copy(auxt[:, 0:2, 1:T + 1], pa[:, 0:2, :])
            link(dve, v_.tensor_copy(auxt[0:32, 2, 1:T + 1], pa[0:32, 2, :]))
            link(dve, v_.tensor_tensor(lora[:, :, :], auxt[:, :, 0:T], auxt[:, :, 1:T + 1], ALU.subtract))
            for m, name in enumerate(("mu_wa", "mu_g0", "mu_g1")):
                op = v_.scalar_tensor_tensor(lora[:, m, :], lora[:, m, :], prm[:, PRM[name]:PRM[name] + 1],
                                             auxt[:, m, 1:T + 1], ALU.mult, ALU.add)
            op.then_inc(sem("lora_mixed"), 1)
            dve.wait_ge(sem("gdn_loaded"), 32)
            v_.tensor_copy(beta_t[0:GHV, :], pa[0:GHV, 3, :]).then_inc(sem("beta_raw"), 1)
            link(dve, v_.tensor_scalar(sp_a[0:GHV, :], pb[0:GHV, 0, :], dtb, None, ALU.add))
            link(dve, v_.tensor_scalar(gc_t[0:GHV, :], sp_a[0:GHV, :], -1.0, None, ALU.mult))
            v_.tensor_tensor(sp_b[0:GHV, :], sp_a[0:GHV, :], gc_t[0:GHV, :], ALU.max).then_inc(sem("abs_ready"), 1)
            dve.wait_ge(sem("ln_ready"), 1)
            link(dve, v_.scalar_tensor_tensor(sp_a[0:GHV, :], sp_a[0:GHV, :], 0.0, sp_b[0:GHV, :], ALU.max, ALU.add))
            link(dve, v_.tensor_scalar(nal, nal, -1.0, None, ALU.mult))
            link(dve, v_.tensor_scalar(sp_a[0:GHV, :], sp_a[0:GHV, :], nal, None, ALU.mult))
            v_.tensor_tensor_scan(gc_t[0:GHV, :], scanmask[0:GHV, :], sp_a[0:GHV, :], 0.0, ALU.mult, ALU.add).then_inc(sem("gc_ready"), 1)
            dve.wait_ge(sem("scalars_turned"), 1)
            v_.tensor_copy(scal[:, 0:32], pb[:, 2, 0:32]).then_inc(sem("scalars_ready"), 1)
            dve.wait_ge(sem("exp_gc"), 1)
            link(dve, v_.scalar_tensor_tensor(scal[:, 32:48], scal[:, 32:48], -1.0, scal[:, 16:32], ALU.mult, ALU.mult))

        def aux_act(act):
            act.wait_ge(sem("lora_mixed"), 1)
            nc.scalar.activation(lora[0:LORA_D, 0, :], lora[0:LORA_D, 0, :], ACT.Tanh)
            nc.scalar.activation(lora[:, 1:3, :], lora[:, 1:3, :], ACT.Sigmoid)
            act.wait_ge(sem("beta_raw"), 1)
            link(act, nc.scalar.activation(beta_t[0:GHV, :], beta_t[0:GHV, :], ACT.Sigmoid))
            act.wait_ge(sem("gdn_loaded"), 32)
            link(act, nc.scalar.activation(nal, nal, ACT.Exp))
            act.wait_ge(sem("abs_ready"), 1)
            link(act, nc.scalar.activation(sp_b[0:GHV, :], sp_b[0:GHV, :], ACT.Exp, scale=-1.0))
            nc.scalar.activation(sp_b[0:GHV, :], sp_b[0:GHV, :], ACT.Ln, bias=one_c[0:GHV, :]).then_inc(sem("ln_ready"), 1)
            act.wait_ge(sem("scalars_ready"), 1)
            nc.scalar.activation(scal[:, 32:48], scal[:, 0:16], ACT.Exp).then_inc(sem("exp_gc"), 1)

        def gdn_pe(pe, hf):
            g = prods[f"gdn{hf}"]
            n = hf + 1
            if hf == 0:
                multiply(pe, g[0], g[0]["free"], (xhi, xlo))
                multiply(pe, g[1], g[1]["free"], (xhi, xlo))
                mix_turn(pe, 0, nat, (sem(g[0]["released"][0]), g[0]["released"][1]))
                multiply(pe, g[2], g[2]["free"], (xhi, xlo))
                mix_turn(pe, 1, nat, (sem(g[1]["released"][0]), g[1]["released"][1]))
            else:
                pe.wait_ge(sem("y_ready"), 1)
                mix_turn(pe, 2, gs, (sem("gs_loaded"), 16))
                mix_turn(pe, 3, nat, (sem("nat_loaded"), 16))
            bg_pe(pe, f"gdn{hf}.conv")
            pe.wait_ge(sem("g_sq"), n)
            for kk in range(4):
                mm = nc.tensor.matmul(pb[:, kk, :], ones[:, :], sq_g[:, kk, :], start=True, stop=True)
            mm.then_inc(sem("g_norms"), 1)
            bg_pe(pe, f"gdn{hf}.norms")
            pe.wait_ge(sem("mix_take"), 2 * n)
            pe.wait_ge(sem("g_rooted"), n)
            for hl in range(4):
                hv = 4 * hf + hl
                nc.tensor.matmul(pa[:, hl, :], sel[0:GHV, hv, :], gc_t[0:GHV, :], start=True, stop=True)
                mm = nc.tensor.matmul(pb[:, hl, :], sel[0:GHV, hv, :], beta_t[0:GHV, :], start=True, stop=True)
            mm.then_inc(sem("g_rows"), 1)
            bg_pe(pe, f"gdn{hf}.rows")
            pe.wait_ge(sem("g_qk"), n)
            pe.wait_ge(sem("g_dec"), n)
            pe.wait_ge(sem("g_vact"), n)
            for tt in range(TT):
                tok = slice(tt * P, (tt + 1) * P)
                for kk in range(2):
                    nc.tensor.transpose(bank[2][:, tt, kk * P:(kk + 1) * P], qk[:, 2 + kk, tok], ident[:, :])
                for kk in range(4):
                    mm = nc.tensor.transpose(bank[tt][:, kk // 2, (kk % 2) * P:(kk % 2 + 1) * P], vg[:, kk, tok], ident[:, :])
            mm.then_inc(sem("g_naturals"), 1)
            bg_pe(pe, f"gdn{hf}.naturals")
            pe.wait_ge(sem("g_kb"), n)
            for u in range(8):
                tt, hl = u // 4, u % 4
                for cp in range(2):
                    r = slice(cp * C, (cp + 1) * C)
                    tok = slice(tt * P + cp * C, tt * P + (cp + 1) * C)
                    nc.tensor.matmul(units[2][r, u, :], qk[:, 2 + hl // 2, tok], kb[:, hl, tok], start=True, stop=True)
                    mm = nc.tensor.matmul(units[3][r, u, :], qk[:, 2 + hl // 2, tok], qk[:, hl // 2, tok], start=True, stop=True)
            mm.then_inc(sem("g_mats"), 1)
            bg_pe(pe, f"gdn{hf}.mats")
            invert_pe(pe, hf, inv_g)
            pe.wait_ge(sem("inv_dve"), INV_DVE * n)
            for c in range(NCH):
                tt, cp = c // 2, c % 2
                r = slice(cp * C, (cp + 1) * C)
                tok = slice(c * C, (c + 1) * C)
                m = NCH * hf + c
                pe.wait_ge(sem("g_state"), (NCH + 1) * hf + c + 1)
                for hl in range(4):
                    mm = nc.tensor.matmul(heads4[0][r, hl, :], qk[:, 2 + hl // 2, tok], s_g[:, c % 2, hl, :], start=True, stop=True)
                mm.then_inc(sem("g_ks"), 1)
                bg_pe(pe, f"gdn{hf}.ks{c}")
                pe.wait_ge(sem("g_r"), m + 1)
                for hl in range(4):
                    mm = nc.tensor.matmul(heads4[1][r, hl, :], ut_g[r, 4 * tt + hl, :], r_g[r, hl, :], start=True, stop=True)
                mm.then_inc(sem("g_vnew"), 1)
                bg_pe(pe, f"gdn{hf}.vnew{c}")
                pe.wait_ge(sem("g_vn"), m + 1)
                for hl in range(4):
                    mm = nc.tensor.matmul(heads4[3][:, hl, :], kn[r, tt, (hl // 2) * P:(hl // 2 + 1) * P], vs_g[r, hl, :],
                                          start=True, stop=True)
                mm.then_inc(sem("g_ds"), 1)
                if m > 0:
                    pe.wait_ge(sem("g_o"), m)
                for hl in range(4):
                    nc.tensor.matmul(heads4[2][r, hl, :], qe[:, hl, tok], s_g[:, c % 2, hl, :], start=True, stop=False)
                    mm = nc.tensor.matmul(heads4[2][r, hl, :], att[r, 4 * tt + hl, :], vn_g[r, hl, :], start=False, stop=True)
                mm.then_inc(sem("g_omm"), 1)
                bg_pe(pe, f"gdn{hf}.state{c}")
            bg_pe(pe, f"gdn{hf}.out")
            pe.wait_ge(sem("g_out"), n)
            for kk in range(4):
                for tt in range(TT):
                    mm = nc.tensor.transpose(pa[:, kk, tt * P:(tt + 1) * P], nat[:, tt, kk * P:(kk + 1) * P], ident[:, :])
            mm.then_inc(sem("g_out_turned"), 1)

        def gdn_act(act, hf):
            g = prods[f"gdn{hf}"]
            n = hf + 1

            def bg(name):
                bg_act(act, f"gdn{hf}.{name}", spool_g)

            if hf == 0:
                for m in range(3):
                    for j in range(RING if m == 0 else 0, KT // SK):
                        split_hi(act, g[m]["slot"], j)
                next_hi(act, "gdn1")
                act.wait_ge(slot_used, g[2]["done"])
                nc.scalar.activation(zg[:, :, :], pair(g[2]["par"]), ACT.Silu).then_inc(sem(g[2]["released"][0]), 1)
            else:
                act.wait_ge(sem("z_loaded"), 16)
                nc.scalar.activation(zg[:, :, :], zg[:, :, :], ACT.Silu).then_inc(sem("z_act"), 1)
            bg("conv")
            act.wait_ge(sem("g_conv"), 2 * hf + 1)
            link(act, nc.scalar.activation(qk[:, :, :], qk[:, :, :], ACT.Silu))
            nc.scalar.activation(sq_g[:, :, :], qk[:, :, :], ACT.Square).then_inc(sem("g_sq"), 1)
            act.wait_ge(sem("g_conv"), 2 * n)
            nc.scalar.activation(vg[:, :, :], vg[:, :, :], ACT.Silu).then_inc(sem("g_vact"), 1)
            act.wait_ge(sem("g_norms"), n)
            nc.scalar.activation(ri_g[:, 0:2, :], pb[:, 0:2, :], ACT.Sqrt, bias=eps_q, scale=float(GH))
            nc.scalar.activation(ri_g[:, 2:4, :], pb[:, 2:4, :], ACT.Sqrt, bias=eps_k).then_inc(sem("g_rooted"), 1)
            bg("norms")
            act.wait_ge(sem("g_rows"), n)
            nc.scalar.activation(eg[:, :, :], pa[:, :, :], ACT.Exp)
            copy(act, bb[:, :, :], pb[:, :, :]).then_inc(sem("g_eg"), 1)
            bg("rows")
            act.wait_ge(sem("g_diff"), n)
            nc.scalar.activation(dec[:, :, :], dec[:, :, :], ACT.Exp).then_inc(sem("g_decexp"), 1)
            bg("mats")
            invert_act(act, hf, inv_g, spool_g)
            for c in range(NCH):
                tt, cp = c // 2, c % 2
                r = slice(cp * C, (cp + 1) * C)
                bg(f"vnew{c}")
                act.wait_ge(sem("g_omm"), NCH * hf + c + 1)
                op = copy(act, o_g[r, tt, :], heads4[2][r, :, :].rearrange("p h d -> p (h d)"))
                op.then_inc(sem("g_o"), 1)
                bg(f"state{c}")
            act.wait_ge(sem("g_o"), NCH * n)
            nc.scalar.activation(so_g[:, :, :].rearrange("p a t -> p (a t)"), o_g[:, :, :].rearrange("p t d -> p (t d)"),
                                 ACT.Square).then_inc(sem("g_osq"), 1)
            act.wait_ge(sem("g_oms"), n)
            nc.scalar.activation(mroot[:, 0:8], msum[:, 0:8], ACT.Sqrt, bias=eps_k, scale=1.0 / GH).then_inc(sem("g_oroot"), 1)
            bg("out")

        def gdn_dve(dve, hf):
            g = prods[f"gdn{hf}"]
            n = hf + 1
            v_ = nc.vector
            link(dve, v_.memset(qkp[:, :, 0:CONV - 1], 0.0))
            link(dve, v_.memset(vp[:, :, 0:CONV - 1], 0.0))

            def bg(name):
                bg_dve(dve, f"gdn{hf}.{name}")

            if hf == 0:
                for j in range(RING, KT // SK):
                    split_lo(dve, g[0]["slot"], j)
                for j in range(KT // SK):
                    split_lo(dve, g[1]["slot"], j)
                    if j == 4:
                        mix_nat(dve, g[0], 0)
                for j in range(KT // SK):
                    split_lo(dve, g[2]["slot"], j)
                    if j == 4:
                        mix_take(dve, qkp[:, :, CONV - 1:], 0)
                        mix_nat(dve, g[1], 1)
                next_lo(dve, "gdn1")
            else:
                mix_take(dve, qkp[:, :, CONV - 1:], 2)
            mix_take(dve, vp[:, :, CONV - 1:], 2 * hf + 1)

            def conv(dst, src, tiles):
                for kk, tile in enumerate(tiles):
                    for tap in range(CONV):
                        w = prm[:, PRM["conv"] + 16 * tap + tile:PRM["conv"] + 16 * tap + tile + 1]
                        x = src[:, kk, tap:tap + T]
                        if tap == 0:
                            link(dve, v_.tensor_scalar(dst[:, kk, :], x, w, None, ALU.mult))
                        elif tap < CONV - 1:
                            link(dve, v_.scalar_tensor_tensor(dst[:, kk, :], x, w, dst[:, kk, :], ALU.mult, ALU.add))
                        else:
                            op = v_.scalar_tensor_tensor(dst[:, kk, :], x, w, dst[:, kk, :], ALU.mult, ALU.add)
                op.then_inc(sem("g_conv"), 1)

            conv(qk, qkp, [2 * hf, 2 * hf + 1, 4 + 2 * hf, 5 + 2 * hf])
            bg("conv")
            conv(vg, vp, [8 + 4 * hf + k for k in range(4)])
            dve.wait_ge(sem("g_conv"), 2 * n)
            dve.wait_ge(sem("g_rooted"), n)
            bg("norms")
            link(dve, v_.reciprocal(ri_g[:, :, :], ri_g[:, :, :]))
            v_.tensor_tensor(qk[:, :, :], qk[:, :, :], ri_g[:, :, :], ALU.mult).then_inc(sem("g_qk"), 1)
            dve.wait_ge(sem("g_eg"), n)
            for tt in range(TT):
                for cp in range(2):
                    r = slice(cp * C, (cp + 1) * C)
                    tok = slice(tt * P + cp * C, tt * P + (cp + 1) * C)
                    own = gc_n[r, tt, 4 * hf:4 * hf + 4].unsqueeze(2).to_broadcast([C, 4, C])
                    op = v_.tensor_tensor(dec[r, 4 * tt:4 * tt + 4, :], pa[r, :, tok], own, ALU.subtract)
            link(dve, op)
            v_.tensor_scalar(dec[:, :, :], dec[:, :, :], 0.0, None, ALU.min).then_inc(sem("g_diff"), 1)
            dve.wait_ge(sem("g_decexp"), n)
            v_.tensor_tensor(dec[:, :, :], dec[:, :, :], over_units(m_inc), ALU.mult).then_inc(sem("g_dec"), 1)
            dve.wait_ge(sem("g_qk"), n)
            for hl in range(4):
                v_.tensor_tensor(kb[:, hl, :], qk[:, 2 + hl // 2, :], bb[:, hl, :], ALU.mult)
                v_.tensor_tensor(qe[:, hl, :], qk[:, hl // 2, :], eg[:, hl, :], ALU.mult)
            bg("rows")
            dve.wait_ge(sem("g_naturals"), n)
            v_.tensor_copy(kn[:, :, :], bank[2])
            for tt in range(TT):
                own = be_n[:, tt, 4 * hf:4 * hf + 4].unsqueeze(2).to_broadcast([P, 4, GH])
                op = v_.tensor_tensor(vb[:, tt, :].rearrange("p (h d) -> p h d", h=4), heads4[tt], own, ALU.mult)
            op.then_inc(sem("g_kb"), 1)
            bg("naturals")
            dve.wait_ge(sem("g_mats"), n)
            dve.wait_ge(sem("g_dec"), n)
            v_.tensor_tensor(att[:, :, :], units[3], dec[:, :, :], ALU.mult)
            link(dve, v_.scalar_tensor_tensor(inv_g[1][:, :, :], units[2], -1.0, dec[:, :, :], ALU.mult, ALU.mult))
            v_.tensor_tensor(inv_g[5][:, :, :], inv_g[1][:, :, :], over_units(m_upo), ALU.mult)
            v_.tensor_tensor(inv_g[0][:, :, :], inv_g[1][:, :, :], over_units(m_upd), ALU.mult).then_inc(sem("inv_in"), 1)
            bg("mats")
            dve.wait_ge(sem("inv_in"), n)
            invert_dve(dve, hf, inv_g, ut_g[:, :, :])
            v_.memset(s_g[:, 0, :, :], 0.0).then_inc(sem("g_state"), 1)
            dve.wait_ge(sem("g_state"), (NCH + 1) * hf + 1)
            for c in range(NCH):
                tt, cp = c // 2, c % 2
                r = slice(cp * C, (cp + 1) * C)
                m = NCH * hf + c
                own = nbe_n[r, tt, 4 * hf:4 * hf + 4].unsqueeze(2).to_broadcast([C, 4, GH])
                dve.wait_ge(sem("g_ks"), m + 1)
                link(dve, v_.tensor_tensor(r_g[r, :, :], heads4[0][r, :, :], own, ALU.mult))
                v_.tensor_tensor(r_g[r, :, :], r_g[r, :, :], vb[r, tt, :].rearrange("p (h d) -> p h d", h=4), ALU.add).then_inc(sem("g_r"), 1)
                bg(f"ks{c}")
                dve.wait_ge(sem("g_vnew"), m + 1)
                v_.tensor_copy(vn_g[r, :, :], heads4[1][r, :, :])
                last = dec[r, 4 * tt:4 * tt + 4, C - 1:C].to_broadcast([C, 4, GH])
                v_.tensor_tensor(vs_g[r, :, :], heads4[1][r, :, :], last, ALU.mult).then_inc(sem("g_vn"), 1)
                bg(f"vnew{c}")
                dve.wait_ge(sem("g_ds"), m + 1)
                if c > 0:
                    dve.wait_ge(sem("g_omm"), m)
                for hl in range(4):
                    end = (c + 1) * C - 1
                    op = v_.scalar_tensor_tensor(s_g[:, (c + 1) % 2, hl, :], s_g[:, c % 2, hl, :], eg[:, hl, end:end + 1],
                                                 heads4[3][:, hl, :], ALU.mult, ALU.add)
                op.then_inc(sem("g_state"), 1)
                bg(f"state{c}")
                dve.wait_ge(sem("g_state"), (NCH + 1) * hf + c + 2)
            dve.wait_ge(sem("g_osq"), n)
            v_.tensor_reduce(msum[:, 0:8], so_g[:, :, :].rearrange("p a (h d) -> p (a h) d", d=GH), AX_X, ALU.add).then_inc(sem("g_oms"), 1)
            dve.wait_ge(sem("g_oroot"), n)
            link(dve, v_.reciprocal(mroot2[:, 0:8], mroot[:, 0:8]))
            link(dve, v_.tensor_tensor(o_g[:, :, :].rearrange("p t (h d) -> p (t h) d", d=GH),
                                       o_g[:, :, :].rearrange("p t (h d) -> p (t h) d", d=GH),
                                       mroot2[:, 0:8].unsqueeze(2).to_broadcast([P, 8, GH]), ALU.mult))
            if hf == 0:
                dve.wait_ge(sem(g[2]["released"][0]), g[2]["released"][1])
            else:
                dve.wait_ge(sem("z_act"), 1)
            dve.wait_ge(sem("mix_turned"), 2 * n)
            v_.tensor_tensor(nat[:, :, :], o_g[:, :, :], zg[:, :, :], ALU.mult).then_inc(sem("g_out"), 1)
            bg("out")
            dve.wait_ge(sem("g_out_turned"), n)
            if hf > 0:
                dve.wait_ge(sem("y_stored"), 16 * hf)
            v_.tensor_scalar(xf[:, :, :], pa[:, :, :], prm[:, PRM["gdn_norm"]:PRM["gdn_norm"] + 1], None, ALU.mult).then_inc(sem("y_ready"), 1)
            dve.wait_ge(sem("y_ready"), n)

        def rw_pe(pe, hf):
            n = hf + 1
            m0 = 2 * HALVES + 3 * hf
            pe.wait_ge(sem("y_ready"), HALVES + hf)
            pe.wait_ge(sem("lora_loaded"), 64 * n)
            for dt in range(4):
                cols = slice(dt * P, (dt + 1) * P)
                nc.tensor.matmul(pa[:, dt, :], w2z[:, cols], lora[:, 0, :], start=True, stop=True)
                mm = nc.tensor.matmul(pb[:, dt, :], a2z[:, cols], lora[:, 0, :], start=True, stop=True)
            mm.then_inc(sem("r_lora"), 1)
            bg_pe(pe, f"rw{hf}.lora")
            pe.wait_ge(sem("r_sig"), n)
            for dt in range(4):
                cols = slice(dt * P, (dt + 1) * P)
                nc.tensor.matmul(pa[:, dt, :], g2a[:, cols], lora[:, 1, :], start=True, stop=False)
                mm = nc.tensor.matmul(pa[:, dt, :], g2b[0:32, cols], lora[0:32, 2, :], start=False, stop=True)
            mm.then_inc(sem("r_g"), 1)
            bg_pe(pe, f"rw{hf}.g")
            pe.wait_ge(sem("r_gt"), n)
            mix_turn(pe, m0, gs, (sem("gs_loaded"), 16 * (2 + 2 * hf)))
            bg_pe(pe, f"rw{hf}.r")
            mix_turn(pe, m0 + 1, nat, (sem("nat_loaded"), 16 * (2 + hf)))
            bg_pe(pe, f"rw{hf}.k")
            mix_turn(pe, m0 + 2, gs, (sem("gs_loaded"), 16 * (3 + 2 * hf)))
            for name in ("v", "shift"):
                bg_pe(pe, f"rw{hf}.{name}")
            pe.wait_ge(sem("r_kksq"), n)
            for dt in range(4):
                mm = nc.tensor.matmul(pb[:, dt, :], headones[:, :], gs_t[:, dt, :], start=True, stop=True)
            mm.then_inc(sem("r_kknorm"), 1)
            bg_pe(pe, f"rw{hf}.kk")
            pe.wait_ge(sem("r_rkk"), n)
            pe.wait_ge(sem("mix_take"), m0 + 3)
            for dt in range(4):
                mm = nc.tensor.matmul(pa[:, dt, :], headones[:, :], nat_t[:, dt, :], start=True, stop=True)
            mm.then_inc(sem("r_bonus"), 1)
            for name in ("tilde", "bonus"):
                bg_pe(pe, f"rw{hf}.{name}")
            pe.wait_ge(sem("r_tilde"), n)
            for k, (src, banks, need) in enumerate(((bt, bank[2:4], None), (kt, bank[0:2], "r_bonus_out"), (tmp[2], bank[2:4], "r_nat"))):
                if need is not None:
                    pe.wait_ge(sem(need), n if need == "r_bonus_out" else 3 * hf + 1)
                for tt in range(TT):
                    for dt in range(4):
                        mm = nc.tensor.transpose(banks[tt][:, dt // 2, (dt % 2) * P:(dt % 2 + 1) * P],
                                                 src[:, dt, tt * P:(tt + 1) * P], ident[:, :])
                mm.then_inc(sem("r_nat_turned"), 1)
            bg_pe(pe, f"rw{hf}.nat")
            for tt in range(TT):
                v = HALVES + TT * hf + tt
                if tt == 0:
                    pe.wait_ge(sem("r_nat"), 3 * n)
                else:
                    pe.wait_ge(sem("inv_dve"), INV_DVE * v)
                for u in range(8):
                    for cp in range(2):
                        r = slice(cp * C, (cp + 1) * C)
                        tok = slice(tt * P + cp * C, tt * P + (cp + 1) * C)
                        for k, (left, right) in enumerate(((bt, az), (bt, rz), (kt, az), (kt, rz))):
                            mm = nc.tensor.matmul(units[k][r, u, :], left[:, u // 2, tok], right[:, u // 2, u % 2, tok],
                                                  start=True, stop=True)
                mm.then_inc(sem("r_mats"), 1)
                bg_pe(pe, f"rw{hf}.mats{tt}")
                invert_pe(pe, v, inv_r)
            pe.wait_ge(sem("inv_dve"), INV_DVE * (HALVES + TT * n))
            for c in range(NCH):
                tt, cp = c // 2, c % 2
                r = slice(cp * C, (cp + 1) * C)
                tok = slice(c * C, (c + 1) * C)
                m = NCH * hf + c
                s_in = s_r[:, c % 2, :, :]
                pe.wait_ge(sem("r_state"), m + hf + 1)
                for u in range(8):
                    nc.tensor.matmul(units[0][r, u, :], az[:, u // 2, u % 2, tok], s_in[:, u // 2, :], start=True, stop=False)
                    mm = nc.tensor.matmul(units[0][r, u, :], ak[r, tt, u, :], vn_r[r, tt, u * C:(u + 1) * C], start=False, stop=True)
                mm.then_inc(sem("r_rmm"), 1)
                bg_pe(pe, f"rw{hf}.r{c}")
                pe.wait_ge(sem("r_r"), m + 1)
                for u in range(8):
                    mm = nc.tensor.matmul(units[1][r, u, :], ut_r[r, tt, u, :], r_r[r, u, :], start=True, stop=True)
                mm.then_inc(sem("r_samm"), 1)
                bg_pe(pe, f"rw{hf}.sa{c}")
                pe.wait_ge(sem("r_sa"), m + 1)
                for u in range(8):
                    out = heads_state[(u % 2) * C:(u % 2 + 1) * C, u // 2, :]
                    cols = slice(u * C, (u + 1) * C)
                    nc.tensor.matmul(out, bn[r, tt, cols], sa_r[r, u, :], start=True, stop=False)
                    mm = nc.tensor.matmul(out, kn_r[r, tt, cols], vn_r[r, tt, cols], start=False, stop=True)
                mm.then_inc(sem("r_ds"), 1)
                if m > 0:
                    pe.wait_ge(sem("r_y"), m)
                for u in range(8):
                    cols = slice(u * C, (u + 1) * C)
                    nc.tensor.matmul(units[2][r, u, :], rz[:, u // 2, u % 2, tok], s_in[:, u // 2, :], start=True, stop=False)
                    nc.tensor.matmul(units[2][r, u, :], rb[r, tt, u, :], sa_r[r, u, :], start=False, stop=False)
                    mm = nc.tensor.matmul(units[2][r, u, :], rk[r, tt, u, :], vn_r[r, tt, cols], start=False, stop=True)
                mm.then_inc(sem("r_ymm"), 1)
                bg_pe(pe, f"rw{hf}.y{c}")
            bg_pe(pe, f"rw{hf}.out" if hf == 0 else "rest")
            pe.wait_ge(sem("r_out"), n)
            for kk in range(4):
                for tt in range(TT):
                    mm = nc.tensor.transpose(pa[:, kk, tt * P:(tt + 1) * P], nat[:, tt, kk * P:(kk + 1) * P], ident[:, :])
            mm.then_inc(sem("r_out_turned"), 1)

        def rw_act(act, hf):
            n = hf + 1

            def bg(name):
                bg_act(act, f"rw{hf}.{name}", spool_r)

            act.wait_ge(sem("r_lora"), n)
            for dt in range(4):
                b = 4 * hf + dt
                nc.scalar.activation(tmp[3][:, dt, :], pa[:, dt, :], ACT.Sigmoid, bias=prm[:, PRM["w0"] + b:PRM["w0"] + b + 1])
            for dt in range(4):
                b = 4 * hf + dt
                op = nc.scalar.activation(tmp[4][:, dt, :], pb[:, dt, :], ACT.Sigmoid, bias=prm[:, PRM["a0"] + b:PRM["a0"] + b + 1])
            op.then_inc(sem("r_sig"), 1)
            bg("lora")
            act.wait_ge(sem("r_g"), n)
            copy(act, gt[:, :, :], pa[:, :, :]).then_inc(sem("r_gt"), 1)
            for name in ("g", "r", "k", "v", "shift"):
                bg(name)
            act.wait_ge(sem("r_kk0"), n)
            act.wait_ge(sem("mix_turned"), 7 + 3 * hf)
            nc.scalar.activation(gs_t[:, :, :], xf[:, :, :], ACT.Square).then_inc(sem("r_kksq"), 1)
            act.wait_ge(sem("r_kknorm"), n)
            nc.scalar.activation(gs_t[:, :, :], pb[:, :, :], ACT.Sqrt, bias=eps_k).then_inc(sem("r_kkroot"), 1)
            act.wait_ge(sem("r_cum"), n)
            nc.scalar.activation(tmp[6][:, :, :], tmp[5][:, :, :], ACT.Exp)
            nc.scalar.activation(tmp[7][:, :, :], tmp[5][:, :, :], ACT.Exp, scale=-1.0).then_inc(sem("r_exp"), 1)
            bg("kk")
            act.wait_ge(sem("r_cumx"), n)
            nc.scalar.activation(tmp[5][:, :, :], tmp[5][:, :, :], ACT.Exp).then_inc(sem("r_expx"), 1)
            for name in ("tilde", "bonus", "nat"):
                bg(name)
            for tt in range(TT):
                bg(f"mats{tt}")
                invert_act(act, HALVES + TT * hf + tt, inv_r, spool_r)
            for c in range(NCH):
                tt, cp = c // 2, c % 2
                r = slice(cp * C, (cp + 1) * C)
                m = NCH * hf + c
                act.wait_ge(sem("r_rmm"), m + 1)
                copy(act, r_r[r, :, :], units[0][r, :, :]).then_inc(sem("r_r"), 1)
                bg(f"r{c}")
                act.wait_ge(sem("r_samm"), m + 1)
                copy(act, sa_r[r, :, :], units[1][r, :, :]).then_inc(sem("r_sa"), 1)
                bg(f"sa{c}")
                act.wait_ge(sem("r_ymm"), m + 1)
                copy(act, y_r[r, tt, :], units[2][r, :, :].rearrange("p u c -> p (u c)")).then_inc(sem("r_y"), 1)
                bg(f"y{c}")
            if hf > 0:
                bg_act(act, "rest", spool_r)
                spool_out(act, len(BG) - 1, spool_r)
            else:
                bg("out")
            act.wait_ge(sem("r_cent"), n)
            nc.scalar.activation(gs[:, :, :], y_r[:, :, :], ACT.Square).then_inc(sem("r_centsq"), 1)
            act.wait_ge(sem("r_var"), n)
            nc.scalar.activation(mroot[:, :], msum[:, :], ACT.Sqrt, bias=eps_gn, scale=1.0 / RH).then_inc(sem("r_std"), 1)

        def rw_dve(dve, hf):
            n = hf + 1
            m0 = 2 * HALVES + 3 * hf
            v_ = nc.vector

            def col(name, dt):
                k = PRM[name] + 4 * hf + dt
                return prm[:, k:k + 1]

            if hf == 0:
                link(dve, v_.memset(az[:, :, :, :], 0.0))
                link(dve, v_.memset(rz[:, :, :, :], 0.0))
            link(dve, v_.memset(w2z[:, :], 0.0))
            v_.memset(a2z[:, :], 0.0).then_inc(sem("lora_clear"), 1)
            for m in range(3):
                link(dve, v_.memset(rkv[m][:, :, 0:1], 0.0))

            def bg(name):
                bg_dve(dve, f"rw{hf}.{name}")

            if hf == 0:
                dve.wait_ge(sem("spooled"), 16 * spooled_before)
            bg("lora")
            bg("g")
            for m in range(3):
                mix_take(dve, rkv[m][:, :, 1:T + 1], m0 + m)
                bg("rkv"[m])
                link(dve, v_.tensor_tensor(tmp[m][:, :, :], rkv[m][:, :, 0:T], rkv[m][:, :, 1:T + 1], ALU.subtract))
                for dt in range(4):
                    k = PRM["mu_rkv"] + 8 * m + 4 * hf + dt
                    op = v_.scalar_tensor_tensor(tmp[m][:, dt, :], tmp[m][:, dt, :], prm[:, k:k + 1], rkv[m][:, dt, 1:T + 1],
                                                 ALU.mult, ALU.add)
                link(dve, op)
            r_, k_, v__, sg, a_, cum, ecum, encum = tmp
            bg("shift")
            dve.wait_ge(sem("y_stored"), 16 * (HALVES + hf))
            for dt in range(4):
                op = v_.tensor_scalar(xf[:, dt, :], k_[:, dt, :], col("k_k", dt), None, ALU.mult)
            op.then_inc(sem("r_kk0"), 1)
            dve.wait_ge(sem("r_sig"), n)
            link(dve, v_.tensor_scalar(sg[:, :, :], sg[:, :, :], -EXP_HALF, None, ALU.mult))
            for dt in range(4):
                op = v_.tensor_tensor_scan(cum[:, dt, :], scanmask[:, :], sg[:, dt, :], 0.0, ALU.mult, ALU.add)
            op.then_inc(sem("r_cum"), 1)
            bg("kk")
            dve.wait_ge(sem("r_exp"), n)
            v_.tensor_tensor(cum[:, :, :], cum[:, :, :], sg[:, :, :], ALU.subtract).then_inc(sem("r_cumx"), 1)
            dve.wait_ge(sem("r_cumx"), n)
            for dt in range(4):
                op = v_.tensor_scalar(sg[:, dt, :], a_[:, dt, :], 1.0, col("k_a", dt), ALU.subtract, ALU.mult)
            link(dve, op)
            link(dve, v_.scalar_tensor_tensor(k_[:, :, :], sg[:, :, :], 1.0, k_[:, :, :], ALU.add, ALU.mult))
            for dt in range(4):
                op = v_.scalar_tensor_tensor(nat_t[:, dt, :], r_[:, dt, :], col("r_k", dt), k_[:, dt, :], ALU.mult, ALU.mult)
            op.then_inc(sem("r_rkk"), 1)
            bg("tilde")
            v_.tensor_copy(pc, ecum[:, :, :].rearrange("p d (c t) -> p d c t", t=C)[:, :, :, C - 1])
            v_.tensor_tensor(kt[:, :, :], k_[:, :, :], encum[:, :, :], ALU.mult)
            for e in range(2):
                half = slice(e * C, (e + 1) * C)
                v_.tensor_tensor(rz[half, :, e, :], r_[half, :, :], ecum[half, :, :], ALU.mult)
            dve.wait_ge(sem("r_kkroot"), n)
            link(dve, v_.reciprocal(gs_t[:, :, :], gs_t[:, :, :]))
            link(dve, v_.tensor_tensor(xf[:, :, :], xf[:, :, :], gs_t[:, :, :], ALU.mult))
            link(dve, v_.tensor_tensor(gs_t[:, :, :], xf[:, :, :], a_[:, :, :], ALU.mult))
            v_.tensor_tensor(bt[:, :, :], gs_t[:, :, :], encum[:, :, :], ALU.mult)
            dve.wait_ge(sem("r_expx"), n)
            for e in range(2):
                half = slice(e * C, (e + 1) * C)
                op = v_.scalar_tensor_tensor(az[half, :, e, :], xf[half, :, :], -1.0, cum[half, :, :], ALU.mult, ALU.mult)
            op.then_inc(sem("r_tilde"), 1)
            dve.wait_ge(sem("r_bonus"), n)
            v_.tensor_tensor(bonus[:, :, :], pa[:, :, :], v__[:, :, :], ALU.mult).then_inc(sem("r_bonus_out"), 1)
            bg("bonus")
            dve.wait_ge(sem("r_tilde"), n)
            for k, (dst, lo, hi) in enumerate(((bn, 2, 4), (kn_r, 0, 2), (vn_r, 2, 4))):
                dve.wait_ge(sem("r_nat_turned"), 3 * hf + k + 1)
                src = (pa, pb)[lo // 2][:, :, :].rearrange("p a t -> p (a t)")
                v_.tensor_copy(dst[:, :, :].rearrange("p t d -> p (t d)"), src).then_inc(sem("r_nat"), 1)
            bg("nat")
            for tt in range(TT):
                v = HALVES + TT * hf + tt
                dve.wait_ge(sem("r_mats"), TT * hf + tt + 1)
                for dst, k, mask in ((inv_r[5][:, :, :], 0, m_upo), (rb[:, tt, :, :], 1, m_inc), (ak[:, tt, :, :], 2, m_up),
                                     (rk[:, tt, :, :], 3, m_inc)):
                    v_.tensor_tensor(dst, units[k], over_units(mask), ALU.mult)
                v_.tensor_tensor(inv_r[0][:, :, :], units[0], over_units(m_upd), ALU.mult).then_inc(sem("inv_in"), 1)
                bg(f"mats{tt}")
                dve.wait_ge(sem("inv_in"), v + 1)
                invert_dve(dve, v, inv_r, ut_r[:, tt, :, :])
            v_.memset(s_r[:, 0, :, :], 0.0).then_inc(sem("r_state"), 1)
            dve.wait_ge(sem("r_state"), (NCH + 1) * hf + 1)
            for c in range(NCH):
                m = NCH * hf + c
                bg(f"sa{c}")
                dve.wait_ge(sem("r_ds"), m + 1)
                if m > 0 and c > 0:
                    dve.wait_ge(sem("r_ymm"), m)
                s_in, s_out = s_r[:, c % 2, :, :], s_r[:, (c + 1) % 2, :, :]
                link(dve, v_.tensor_tensor(s_out, s_in, heads_state, ALU.add))
                v_.tensor_tensor(s_out, s_out, pc[:, :, c:c + 1].to_broadcast([P, 4, C]), ALU.mult).then_inc(sem("r_state"), 1)
                bg(f"y{c}")
                dve.wait_ge(sem("r_state"), m + hf + 2)
            if hf > 0:
                bg_dve(dve, "rest")
            else:
                bg("out")
            dve.wait_ge(sem("r_y"), NCH * n)
            yv = y_r[:, :, :].rearrange("p t (h c) -> p (t h) c", c=RH)
            link(dve, v_.tensor_reduce(msum2[:, :], yv, AX_X, ALU.add))
            link(dve, v_.tensor_scalar(mroot2[:, :], msum2[:, :], 1.0 / RH, None, ALU.mult))
            v_.tensor_tensor(yv, yv, mroot2[:, :].unsqueeze(2).to_broadcast([P, 16, RH]), ALU.subtract).then_inc(sem("r_cent"), 1)
            dve.wait_ge(sem("r_centsq"), n)
            v_.tensor_reduce(msum[:, :], gs[:, :, :].rearrange("p t (h c) -> p (t h) c", c=RH), AX_X, ALU.add).then_inc(sem("r_var"), 1)
            dve.wait_ge(sem("r_std"), n)
            link(dve, v_.reciprocal(msum2[:, :], mroot[:, :]))
            v_.tensor_tensor(nat[:, :, :].rearrange("p t (h c) -> p (t h) c", c=RH), yv,
                             msum2[:, :].unsqueeze(2).to_broadcast([P, 16, RH]), ALU.mult).then_inc(sem("r_out"), 1)
            dve.wait_ge(sem("r_out_turned"), n)
            for dt in range(4):
                op = v_.tensor_scalar(xf[:, dt, :], pa[:, dt, :], col("ln_w", dt), col("ln_b", dt), ALU.mult, ALU.add)
            link(dve, op)
            link(dve, v_.tensor_tensor(xf[:, :, :], xf[:, :, :], bonus[:, :, :], ALU.add))
            v_.tensor_tensor(xf[:, :, :], xf[:, :, :], gt[:, :, :], ALU.mult).then_inc(sem("y_ready"), 1)
            dve.wait_ge(sem("y_ready"), HALVES + n)

        gs_t = gs[:, :, :].rearrange("p a (b t) -> p (a b) t", t=T)
        nat_t = nat[:, :, :].rearrange("p a (b t) -> p (a b) t", t=T)
        heads_state = bank[3].rearrange("p a (u c) -> p (a u) c", c=C)[:, 0:4, :]

        def lift_pe(pe):
            L = prods["lift"]
            t0, s0 = turns["merged"]
            pe.wait_ge(sem("y_split"), 1)
            for c in range(NDC):
                multiply(pe, L[2 * c], L[2 * c]["free"], (yhi, ylo))
                if c > 0:
                    turn(pe, t0 + c - 1)
                multiply(pe, L[2 * c + 1], L[2 * c + 1]["free"], (yhi, ylo), k0=8)
            turn(pe, t0 + NDC - 1)
            pe.wait_ge(x_ready, s0 + NDC)

        def gates_act(act, c):
            act.wait_ge(sem("ga_loaded"), 16 * (c + 1))
            nc.scalar.activation(ga[:, :, :], ga[:, :, :], ACT.Sigmoid)
            act.wait_ge(sem("gb_loaded"), 16 * (c + 1))
            nc.scalar.activation(gb[:, :, :], gb[:, :, :], ACT.Sigmoid).then_inc(sem("gates_ready"), 1)

        def lift_act(act):
            L = prods["lift"]
            t0, s0 = turns["merged"]
            act.wait_ge(sem("y_loaded"), 16)
            copy(act, yhi[:, :, :], yf[:, :, :]).then_inc(sem("y_hi"), 1)
            for c in range(NDC):
                la, lb = L[2 * c:2 * c + 2]
                for j in range(RING if c == 0 else 0, la["ns"]):
                    split_hi(act, la["slot"], j)
                if c == 0:
                    gates_act(act, 0)
                for j in range(lb["ns"]):
                    split_hi(act, lb["slot"], j)
                if c > 0:
                    x_hi(act, t0 + c - 1, mhi[:, 4 * c - 4:4 * c, :])
                    gates_act(act, c)
            for j in range(RING):
                split_hi(act, prods["out"][0]["slot"], j)
            x_hi(act, t0 + NDC - 1, mhi[:, 12:16, :])

        def lift_dve(dve):
            L = prods["lift"]
            t0, s0 = turns["merged"]
            v_ = nc.vector

            def branch(c, m, gate):
                pr = L[2 * c + m]
                dve.wait_ge(slot_used, pr["done"])
                dve.wait_ge(sem("gates_ready"), c + 1)
                v_.tensor_tensor(gate[:, :, :], gate[:, :, :], pair(pr["par"]), ALU.mult).then_inc(sem(pr["released"][0]), 1)
                dve.wait_ge(sem(pr["released"][0]), pr["released"][1])

            def merge(c):
                if c > 0:
                    dve.wait_ge(turned, t0 + c)
                else:
                    dve.wait_ge(sem("r_out_turned"), HALVES)
                v_.tensor_tensor(nat[:, :, :], ga[:, :, :], gb[:, :, :], ALU.add).then_inc(nat_ready, 1)

            dve.wait_ge(sem("y_hi"), 1)
            v_.tensor_tensor(ylo[:, :, :], yf[:, :, :], yhi[:, :, :].bitcast(F32), ALU.subtract).then_inc(sem("y_split"), 1)
            for c in range(NDC):
                la, lb = L[2 * c:2 * c + 2]
                for j in range(RING if c == 0 else 0, la["ns"]):
                    split_lo(dve, la["slot"], j)
                if c > 0:
                    branch(c - 1, 1, gb)
                    merge(c - 1)
                for j in range(lb["ns"]):
                    split_lo(dve, lb["slot"], j)
                if c > 0:
                    take(dve, t0 + c - 1, s0 + c - 1)
                branch(c, 0, ga)
                if c > 0:
                    x_lo(dve, s0 + c - 1, mhi[:, 4 * c - 4:4 * c, :], mlo[:, 4 * c - 4:4 * c, :])
            for j in range(RING):
                split_lo(dve, prods["out"][0]["slot"], j)
            branch(NDC - 1, 1, gb)
            merge(NDC - 1)
            take(dve, t0 + NDC - 1, s0 + NDC - 1)
            x_lo(dve, s0 + NDC - 1, mhi[:, 12:16, :], mlo[:, 12:16, :])

        def attn_pe(pe):
            O, KV, Q, MO = prods["out"], prods["mkv"], prods["mq"], prods["mo"]
            tm, tk, tq, th = (turns[k][0] for k in ("memnorm", "mk", "qnorm", "mq"))
            for c in range(NDC):
                multiply(pe, O[c], O[c]["free"], (mhi, mlo))
                turn(pe, tm + c)
            pe.wait_ge(x_ready, turns["memnorm"][1] + NDC)
            for c in range(2 * NDC):
                multiply(pe, KV[c], KV[c]["free"], (xhi, xlo))
                if 1 <= c <= NDC:
                    turn(pe, tk + c - 1)
                if c > NDC:
                    turn(pe, tq + c - NDC - 1)
            turn(pe, tq + NDC - 1)
            pe.wait_ge(x_ready, turns["qnorm"][1] + NDC)
            for c in range(NDC):
                multiply(pe, Q[c], Q[c]["free"], (mhi, mlo))
                if c > 0:
                    turn(pe, th + c - 1)
            turn(pe, th + NDC - 1)
            pe.wait_ge(xf_ready, th + NDC)
            pe.wait_ge(sem(Q[NDC - 1]["released"][0]), Q[NDC - 1]["released"][1])
            for g in range(MH + 1):
                if g < MH:
                    if g >= 2:
                        pe.wait_ge(sem("p_exp"), g - 1)
                    sc = bank[2 + g % 2]
                    for tt in range(TT):
                        for kk in range(MHK):
                            mm = nc.tensor.matmul(sc[:, tt, :], qt[:, MHK * g + kk, tt * P:(tt + 1) * P], kt_m[:, MHK * g + kk, :],
                                                  start=(kk == 0), stop=(kk == MHK - 1))
                    mm.then_inc(sem("p_scores"), 1)
                if g > 0:
                    e = g - 1
                    pe.wait_ge(sem("p_norm"), e + 1)
                    for mt in range(TT):
                        for tt in range(TT):
                            mm = nc.tensor.transpose(bank[e % 2][:, mt, tt * P:(tt + 1) * P], pr_m[:, e % 2, tt, mt * P:(mt + 1) * P],
                                                     ident[:, :])
                    mm.then_inc(sem("p_turned"), 1)
                    pe.wait_ge(sem("p_t"), e + 1)
                    if e >= 2:
                        pe.wait_ge(sem("o_take"), e - 1)
                    out = pair(e % 2).rearrange("p a (b t) -> p (a b) t", t=T)
                    for kk in range(MHK):
                        for mt in range(TT):
                            mm = nc.tensor.matmul(out[:, kk, :], v_m[:, mt, e * MHD + kk * P:e * MHD + (kk + 1) * P],
                                                  pt_m[:, e % 2, mt, :], start=(mt == 0), stop=(mt == TT - 1))
                    mm.then_inc(sem("o_mm"), 1)
            pe.wait_ge(sem("o_ready"), MH)
            for c in range(NDC):
                multiply(pe, MO[c], MO[c]["free"], (xhi, xlo))

        def attn_act(act):
            O, KV, Q, MO = prods["out"], prods["mkv"], prods["mq"], prods["mo"]
            tm, tk, tq, th = (turns[k][0] for k in ("memnorm", "mk", "qnorm", "mq"))
            act.wait_ge(sem("mem_loaded"), 16 * TT)
            for c in range(NDC):
                sumsq(act, msb, 2, c)
            norm_root(act, 2)
            for c in range(NDC):
                for j in range(RING if c == 0 else 0, KT // SK):
                    split_hi(act, O[c]["slot"], j)
                    if c > 0 and j == 5:
                        act.wait_ge(sem(O[c - 1]["released"][0]), O[c - 1]["released"][1])
                        sumsq(act, h, 3, c - 1)
                        x_hi(act, tm + c - 1, xhi[:, 4 * c - 4:4 * c, :])
            for j in range(RING):
                split_hi(act, KV[0]["slot"], j)
            act.wait_ge(sem(O[3]["released"][0]), O[3]["released"][1])
            sumsq(act, h, 3, 3)
            x_hi(act, tm + 3, xhi[:, 12:16, :])
            for c in range(2 * NDC):
                for j in range(RING if c == 0 else 0, KT // SK):
                    split_hi(act, KV[c]["slot"], j)
                    if c == NDC and j == 5:
                        norm_root(act, 3)
                if c > NDC + 1:
                    x_hi(act, tq + c - NDC - 2, mhi[:, 4 * (c - NDC - 2):4 * (c - NDC - 1), :])
            for j in range(RING):
                split_hi(act, Q[0]["slot"], j)
            for k in (2, 3):
                x_hi(act, tq + k, mhi[:, 4 * k:4 * k + 4, :])
            for c in range(NDC):
                for j in range(RING if c == 0 else 0, KT // SK):
                    split_hi(act, Q[c]["slot"], j)
            for j in range(RING):
                split_hi(act, MO[0]["slot"], j)
            for g in range(MH + 1):
                if g < MH:
                    act.wait_ge(sem("p_max"), g + 1)
                    for tt in range(TT):
                        op = nc.scalar.activation(pr_m[:, g % 2, tt, :], bank[2 + g % 2][:, tt, :], ACT.Exp, bias=nmx[:, g, tt:tt + 1],
                                                  scale=MHD ** -0.5, accum_out=den[:, g, tt:tt + 1])
                    op.then_inc(sem("p_exp"), 1)
                if g > 0:
                    act.wait_ge(sem("o_take"), g)
                    e = g - 1
                    copy(act, xhi[:, MHK * e:MHK * (e + 1), :], xf[:, :, :]).then_inc(sem("o_hi"), 1)
            for c in range(NDC):
                for j in range(RING if c == 0 else 0, KT // SK):
                    split_hi(act, MO[c]["slot"], j)
                    if c > 0 and j == 5:
                        act.wait_ge(sem(MO[c - 1]["released"][0]), MO[c - 1]["released"][1])
                        sumsq(act, h, 4, c - 1)

        def attn_dve(dve):
            O, KV, Q, MO = prods["out"], prods["mkv"], prods["mq"], prods["mo"]
            (tm, sm), (tk, _), (tq, sq), (th, _) = (turns[k] for k in ("memnorm", "mk", "qnorm", "mq"))
            v_ = nc.vector
            norm_scale(dve, 2)
            norm_chunk(dve, msb, 0, tm)
            for c in range(NDC):
                for j in range(RING if c == 0 else 0, KT // SK):
                    split_lo(dve, O[c]["slot"], j)
                    if c > 0 and j == 4:
                        residual(dve, O[c - 1], c - 1, 1.0)
                        take(dve, tm + c - 1, sm + c - 1, PRM["mem_kv_norm"] + 4 * (c - 1))
                        norm_chunk(dve, msb, c, tm + c)
                    if c > 0 and j == 7:
                        x_lo(dve, sm + c - 1, xhi[:, 4 * c - 4:4 * c, :], xlo[:, 4 * c - 4:4 * c, :])
            for j in range(RING):
                split_lo(dve, KV[0]["slot"], j)
            residual(dve, O[3], 3, 1.0)
            take(dve, tm + 3, sm + 3, PRM["mem_kv_norm"] + 12)
            x_lo(dve, sm + 3, xhi[:, 12:16, :], xlo[:, 12:16, :])

            def k_nat(c):
                dve.wait_ge(slot_used, KV[c]["done"])
                dve.wait_ge(turned, tk + c)
                v_.tensor_copy(nat[:, :, :], pair(KV[c]["par"])).then_inc(nat_ready, 1)
                dve.wait_ge(nat_ready, tk + c + 1)
                dve.sem_inc(sem(KV[c]["released"][0]), 1)

            def plain(dst, t):
                dve.wait_ge(turned, t + 1)
                v_.tensor_copy(dst, pa[:, :, :]).then_inc(xf_ready, 1)

            def v_nat(c):
                dve.wait_ge(slot_used, KV[NDC + c]["done"])
                v_.tensor_copy(v_m[:, :, c * CW:(c + 1) * CW], pair(KV[NDC + c]["par"])).then_inc(sem(KV[NDC + c]["released"][0]), 1)

            for c in range(2 * NDC):
                for j in range(RING if c == 0 else 0, KT // SK):
                    split_lo(dve, KV[c]["slot"], j)
                    if j == 4 and 1 <= c <= NDC:
                        k_nat(c - 1)
                    if j == 4 and c > NDC:
                        v_nat(c - 1 - NDC)
                    if j == 1 and 2 <= c <= NDC + 1:
                        plain(kt_m[:, MHK * (c - 2):MHK * (c - 1), :], tk + c - 2)
                    if j == 5 and c == NDC:
                        norm_scale(dve, 3)
                    if j == 5 and c > NDC:
                        norm_chunk(dve, h, c - NDC - 1, tq + c - NDC - 1)
                    if j == 1 and c > NDC + 1:
                        take(dve, tq + c - NDC - 2, sq + c - NDC - 2, PRM["mem_q_norm"] + 4 * (c - NDC - 2))
                if c > NDC + 1:
                    e = c - NDC - 2
                    x_lo(dve, sq + e, mhi[:, 4 * e:4 * e + 4, :], mlo[:, 4 * e:4 * e + 4, :])
            for j in range(RING):
                split_lo(dve, Q[0]["slot"], j)
            v_nat(NDC - 1)
            take(dve, tq + 2, sq + 2, PRM["mem_q_norm"] + 8)
            norm_chunk(dve, h, 3, tq + 3)
            x_lo(dve, sq + 2, mhi[:, 8:12, :], mlo[:, 8:12, :])
            take(dve, tq + 3, sq + 3, PRM["mem_q_norm"] + 12)
            x_lo(dve, sq + 3, mhi[:, 12:16, :], mlo[:, 12:16, :])

            def q_nat(c):
                dve.wait_ge(slot_used, Q[c]["done"])
                dve.wait_ge(turned, th + c)
                v_.tensor_copy(nat[:, :, :], pair(Q[c]["par"])).then_inc(nat_ready, 1)
                dve.wait_ge(nat_ready, th + c + 1)
                dve.sem_inc(sem(Q[c]["released"][0]), 1)

            for c in range(NDC):
                for j in range(RING if c == 0 else 0, KT // SK):
                    split_lo(dve, Q[c]["slot"], j)
                    if j == 4 and c > 0:
                        q_nat(c - 1)
                    if j == 1 and c > 1:
                        plain(qt[:, MHK * (c - 2):MHK * (c - 1), :], th + c - 2)
            for j in range(RING):
                split_lo(dve, MO[0]["slot"], j)
            plain(qt[:, 8:12, :], th + 2)
            q_nat(3)
            plain(qt[:, 12:16, :], th + 3)
            for g in range(MH + 1):
                if g < MH:
                    dve.wait_ge(sem("p_scores"), g + 1)
                    link(dve, v_.tensor_reduce(mx[:, g, :], bank[2 + g % 2], AX_X, ALU.max))
                    v_.tensor_scalar(nmx[:, g, :], mx[:, g, :], -MHD ** -0.5, None, ALU.mult).then_inc(sem("p_max"), 1)
                    dve.wait_ge(sem("p_exp"), g + 1)
                    link(dve, v_.reciprocal(rden[:, g, :], den[:, g, :]))
                    for tt in range(TT):
                        op = v_.tensor_scalar(pr_m[:, g % 2, tt, :], pr_m[:, g % 2, tt, :], rden[:, g, tt:tt + 1], None, ALU.mult)
                    op.then_inc(sem("p_norm"), 1)
                    dve.wait_ge(sem("p_turned"), g + 1)
                    v_.tensor_copy(pt_m[:, g % 2, :, :], bank[g % 2]).then_inc(sem("p_t"), 1)
                if g > 0:
                    e = g - 1
                    dve.wait_ge(sem("o_mm"), e + 1)
                    if e > 0:
                        dve.wait_ge(sem("o_hi"), e)
                        dve.wait_ge(sem("o_ready"), e)
                    v_.tensor_copy(xf[:, :, :], pair(e % 2).rearrange("p a (b t) -> p (a b) t", t=T)).then_inc(sem("o_take"), 1)
                    dve.wait_ge(sem("o_hi"), e + 1)
                    v_.tensor_tensor(xlo[:, MHK * e:MHK * (e + 1), :], xf[:, :, :], xhi[:, MHK * e:MHK * (e + 1), :].bitcast(F32),
                                     ALU.subtract).then_inc(sem("o_ready"), 1)
            for c in range(NDC):
                for j in range(RING if c == 0 else 0, KT // SK):
                    split_lo(dve, MO[c]["slot"], j)
                    if c > 0 and j == 4:
                        residual(dve, MO[c - 1], c - 1, 1.0)

        fgain = at("fgain", 64, [D])

        def next_hi(act, phase):
            for j in range(RING):
                split_hi(act, prods[phase][0]["slot"], j)

        def next_lo(dve, phase):
            for j in range(RING):
                split_lo(dve, prods[phase][0]["slot"], j)

        def store_y(sp, tile, n):
            sp.wait_ge(sem("y_ready"), n)
            sp.dma_start(y_turned[tile:tile + 4].rearrange("k p t -> p k t"), xf[:, :, :]).then_inc(sem("y_stored"), 16)

        def last_sumsq(act, pr, q):
            act.wait_ge(sem(pr["released"][0]), pr["released"][1])
            sumsq(act, h, q, NDC - 1)

        block = ctx.enter_context(nc.Block())

        @block.gpsimd
        def _(pool):
            g = nc.gpsimd
            g.memset(nat[:, :, :], 0.0).then_inc(prm_clear, 1)
            pool.wait_ge(prm_clear, 1)
            link(pool, g.memset(epsn[:, :], RMS_EPS))
            link(pool, g.memset(ident[:, :], 0.0))
            link(pool, g.affine_select(out=ident[:, :], in_=ident[:, :], compare_op=ALU.not_equal, fill=1.0, base=0,
                                       pattern=[[-1, P]], channel_multiplier=1))
            link(pool, g.memset(ones[:, :], 1.0))
            link(pool, g.memset(headones[:, :], 0.0))
            link(pool, g.memset(eye[:, :], 0.0))
            for c in range(2):
                rows = slice(c * C, (c + 1) * C)
                link(pool, g.memset(headones[rows, rows], 1.0))
                link(pool, g.affine_select(out=eye[rows, :], in_=eye[rows, :], compare_op=ALU.not_equal, fill=1.0, base=0,
                                           pattern=[[-1, C]], channel_multiplier=1))
                for mask, op, pattern in ((m_inc, ALU.is_ge, [[1, C]]), (m_up, ALU.is_gt, [[1, C]]),
                                          (m_upo, ALU.is_gt, [[16, C // 16], [0, 16]])):
                    link(pool, g.affine_select(out=mask[rows, :], in_=ones[rows, 0:C], compare_op=op, fill=0.0, base=0,
                                               pattern=pattern, channel_multiplier=-1))
            link(pool, g.tensor_tensor(m_upd[:, :], m_up[:, :], m_upo[:, :], ALU.subtract))
            link(pool, g.memset(scanmask[:, :], 1.0))
            link(pool, g.memset(scanmask[:, :].rearrange("p (c t) -> p c t", t=C)[:, :, 0:1], 0.0))
            link(pool, g.memset(sel[0:GHV, :, :], 1.0))
            g.affine_select(out=sel[0:GHV, :, :], in_=sel[0:GHV, :, :], compare_op=ALU.is_equal, fill=0.0, base=0,
                            pattern=[[-1, GHV], [0, P]], channel_multiplier=1).then_inc(consts_ready, 1)

            def fetch(q, dst, loaded, *free):
                pool.wait_ge(sem("spooled"), 16 * (q + 1))
                for name, value in free:
                    pool.wait_ge(sem(name), value)
                g.dma_start(dst[:, :, :], proj[q].rearrange("(t p) c -> p t c", p=P)).then_inc(sem(loaded), 16)

            fetch(0, gs, "gs_loaded")
            fetch(2, zg, "z_loaded", ("g_out", 1))
            fetch(1, nat, "nat_loaded", ("g_out_turned", 1))
            store_y(pool, 8, 1)
            fetch(3, gs, "gs_loaded", ("mix_turned", 3))
            for hf in range(HALVES):
                cols = slice(hf * CW, (hf + 1) * CW)
                pool.wait_ge(sem("lora_clear"), hf + 1)
                g.dma_start(w2z[0:LORA_D, :], A["rw_w2"][0][:, cols]).then_inc(sem("lora_loaded"), 16)
                g.dma_start(a2z[LORA_D:P, :], A["rw_a2"][0][:, cols]).then_inc(sem("lora_loaded"), 16)
                g.dma_start(g2a[:, :], A["rw_g2"][0][0:P, cols]).then_inc(sem("lora_loaded"), 16)
                g.dma_start(g2b[0:32, :], A["rw_g2"][0][P:LORA_G, cols]).then_inc(sem("lora_loaded"), 16)
                fetch(4 + 3 * hf, nat, "nat_loaded", ("g_out_turned", HALVES) if hf == 0 else ("r_out_turned", 1))
                store_y(pool, 12 if hf == 0 else 0, HALVES + hf)
                fetch(5 + 3 * hf, gs, "gs_loaded", ("mix_turned", 5 + 3 * hf))
                if hf == 0:
                    fetch(6, gs, "gs_loaded", ("r_var", 1))
            for c in range(NDC):
                free = () if c == 0 else (("nat_ready", turns["merged"][0] + c),)
                if c == 0:
                    free = (("r_std", 2),)
                fetch(9 + c, ga, "ga_loaded", *free)
                fetch(9 + NDC + c, gb, "gb_loaded", *free)
                if c == 0:
                    store_y(pool, 4, HALVES + 2)
                    pool.wait_ge(sem("y_stored"), 16 * 2 * HALVES)
                    g.dma_start(yf[:, :, :], y_turned.rearrange("k p t -> p k t")).then_inc(sem("y_loaded"), 16)
            pool.wait_ge(slot_used, prods["f2dn"][0]["slot"])
            g.dma_start(fgain[:, :], A["final_norm"].rearrange("(m d) -> m d", m=1).to_broadcast([P, D])).then_inc(sem("fgain_loaded"), 16)


        @block.sync
        def _(sp):
            for tt in range(TT):
                sp.dma_start(h[:, tt, :], A["x"][0, tt * P:(tt + 1) * P, :]).then_inc(x_loaded, 16)
            sp.wait_ge(prm_clear, 1)
            for name, src, m in prm_sources(A):
                r = PRM[name]
                sp.dma_start(nat[r % P:r % P + m, r // P, 0:src.shape[-1]], src).then_inc(prm_loaded, 16)
            for cell, name in ((dtb, "gdn_dt_bias"), (nal, "gdn_a_log")):
                sp.dma_start(cell, A[name][0].rearrange("(g m) -> g m", m=1)).then_inc(sem("gdn_loaded"), 16)
            ffn_load(sp, "f1", A["ffn1_w_gate"][0], A["ffn1_w_up"][0], A["ffn1_w_down"][0])

            def weights(w, cols, pr, rows0=0):
                for j in range(pr["ns"]):
                    rows = slice(rows0 + j * SK * P, rows0 + (j + 1) * SK * P)
                    load_slot(sp, w[rows, cols].rearrange("(k p) n -> p k n", p=P), pr["slot"], j)

            w_in = A["w_in"][0]
            for j in range(KT // SK):
                rows = slice(j * SK * P, (j + 1) * SK * P)
                s, n, _ = slot_of(AUX["slot"], j)
                sp.wait_ge(wlo_ready, n - RING + 1)
                for at_, c0, c1 in ((0, 3 * RW, RW_COLS), (LORA, BA0, GATE0)):
                    sp.dma_start(raw[:, s, :, at_:at_ + c1 - c0], w_in[rows, c0:c1].rearrange("(k p) n -> p k n", p=P)).then_inc(LOADED[s], 16)
            for hf in range(HALVES):
                g = prods[f"gdn{hf}"]
                for j in range(KT // SK):
                    rows = slice(j * SK * P, (j + 1) * SK * P)
                    s, n, _ = slot_of(g[0]["slot"], j)
                    sp.wait_ge(wlo_ready, n - RING + 1)
                    for at_, c0 in ((0, GDN0 + hf * 256), (256, GDN0 + GQ + hf * 256)):
                        sp.dma_start(raw[:, s, :, at_:at_ + 256], w_in[rows, c0:c0 + 256].rearrange("(k p) n -> p k n", p=P)).then_inc(LOADED[s], 16)
                for m, c0 in ((1, GDN0 + 2 * GQ), (2, Z0)):
                    weights(w_in, slice(c0 + hf * CW, c0 + (hf + 1) * CW), g[m])
            for hf in range(HALVES):
                for m in range(3):
                    weights(w_in, slice(m * RW + hf * CW, m * RW + (hf + 1) * CW), prods[f"rw{hf}"][m])
            for c in range(2 * NDC):
                weights(w_in, slice(GATE0 + c * CW, GATE0 + (c + 1) * CW), prods["gates"][c])
            for c in range(NDC):
                for m in range(2):
                    weights(A["w_lift"][0, m], slice(c * CW, (c + 1) * CW), prods["lift"][2 * c + m])
            sp.wait_ge(slot_used, prods["lift"][-1]["done"])
            for tt in range(TT):
                sp.dma_start(msb[:, tt, :], A["mem"][0, tt * P:(tt + 1) * P, :]).then_inc(sem("mem_loaded"), 16)
            for phase, ws in (("out", ("w_out",)), ("mkv", ("w_mk", "w_mv")), ("mq", ("w_mq",)), ("mo", ("w_mo",))):
                for m, w in enumerate(ws):
                    for c in range(NDC):
                        weights(A[w][0], slice(c * CW, (c + 1) * CW), prods[phase][NDC * m + c])
            ffn_load(sp, "f2", A["ffn2_w_gate"][0], A["ffn2_w_up"][0], A["ffn2_w_down"][0])
            for c in range(NDC):
                sp.wait_ge(sem("out_ready"), c + 1)
                sp.dma_start(A["out"][0].rearrange("(t p) d -> p t d", p=P)[:, :, c * CW:(c + 1) * CW],
                             h[:, :, c * CW:(c + 1) * CW]).then_inc(stored, 16)
            sp.wait_ge(stored, 16 * NDC)

        @block.scalar
        def _(act):
            next_hi(act, "f1gu")
            act.wait_ge(x_loaded, 16 * TT)
            for c in range(NDC):
                sumsq(act, h, 0, c)
            act.wait_ge(consts_ready, 1)
            norm_act(act, 0, "f1norm")
            ffn_act(act, "f1")
            for j in range(RING):
                split_hi(act, AUX["slot"], j, width=AUXW)
            last_sumsq(act, prods["f1dn"][3], 1)
            norm_act(act, 1, "mixnorm")
            for j in range(RING, KT // SK):
                split_hi(act, AUX["slot"], j, width=AUXW)
            next_hi(act, "gdn0")
            aux_act(act)
            for hf in range(HALVES):
                gdn_act(act, hf)
            for hf in range(HALVES):
                rw_act(act, hf)
            next_hi(act, "lift")
            lift_act(act)
            attn_act(act)
            next_hi(act, "f2gu")
            last_sumsq(act, prods["mo"][3], 4)
            norm_act(act, 4, "f2norm")
            ffn_act(act, "f2")
            last_sumsq(act, prods["f2dn"][3], 5)
            norm_root(act, 5)

        @block.vector
        def _(dve):
            dve.wait_ge(prm_turned, 1)
            nc.vector.tensor_copy(prm[:, 0:NPRM], pb[:, :, :].rearrange("p a b -> p (a b)")[:, 0:NPRM]).then_inc(prm_ready, 1)
            dve.wait_ge(prm_ready, 1)
            next_lo(dve, "f1gu")
            norm_dve(dve, 0, h, "f1norm", "ffn1_norm")
            ffn_dve(dve, "f1")
            for j in range(RING):
                split_lo(dve, AUX["slot"], j, width=AUXW)
            residual(dve, prods["f1dn"][3], 3, 0.5)
            norm_dve(dve, 1, h, "mixnorm", "mix_norm")
            for j in range(RING, KT // SK):
                split_lo(dve, AUX["slot"], j, width=AUXW)
            next_lo(dve, "gdn0")
            aux_dve(dve)
            for hf in range(HALVES):
                gdn_dve(dve, hf)
            for hf in range(HALVES):
                rw_dve(dve, hf)
            next_lo(dve, "lift")
            lift_dve(dve)
            attn_dve(dve)
            next_lo(dve, "f2gu")
            residual(dve, prods["mo"][3], 3, 1.0)
            norm_dve(dve, 4, h, "f2norm", "ffn2_norm")
            ffn_dve(dve, "f2")
            residual(dve, prods["f2dn"][3], 3, 0.5)
            norm_scale(dve, 5)
            dve.wait_ge(sem("fgain_loaded"), 16)
            for c in range(NDC):
                cols = slice(c * CW, (c + 1) * CW)
                for tt in range(TT):
                    op = nc.vector.scalar_tensor_tensor(h[:, tt, cols], h[:, tt, cols], rstd[:, tt:tt + 1], fgain[:, cols], ALU.mult, ALU.mult)
                op.then_inc(sem("out_ready"), 1)

        @block.tensor
        def _(pe):
            pe.wait_ge(consts_ready, 1)
            pe.wait_ge(prm_loaded, 16 * len(PRM))
            for g in range(2):
                mm = nc.tensor.transpose(pb[:, g // 2, g * P:(g + 1) * P], nat[:, g, 0:P], ident[:, :])
            mm.then_inc(prm_turned, 1)
            norm_pe(pe, "f1norm")
            ffn_pe(pe, "f1")
            norm_pe(pe, "mixnorm")
            pe.wait_ge(x_ready, turns["mixnorm"][1] + NDC)
            aux_pe(pe)
            for hf in range(HALVES):
                gdn_pe(pe, hf)
            for hf in range(HALVES):
                rw_pe(pe, hf)
            lift_pe(pe)
            attn_pe(pe)
            norm_pe(pe, "f2norm")
            ffn_pe(pe, "f2")


def prm_sources(A):
    def rows(v):
        return v.rearrange("(m p) -> m p", p=P)

    mu = A["rw_shift_mu"][0]
    wide = 3 * RW
    out = [("ffn1_norm", rows(A["ffn1_norm"][0]), KT), ("mix_norm", rows(A["mix_norm"][0]), KT),
           ("mem_q_norm", rows(A["mem_q_norm"][0]), KT), ("mem_kv_norm", rows(A["mem_kv_norm"][0]), KT),
           ("ffn2_norm", rows(A["ffn2_norm"][0]), KT), ("mu_rkv", rows(mu[0:wide]), wide // P),
           ("mu_wa", rows(mu[wide:wide + P]), 1), ("mu_g0", rows(mu[wide + P:wide + 2 * P]), 1),
           ("mu_g1", mu[wide + 2 * P:RW_COLS].rearrange("(m p) -> m p", m=1), 1)]
    for name in ("w0", "a0", "k_k", "k_a", "ln_w", "ln_b"):
        out.append((name, rows(A["rw_" + name][0]), RW // P))
    out.append(("r_k", A["rw_r_k"][0].rearrange("(m a) n -> m (a n)", a=2), RW // P))
    out.append(("conv", A["gdn_conv_w"][0].rearrange("k (m p) -> (k m) p", p=P), CONV * 16))
    out.append(("gdn_norm", A["gdn_norm_w"][0].rearrange("(m p) -> m p", m=1), 1))
    return out


_INS = ['x', 'mem', 'ffn1_norm', 'ffn1_w_gate', 'ffn1_w_up', 'ffn1_w_down', 'mix_norm', 'w_in', 'rw_shift_mu', 'rw_w0',
        'rw_w2', 'rw_a0', 'rw_a2', 'rw_g2', 'rw_k_k', 'rw_k_a', 'rw_r_k', 'rw_ln_w', 'rw_ln_b', 'gdn_conv_w',
        'gdn_a_log', 'gdn_dt_bias', 'gdn_norm_w', 'w_lift', 'w_out', 'mem_q_norm', 'mem_kv_norm', 'w_mq', 'w_mk',
        'w_mv', 'w_mo', 'ffn2_norm', 'ffn2_w_gate', 'ffn2_w_up', 'ffn2_w_down', 'final_norm']


def kernel(**inputs):
    import numpy as np
    import concourse.bacc as bacc
    from concourse.bass_utils import run_bass_kernel_spmd

    nc = bacc.Bacc("TRN2", target_bir_lowering=False, num_devices=1)
    arrays, aps = {}, {}
    for name in _INS:
        a = np.ascontiguousarray(inputs[name])
        arrays[f"in_{name}"] = a
        aps[name] = nc.dram_tensor(f"in_{name}", a.shape, mybir.dt.from_np(a.dtype), kind="ExternalInput").ap()
    aps["out"] = nc.dram_tensor("out", (1, T, D), F32, kind="ExternalOutput").ap()
    build(nc, aps)
    r = run_bass_kernel_spmd(nc, [arrays], core_ids=[0])
    return np.asarray(r.results[0]["out"])
```

```python
from contextlib import ExitStack

import concourse.bass as bass
from concourse import mybir

F32 = mybir.dt.float32
F32R = mybir.dt.float32r
ALU = mybir.AluOpType
ACT = mybir.ActivationFunctionType
AX_X = mybir.AxisListType.X
ds = bass.ds

P = 128
T = 256
TT = T // P
D = 2048
KT = D // P
F = 5632
FT = F // P
CW = 512
SK = 2
RING = 4
NFC = F // CW
NDC = D // CW
RMS_EPS = 1e-6
C = 64
NCH = T // C

RW = 1024
RH = 64
RW_GN_EPS = 64e-5
LORA_D, LORA_A, LORA_G = 64, 64, 160
LORA = LORA_D + LORA_A + LORA_G
RW_COLS = 3 * RW + LORA
GH = 128
GHV = 8
GQ = 512
GV = 1024
CONV = 4
GDN0 = RW_COLS
Z0 = GDN0 + 2 * GQ + GV
BA0 = Z0 + GV
GATE0 = BA0 + 2 * GHV
AUXW = LORA + 2 * GHV
MH = 4
MHD = D // MH
MHK = MHD // P
HALVES = 2
EXP_HALF = 0.6065306597126334

PRM_LIST = [("ffn1_norm", KT), ("mix_norm", KT), ("mem_q_norm", KT), ("mem_kv_norm", KT), ("ffn2_norm", KT),
            ("mu_rkv", 3 * RW // P), ("mu_wa", 1), ("mu_g0", 1), ("mu_g1", 1), None,
            ("w0", RW // P), ("a0", RW // P), ("k_k", RW // P), ("k_a", RW // P), ("r_k", RW // P),
            ("ln_w", RW // P), ("ln_b", RW // P), ("conv", CONV * 16), ("gdn_norm", 1)]
PRM = {}
_at = 0
for _entry in PRM_LIST:
    if _entry is None:
        _at = P
    else:
        PRM[_entry[0]] = _at
        _at += _entry[1]
NPRM = _at


def background():
    marks = []

    def section(key, names):
        assert len(names) == len(TILES_BEHIND[key])
        marks.extend(zip(names, TILES_BEHIND[key]))

    def inversion(v):
        section(f"inv{v}", [f"inv{v}.{k + 1}" for k in range(10)])

    for hf in range(HALVES):
        section(f"gdn{hf}", [f"gdn{hf}.{name}" for name in ("conv", "norms", "rows", "naturals", "mats")])
        inversion(hf)
        section(f"gdn{hf}.chunks", [f"gdn{hf}.{name}{c}" for c in range(NCH) for name in ("ks", "vnew", "state")])
        section(f"gdn{hf}.out", [f"gdn{hf}.out", f"gdn{hf}.y"])
    for hf in range(HALVES):
        section(f"rw{hf}", [f"rw{hf}.{name}" for name in ("lora", "g", "r", "k", "v", "shift", "kk", "tilde", "bonus", "nat")])
        for tt in range(TT):
            section(f"rw{hf}.mats{tt}", [f"rw{hf}.mats{tt}"])
            inversion(HALVES + TT * hf + tt)
        section(f"rw{hf}.chunks", [f"rw{hf}.{name}{c}" for c in range(NCH) for name in ("r", "sa", "y")])
        section(f"rw{hf}.out", [f"rw{hf}.out", f"rw{hf}.y"])
    return marks


TILES_BEHIND = {
    "gdn0": [15, 4, 4, 3, 3],
    "inv0": [1, 1, 1, 1, 1, 1, 1, 1, 1, 1],
    "gdn0.chunks": [2, 1, 1, 2, 1, 1, 2, 1, 1, 2, 1, 1],
    "gdn0.out": [4, 2],
    "gdn1": [15, 4, 4, 3, 3],
    "inv1": [1, 1, 1, 1, 1, 1, 1, 0, 1, 1],
    "gdn1.chunks": [2, 1, 1, 2, 1, 1, 2, 1, 1, 3, 1, 1],
    "gdn1.out": [4, 2],
    "rw0": [2, 1, 2, 2, 4, 4, 6, 6, 6, 0],
    "rw0.mats0": [2],
    "inv2": [1, 1, 1, 1, 1, 1, 1, 1, 1, 1],
    "rw0.mats1": [2],
    "inv3": [1, 1, 1, 1, 1, 1, 1, 1, 1, 1],
    "rw0.chunks": [1, 1, 1, 1, 1, 1, 1, 1, 1, 1, 0, 1],
    "rw0.out": [5, 4],
    "rw1": [2, 1, 2, 2, 5, 4, 6, 6, 7, 1],
    "rw1.mats0": [2],
    "inv4": [1, 1, 1, 1, 1, 1, 1, 1, 1, 1],
    "rw1.mats1": [2],
    "inv5": [1, 1, 1, 1, 1, 1, 1, 1, 1, 1],
    "rw1.chunks": [1, 1, 1, 1, 1, 1, 1, 1, 1, 1, 1, 1],
    "rw1.out": [5, 5],
}


def plan():
    prods, turns = {}, {}
    state = dict(p=0, slot=0, t=0, s=0, freed=[0, 0])
    last = [None, None]

    def products(phase, n, nk, ups=None):
        out = []
        for c in range(n):
            k = nk[c % len(nk)]
            par = state["p"] % 2
            if ups is not None and c % 2 == 1:
                released = ("nat_ready", ups + c // 2 + 1)
            else:
                state["freed"][par] += 1
                released = (("pair_free0", "pair_free1")[par], state["freed"][par])
            out.append(dict(par=par, slot=state["slot"], ns=k // SK, free=last[par], released=released,
                            done=state["slot"] + k // SK))
            last[par] = released
            state["p"] += 1
            state["slot"] += k // SK
        prods[phase] = out

    def turned(phase, n, split=True):
        turns[phase] = (state["t"], state["s"])
        state["t"] += n
        if split:
            state["s"] += n

    def ffn(tag):
        turned(tag + "norm", NDC)
        turned(tag + "act", NFC)
        products(tag + "gu", 2 * NFC, [KT], ups=turns[tag + "act"][0])
        products(tag + "dn", NDC, [FT])

    ffn("f1")
    turned("mixnorm", NDC)
    products("aux", 1, [KT])
    for hf in range(HALVES):
        products(f"gdn{hf}", 3, [KT])
    for hf in range(HALVES):
        products(f"rw{hf}", 3, [KT])
    products("gates", 2 * NDC, [KT])
    products("lift", 2 * NDC, [8])
    turned("merged", NDC)
    products("out", NDC, [KT])
    turned("memnorm", NDC)
    products("mkv", 2 * NDC, [KT])
    turned("mk", NDC, False)
    turned("qnorm", NDC)
    products("mq", NDC, [KT])
    turned("mq", NDC, False)
    products("mo", NDC, [KT])
    ffn("f2")
    return prods, turns


def build(nc, A):
    prods, turns = plan()
    with ExitStack() as ctx:
        sems = {}

        def sem(name):
            if name not in sems:
                sems[name] = ctx.enter_context(nc.semaphore(name))
            return sems[name]

        base = -(-nc.sbuf_base // 64) * 64
        ctx.enter_context(nc.sbuf_tensor("slab", [P, 207 * 256], F32))

        def at(name, kib, shape, dt=F32):
            return nc.alloc_sbuf_tensor_at(name, [P] + shape, dt, offset=int(base + kib * 1024))

        h = at("h", 0, [TT, D])
        raw = at("raw", 16, [RING, SK, CW])
        whi = at("whi", 32, [RING, SK, CW], F32R)
        wlo = at("wlo", 48, [RING, SK, CW], F32R)
        xhi = at("xhi", 64, [KT, T], F32R)
        xlo = at("xlo", 80, [KT, T], F32R)
        ident = at("ident", 96, [P])
        ones = at("ones", 96.5, [P])
        headones = at("headones", 97, [P])
        m_up = at("m_up", 97.5, [C])
        m_upd = at("m_upd", 97.75, [C])
        m_upo = at("m_upo", 98, [C])
        m_inc = at("m_inc", 98.25, [C])
        eye = at("eye", 98.5, [C])
        prm = at("prm", 98.75, [NPRM])
        scanmask = at("scanmask", 99.75, [T])
        sel = at("sel", 100.75, [GHV, P])
        AR = 105
        hhi = at("hhi", AR, [FT, T], F32R)
        hlo = at("hlo", AR + 44, [FT, T], F32R)
        nat = at("nat", 193, [TT, CW])
        gs = at("gs", 197, [TT, CW])
        xf = at("xf", 201, [4, T])
        ss = at("ss", 205, [TT, NDC])
        ssum = at("ssum", 205.0625, [TT])
        rms = at("rms", 205.125, [TT])
        rstd = at("rstd", 205.1875, [TT])
        epsn = at("epsn", 205.25, [1])
        scal = at("scal", 205.5, [16 * 24])

        pp = ctx.enter_context(nc.psum_tensor("pp", [P, 4, CW], F32))
        pa = ctx.enter_context(nc.psum_tensor("pa", [P, 4, T], F32))
        pb = ctx.enter_context(nc.psum_tensor("pb", [P, 4, T], F32))

        def pair(par):
            return pp[:, 2 * par:2 * par + 2, :]

        LOADED = [sem(f"loaded{s}") for s in range(RING)]
        whi_ready, wlo_ready, slot_used = sem("whi_ready"), sem("wlo_ready"), sem("slot_used")
        nat_ready, turned, xf_ready = sem("nat_ready"), sem("turned"), sem("xf_ready")
        hi_ready, x_ready = sem("hi_ready"), sem("x_ready")
        sumsq_ready, ms_ready, rms_ready = sem("sumsq_ready"), sem("ms_ready"), sem("rms_ready")
        x_loaded, prm_clear, prm_loaded = sem("x_loaded"), sem("prm_clear"), sem("prm_loaded")
        rstd_ready, ident_ready = sem("rstd_ready"), sem("ident_ready")
        consts_ready, prm_turned, prm_ready = sem("consts_ready"), sem("prm_turned"), sem("prm_ready")
        stored = sem("stored")

        two_pieces = [prods[k][0]["slot"] for k in ("aux", "gdn0", "gdn1")]

        def slot_of(base_slot, j, i=0):
            n = base_slot + j
            twice = sum(min(max((n - first) // RING + 1, 0), 2) for first in two_pieces)
            return n % RING, n + 16 * i, 16 * (n // RING + 1 + twice) + 64 * i

        def wait_pair(eng, need):
            if need is not None:
                eng.wait_ge(sem(need[0]), need[1])

        def load_slot(sp, src, base_slot, j, i=0, width=CW):
            s, n, _ = slot_of(base_slot, j, i)
            if not (isinstance(n, int) and n < RING):
                sp.wait_ge(wlo_ready, n - RING + 1)
            dst = raw[:, s, :, :] if width == CW else raw[:, s, :, 0:width]
            sp.dma_start(dst, src).then_inc(LOADED[s], 16)

        def split_hi(act, base_slot, j, i=0, width=CW):
            s, n, ld = slot_of(base_slot, j, i)
            act.wait_ge(LOADED[s], ld)
            if not (isinstance(n, int) and n < RING):
                act.wait_ge(slot_used, n - RING + 1)
            nc.scalar.activation(whi[:, s, :, 0:width], raw[:, s, :, 0:width], ACT.Copy).then_inc(whi_ready, 1)

        def split_lo(dve, base_slot, j, i=0, width=CW):
            s, n, _ = slot_of(base_slot, j, i)
            dve.wait_ge(whi_ready, n + 1)
            nc.vector.tensor_tensor(wlo[:, s, :, 0:width], raw[:, s, :, 0:width],
                                    whi[:, s, :, 0:width].bitcast(F32), ALU.subtract).then_inc(wlo_ready, 1)

        def multiply(pe, pr, free, acts, i=0, width=CW, k0=0, ahead_of=()):
            wait_pair(pe, free)
            for j in range(pr["ns"]):
                for slot, step in ahead_of:
                    if slot == j:
                        step()
                multiply_slot(pe, pr, j, acts, i, width, k0)

        def multiply_normed(pe, pr, free, tag, width=CW):
            t, s = turns[tag]
            turn(pe, t)
            wait_pair(pe, free)
            for c in range(NDC):
                if c + 1 < NDC:
                    turn(pe, t + c + 1)
                pe.wait_ge(x_ready, s + c + 1)
                for j in range(2 * c, 2 * c + 2):
                    multiply_slot(pe, pr, j, (xhi, xlo), width=width)

        def multiply_slot(pe, pr, j, acts, i=0, width=CW, k0=0, kks=range(SK)):
            a_hi, a_lo = acts
            s, n, _ = slot_of(pr["slot"], j, i)
            if 0 in kks:
                pe.wait_ge(wlo_ready, n + 1)
            for kk in kks:
                k = j * SK + kk
                first, final = k == 0, k == pr["ns"] * SK - 1
                for tt in range(TT):
                    tok = slice(tt * P, (tt + 1) * P)
                    out = pp[:, 2 * pr["par"] + tt, 0:width]
                    w_hi, w_lo = whi[:, s, kk, 0:width], wlo[:, s, kk, 0:width]
                    nc.tensor.matmul(out, a_hi[:, k0 + k, tok], w_hi, start=first, stop=False)
                    nc.tensor.matmul(out, a_lo[:, k0 + k, tok], w_hi, start=False, stop=False)
                    mm = nc.tensor.matmul(out, a_hi[:, k0 + k, tok], w_lo, start=False, stop=final)
            if SK - 1 in kks:
                mm.then_inc(slot_used, 1)

        BG = [pr for phase in ("gdn1", "rw0", "rw1", "gates") for pr in prods[phase]]
        BGN = len(BG) * (KT // SK)
        upto, total = {}, 0
        for name, n in background():
            total = min(total + n, BGN * SK)
            upto[name] = total
        upto["rest"] = BGN * SK
        def split_upto(name):
            return min(upto[name] // SK + LEAD, BGN)

        LEAD = RING - 1
        spooled_before = max(0, (split_upto("gdn1.y") - 5) // (KT // SK))
        at_pe, at_act, at_dve = [0], [RING], [RING]

        def bg_pe(pe, name):
            for k in range(at_pe[0], upto[name]):
                pr, j, kk = BG[k // KT], k % KT // SK, k % SK
                if k % KT == 0:
                    wait_pair(pe, pr["free"])
                multiply_slot(pe, pr, j, (xhi, xlo), kks=(kk,))
            at_pe[0] = max(at_pe[0], upto[name])

        def bg_act(act, name, spool):
            for n in range(at_act[0], split_upto(name)):
                q, j = n // (KT // SK), n % (KT // SK)
                split_hi(act, BG[q]["slot"], j)
                if j == 4 and q > 0:
                    spool_out(act, q - 1, spool)
            at_act[0] = max(at_act[0], split_upto(name))

        def spool_out(act, q, spool):
            pr = BG[q]
            act.wait_ge(slot_used, pr["done"])
            if q > 0:
                act.wait_ge(sem("spooled"), 16 * q)
            nc.scalar.activation(spool[:, :, :], pair(pr["par"]), ACT.Copy).then_inc(sem(pr["released"][0]), 1)
            act.wait_ge(sem(pr["released"][0]), pr["released"][1])
            act.dma_start(proj[q].rearrange("(t p) c -> p t c", p=P), spool[:, :, :]).then_inc(sem("spooled"), 16)

        def bg_dve(dve, name):
            for n in range(at_dve[0], split_upto(name)):
                split_lo(dve, BG[n // (KT // SK)]["slot"], n % (KT // SK))
            at_dve[0] = max(at_dve[0], split_upto(name))

        def turn(pe, t, src_ready=None):
            if src_ready is None:
                pe.wait_ge(nat_ready, t + 1)
            else:
                pe.wait_ge(*src_ready)
            if not (isinstance(t, int) and t == 0):
                pe.wait_ge(xf_ready, t)
            for kk in range(4):
                for tt in range(TT):
                    mm = nc.tensor.transpose(pa[:, kk, tt * P:(tt + 1) * P], nat[:, tt, kk * P:(kk + 1) * P], ident[:, :])
            mm.then_inc(turned, 1)

        def take(dve, t, s, gain=None):
            dve.wait_ge(turned, t + 1)
            if not (isinstance(s, int) and s == 0):
                dve.wait_ge(hi_ready, s)
                dve.wait_ge(x_ready, s)
            if gain is None:
                nc.vector.tensor_copy(xf[:, :, :], pa[:, :, :]).then_inc(xf_ready, 1)
            else:
                for kk in range(4):
                    op = nc.vector.tensor_scalar(xf[:, kk, :], pa[:, kk, :], prm[:, gain + kk:gain + kk + 1], None, ALU.mult)
                op.then_inc(xf_ready, 1)

        def x_hi(act, t, dst):
            act.wait_ge(xf_ready, t + 1)
            nc.scalar.activation(dst, xf[:, :, :], ACT.Copy).then_inc(hi_ready, 1)

        def x_lo(dve, s, dst_hi, dst_lo):
            dve.wait_ge(hi_ready, s + 1)
            nc.vector.tensor_tensor(dst_lo, xf[:, :, :], dst_hi.bitcast(F32), ALU.subtract).then_inc(x_ready, 1)

        def sumsq(act, src, q, c):
            if NDC * q + c > 0:
                act.wait_ge(sumsq_ready, NDC * q + c)
            for tt in range(TT):
                op = nc.scalar.activation(gs[:, tt, :], src[:, tt, c * CW:(c + 1) * CW], ACT.Square,
                                          accum_out=ss[:, tt, c:c + 1])
            op.then_inc(sumsq_ready, 1)

        def norm_root(act, q):
            act.wait_ge(ms_ready, q + 1)
            nc.scalar.activation(rms[:, :], ssum[:, :], ACT.Sqrt, bias=epsn[:, 0:1], scale=1.0 / D).then_inc(rms_ready, 1)

        def norm_scale(dve, q):
            dve.wait_ge(sumsq_ready, NDC * (q + 1))
            nc.vector.tensor_reduce(ssum[:, :], ss[:, :, :], AX_X, ALU.add).then_inc(ms_ready, 1)
            dve.wait_ge(rms_ready, q + 1)
            nc.vector.reciprocal(rstd[:, :], rms[:, :]).then_inc(rstd_ready, 1)
            dve.wait_ge(rstd_ready, q + 1)

        def norm_chunk(dve, src, c, t):
            if t > 0:
                dve.wait_ge(turned, t)
            for tt in range(TT):
                op = nc.vector.tensor_scalar(nat[:, tt, :], src[:, tt, c * CW:(c + 1) * CW], rstd[:, tt:tt + 1], None, ALU.mult)
            op.then_inc(nat_ready, 1)

        EARLY = RING + 2

        def norm_dve(dve, q, tag, gain, pr, width=CW):
            t, s = turns[tag]
            norm_scale(dve, q)
            for c in range(NDC):
                if c == NDC - 1:
                    for j in range(RING, EARLY):
                        split_lo(dve, pr["slot"], j, width=width)
                take(dve, t + c, s + c, PRM[gain] + 4 * c)
                x_lo(dve, s + c, xhi[:, 4 * c:4 * c + 4, :], xlo[:, 4 * c:4 * c + 4, :])

        def norm_act(act, q, src, tag, pr, width=CW):
            t, s = turns[tag]
            norm_root(act, q)
            act.wait_ge(rstd_ready, q + 1)
            for c in range(NDC + 1):
                if c < NDC:
                    if t + c > 0:
                        act.wait_ge(turned, t + c)
                    for tt in range(TT):
                        op = nc.scalar.activation(nat[:, tt, :], src[:, tt, c * CW:(c + 1) * CW], ACT.Copy, scale=rstd[:, tt:tt + 1])
                    op.then_inc(nat_ready, 1)
                if c == NDC:
                    for j in range(RING, EARLY):
                        split_hi(act, pr["slot"], j, width=width)
                if c > 0:
                    x_hi(act, t + c - 1, xhi[:, 4 * c - 4:4 * c, :])

        chain = {}

        def link(eng, ins):
            name = {dve_engine: "dve_chain", act_engine: "act_chain", pool_engine: "pool_chain"}[type(eng)]
            chain[name] = chain.get(name, 0) + 1
            ins.then_inc(sem(name), 1)
            eng.wait_ge(sem(name), chain[name])

        dve_engine, act_engine, pool_engine = type(nc.vector), type(nc.scalar), type(nc.gpsimd)

        def ffn_load(sp, tag, w_gate, w_up, w_down):
            gu, dn = prods[tag + "gu"], prods[tag + "dn"]

            def chunk(i):
                for m, w in enumerate((w_gate, w_up)):
                    for j in range(KT // SK):
                        src = w[j * SK * P:(j + 1) * SK * P, ds(i * CW, CW)].rearrange("(k p) n -> p k n", p=P)
                        load_slot(sp, src, gu[m]["slot"], j, i)

            chunk(0)
            with sp.Fori(1, NFC) as i:
                chunk(i)
            for c in range(NDC):
                for j in range(FT // SK):
                    src = w_down[j * SK * P:(j + 1) * SK * P, c * CW:(c + 1) * CW].rearrange("(k p) n -> p k n", p=P)
                    load_slot(sp, src, dn[c]["slot"], j)

        def ffn_pe(pe, tag):
            gu, dn = prods[tag + "gu"], prods[tag + "dn"]
            t0, s0 = turns[tag + "act"]

            multiply_normed(pe, gu[0], gu[0]["free"], tag + "norm")
            multiply(pe, gu[1], gu[1]["free"], (xhi, xlo))
            with pe.Fori(1, NFC) as i:
                multiply(pe, gu[0], (gu[0]["released"][0], gu[0]["released"][1] + i - 1), (xhi, xlo), i)
                turn(pe, t0 + i - 1)
                multiply(pe, gu[1], ("nat_ready", t0 + i), (xhi, xlo), i)
            pe.wait_ge(x_ready, s0 + NFC - 1)
            for c in range(NDC):
                late = ((RING, lambda: turn(pe, t0 + NFC - 1)),
                        (FT // SK - 2, lambda: pe.wait_ge(x_ready, s0 + NFC))) if c == 0 else ()
                multiply(pe, dn[c], dn[c]["free"], (hhi, hlo), ahead_of=late)

        def ffn_act(act, tag):
            gu, dn = prods[tag + "gu"], prods[tag + "dn"]
            t0, s0 = turns[tag + "act"]

            def chunk(i, first):
                for j in range(EARLY if first else 0, KT // SK):
                    split_hi(act, gu[0]["slot"], j, i)
                for j in range(KT // SK):
                    split_hi(act, gu[1]["slot"], j, i)
                    if j == 4:
                        if not first:
                            x_hi(act, t0 + i - 1, hhi[:, ds(4 * i - 4, 4), :])
                        act.wait_ge(slot_used, gu[0]["done"] + 16 * i)
                        act.wait_ge(nat_ready, t0 + i)
                        nc.scalar.activation(gs[:, :, :], pair(gu[0]["par"]), ACT.Silu).then_inc(sem(gu[0]["released"][0]), 1)

            chunk(0, True)
            with act.Fori(1, NFC) as i:
                chunk(i, False)
            for c in range(NDC):
                for j in range(FT // SK):
                    split_hi(act, dn[c]["slot"], j)
                    if c == 0 and j == 7:
                        x_hi(act, t0 + NFC - 1, hhi[:, 4 * NFC - 4:4 * NFC, :])
                    if c > 0 and j == 5:
                        act.wait_ge(sem(dn[c - 1]["released"][0]), dn[c - 1]["released"][1])
                        sumsq(act, h, 1 if tag == "f1" else 5, c - 1)

        def ffn_dve(dve, tag):
            gu, dn = prods[tag + "gu"], prods[tag + "dn"]
            t0, s0 = turns[tag + "act"]

            def gated(i):
                dve.wait_ge(slot_used, gu[1]["done"] + 16 * i)
                dve.wait_ge(sem(gu[0]["released"][0]), gu[0]["released"][1] + i)
                dve.wait_ge(turned, t0 + i)
                nc.vector.tensor_tensor(nat[:, :, :], gs[:, :, :], pair(gu[1]["par"]), ALU.mult).then_inc(nat_ready, 1)

            def chunk(i, first):
                for j in range(EARLY if first else 0, KT // SK):
                    split_lo(dve, gu[0]["slot"], j, i)
                    if j == 4 and not first:
                        gated(i - 1)
                for j in range(KT // SK):
                    split_lo(dve, gu[1]["slot"], j, i)
                    if j == 2 and not first:
                        take(dve, t0 + i - 1, s0 + i - 1)
                    if j == 6 and not first:
                        x_lo(dve, s0 + i - 1, hhi[:, ds(4 * i - 4, 4), :], hlo[:, ds(4 * i - 4, 4), :])

            chunk(0, True)
            with dve.Fori(1, NFC) as i:
                chunk(i, False)
            for c in range(NDC):
                for j in range(FT // SK):
                    split_lo(dve, dn[c]["slot"], j)
                    if c == 0 and j == 3:
                        gated(NFC - 1)
                    if c == 0 and j == 6:
                        take(dve, t0 + NFC - 1, s0 + NFC - 1)
                    if c == 0 and j == 9:
                        x_lo(dve, s0 + NFC - 1, hhi[:, 4 * NFC - 4:4 * NFC, :], hlo[:, 4 * NFC - 4:4 * NFC, :])
                    if c > 0 and j == 4:
                        residual(dve, dn[c - 1], c - 1, 0.5)

        def residual(dve, pr, c, scale):
            dve.wait_ge(slot_used, pr["done"])
            hc = h[:, :, c * CW:(c + 1) * CW]
            nc.vector.scalar_tensor_tensor(hc, pair(pr["par"]), scale, hc, ALU.mult, ALU.add).then_inc(sem(pr["released"][0]), 1)

        auxt = at("auxt", AR, [3, T + 1])
        lora = at("lora", AR + 3.25, [3, T])
        beta_t = at("beta_t", AR + 6.25, [T])
        gc_t = at("gc_t", AR + 7.25, [T])
        sp_a = at("sp_a", AR + 8.25, [T])
        sp_b = at("sp_b", AR + 9.25, [T])
        qkp = at("qkp", AR + 10.25, [4, T + CONV - 1])
        vp = at("vp", AR + 14.5, [4, T + CONV - 1])
        zg = at("zg", AR + 18.75, [TT, CW])
        qk = at("qk", AR + 22.75, [4, T])
        vg = at("vg", AR + 26.75, [4, T])
        kb = at("kb", AR + 30.75, [4, T])
        qe = at("qe", AR + 34.75, [4, T])
        eg = at("eg", AR + 38.75, [4, T])
        bb = at("bb", AR + 42.75, [4, T])
        kn = at("kn", AR + 46.75, [TT, 2 * P])
        vb = at("vb", AR + 48.75, [TT, CW])
        dec = at("dec", AR + 52.75, [8, C])
        att = at("att", AR + 54.75, [8, C])
        ut_g = at("ut_g", AR + 56.75, [8, C])
        s_g = at("s_g", AR + 70.75, [2, 4, GH])
        r_g = at("r_g", AR + 60.75, [4, GH])
        vn_g = at("vn_g", AR + 62.75, [4, GH])
        vs_g = at("vs_g", AR + 64.75, [4, GH])
        o_g = at("o_g", AR + 66.75, [TT, CW])
        sq_g = at("sq_g", AR + 70.75, [4, T])
        so_g = at("so_g", AR + 74.75, [4, T])
        ri_g = at("ri_g", AR + 74.75, [4, T])
        inv_g = [at(f"inv_g{k}", AR + kib, [8, C]) for k, kib in enumerate((10.25, 12.25, 14.25, 16.25, 78.75, 80.75))]
        w2z = at("w2z", AR + 6.25, [CW])
        a2z = at("a2z", AR + 8.25, [CW])
        g2a = at("g2a", AR + 10.25, [CW])
        g2b = at("g2b", AR + 12.25, [CW])
        rkv = [at(f"rkv{m}", AR + kib, [4, T + 1]) for m, kib in enumerate((14.25, 18.5, 22.75))]
        az = at("az", AR + 27, [4, 2, T])
        rz = at("rz", AR + 35, [4, 2, T])
        bt = at("bt", AR + 43, [4, T])
        kt = at("kt", AR + 47, [4, T])
        gt = at("gt", AR + 51, [4, T])
        tmp = [at(f"tmp{m}", AR + 55 + 4 * m, [4, T]) for m in range(8)]
        bn = at("bn", AR + 55, [TT, CW])
        kn_r = at("kn_r", AR + 59, [TT, CW])
        vn_r = at("vn_r", AR + 63, [TT, CW])
        ut_r = at("ut_r", AR + 67, [TT, 8, C])
        ak = at("ak", AR + 71, [TT, 8, C])
        rb = at("rb", AR + 75, [TT, 8, C])
        rk = at("rk", AR + 79, [TT, 8, C])
        r_r = at("r_r", AR + 14.25, [8, C])
        sa_r = at("sa_r", AR + 16.25, [8, C])
        y_r = at("y_r", AR + 18.5, [TT, CW])
        bonus = at("bonus", AR + 22.75, [4, T])
        s_r = at("s_r", AR, [2, 4, C])
        inv_r = [at(f"inv_r{k}", AR + kib, [8, C]) for k, kib in enumerate((83, 85, 6.25, 8.25, 10.25, 12.25))]
        yhi = at("yhi", AR, [16, T], F32R)
        ylo = at("ylo", AR + 72, [16, T], F32R)
        yf = at("yf", AR + 56, [16, T])
        ga = at("ga", AR + 16, [TT, CW])
        gb = at("gb", AR + 20, [TT, CW])
        mhi = at("mhi", AR + 24, [KT, T], F32R)
        mlo = at("mlo", AR + 40, [KT, T], F32R)
        msb = at("msb", AR + 56, [TT, D])
        qhi = at("qhi", AR + 48, [KT, T], F32R)
        qlo = at("qlo", AR + 64, [KT, T], F32R)
        qt = at("qt", AR, [KT, T])
        kt_m = at("kt_m", AR + 16, [KT, T])
        v_m = at("v_m", AR + 32, [TT, D])
        pr_m = at("pr_m", AR + 80, [2, TT, T])
        pt_m = at("pt_m", AR + 84, [2, TT, T])

        gc_n = scal[:, 0:16].rearrange("p (t g) -> p t g", t=TT)
        be_n = scal[:, 16:32].rearrange("p (t g) -> p t g", t=TT)
        nbe_n = scal[:, 32:48].rearrange("p (t g) -> p t g", t=TT)
        dtb, nal = scal[0:GHV, 48:49], scal[0:GHV, 49:50]
        eps_q, eps_k, eps_gn, one_c = scal[:, 50:51], scal[:, 51:52], scal[:, 52:53], scal[:, 53:54]
        msum = scal[:, 64:80]
        mroot = scal[:, 80:96]
        msum2 = scal[:, 96:112]
        mroot2 = scal[:, 112:128]
        pc = scal[:, 128:144].rearrange("p (d c) -> p d c", d=4)
        omu = scal[:, 176:200]
        mx = scal[:, 144:152].rearrange("p (g t) -> p g t", g=MH)
        nmx = scal[:, 152:160].rearrange("p (g t) -> p g t", g=MH)
        den = scal[:, 160:168].rearrange("p (g t) -> p g t", g=MH)
        rden = scal[:, 168:176].rearrange("p (g t) -> p g t", g=MH)

        spool_g = at("spool_g", AR + 83, [TT, CW])
        spool_r = at("spool_r", 100.75, [TT, CW])
        proj = nc.dram_tensor("proj", (17, T, CW), F32, kind="Internal").ap()
        y_turned = nc.dram_tensor("y_turned", (16, P, T), F32, kind="Internal").ap()

        bank = [pa[:, 0:2, :], pa[:, 2:4, :], pb[:, 0:2, :], pb[:, 2:4, :]]
        units = [b.rearrange("p a (u c) -> p (a u) c", c=C) for b in bank]
        heads4 = [b.rearrange("p a (u c) -> p (a u) c", c=GH) for b in bank]

        def over_units(mask):
            return mask[:, :].unsqueeze(1).to_broadcast([P, 8, C])

        INV_MM, INV_DVE, INV_ACT = 10, 9, 7

        def copy(act, dst, src):
            return nc.scalar.activation(dst, src, ACT.Copy)

        def invert_pe(pe, v, buf):
            a, b, c, d, e, f = buf
            mm_done, by_dve, by_act = sem("inv_mm"), sem("inv_dve"), sem("inv_act")
            dv, ac = INV_DVE * v, INV_ACT * v

            def blocks(out, lhs, rhs):
                for u in range(8):
                    for cp in range(2):
                        r = slice(cp * C, (cp + 1) * C)
                        right = rhs[r, u, :] if rhs is not eye else eye[r, :]
                        mm = nc.tensor.matmul(out[r, u, :], lhs[r, u, :], right, start=True, stop=True)
                return mm

            def mark(k):
                bg_pe(pe, f"inv{v}.{k}")

            pe.wait_ge(sem("inv_in"), v + 1)
            blocks(units[0], a, eye).then_inc(mm_done, 1)
            mark(1)
            pe.wait_ge(by_act, ac + 1)
            blocks(units[1], b, a)
            blocks(units[2], a, b).then_inc(mm_done, 1)
            mark(2)
            pe.wait_ge(by_dve, dv + 2)
            pe.wait_ge(by_act, ac + 2)
            blocks(units[0], d, c)
            blocks(units[3], c, d)
            blocks(units[1], d, e).then_inc(mm_done, 1)
            mark(3)
            pe.wait_ge(by_dve, dv + 4)
            pe.wait_ge(by_act, ac + 3)
            blocks(units[2], a, b)
            blocks(units[0], b, e).then_inc(mm_done, 1)
            mark(4)
            pe.wait_ge(by_dve, dv + 5)
            pe.wait_ge(by_act, ac + 4)
            blocks(units[1], c, e).then_inc(mm_done, 1)
            mark(5)
            pe.wait_ge(by_dve, dv + 6)
            blocks(units[2], e, eye).then_inc(mm_done, 1)
            mark(6)
            pe.wait_ge(by_act, ac + 5)
            blocks(units[0], d, f)
            blocks(units[3], f, d).then_inc(mm_done, 1)
            mark(7)
            pe.wait_ge(by_dve, dv + 7)
            pe.wait_ge(by_act, ac + 6)
            blocks(units[2], a, b).then_inc(mm_done, 1)
            mark(8)
            pe.wait_ge(by_act, ac + 7)
            blocks(units[1], c, e).then_inc(mm_done, 1)
            mark(9)
            pe.wait_ge(by_dve, dv + 8)
            blocks(units[0], b, d).then_inc(mm_done, 1)
            mark(10)

        def invert_act(act, v, buf, spool):
            a, b, c, d, e, f = buf
            for step, dst, u in ((1, b, 0), (2, d, 2), (3, b, 3), (4, c, 2), (6, d, 2), (7, b, 3), (8, c, 2)):
                act.wait_ge(sem("inv_mm"), INV_MM * v + step)
                copy(act, dst[:, :, :], units[u]).then_inc(sem("inv_act"), 1)
                bg_act(act, f"inv{v}.{step if step not in (4, 8) else step + 1}", spool)
            bg_act(act, f"inv{v}.10", spool)

        def invert_dve(dve, v, buf, out):
            a, b, c, d, e, f = buf

            def step(n, ins_of):
                dve.wait_ge(sem("inv_mm"), INV_MM * v + n)
                ins_of().then_inc(sem("inv_dve"), 1)

            v_ = nc.vector
            v_.tensor_tensor(e[:, :, :], a[:, :, :], over_units(eye), ALU.add).then_inc(sem("inv_dve"), 1)
            bg_dve(dve, f"inv{v}.1")
            step(2, lambda: v_.tensor_copy(c[:, :, :], units[1]))
            bg_dve(dve, f"inv{v}.2")
            step(3, lambda: v_.tensor_copy(a[:, :, :], units[0]))
            step(3, lambda: v_.tensor_tensor(e[:, :, :], e[:, :, :], units[1], ALU.add))
            bg_dve(dve, f"inv{v}.3")
            step(4, lambda: v_.tensor_tensor(e[:, :, :], e[:, :, :], units[0], ALU.add))
            bg_dve(dve, f"inv{v}.4")
            step(5, lambda: v_.tensor_tensor(e[:, :, :], e[:, :, :], units[1], ALU.add))
            bg_dve(dve, f"inv{v}.6")
            step(7, lambda: v_.tensor_copy(a[:, :, :], units[0]))
            bg_dve(dve, f"inv{v}.8")
            step(9, lambda: v_.tensor_tensor(d[:, :, :], e[:, :, :], units[1], ALU.add))
            bg_dve(dve, f"inv{v}.9")
            step(10, lambda: v_.tensor_tensor(out, d[:, :, :], units[0], ALU.add))
            bg_dve(dve, f"inv{v}.10")
            dve.wait_ge(sem("inv_dve"), INV_DVE * (v + 1))

        def mix_nat(dve, pr, m):
            dve.wait_ge(slot_used, pr["done"])
            if m > 0:
                dve.wait_ge(sem("mix_turned"), m)
            nc.vector.tensor_copy(nat[:, :, :], pair(pr["par"])).then_inc(sem(pr["released"][0]), 1)

        def mix_turn(pe, m, src, ready):
            pe.wait_ge(*ready)
            if m > 0:
                pe.wait_ge(sem("mix_take"), m)
            for kk in range(4):
                for tt in range(TT):
                    mm = nc.tensor.transpose(pa[:, kk, tt * P:(tt + 1) * P], src[:, tt, kk * P:(kk + 1) * P], ident[:, :])
            mm.then_inc(sem("mix_turned"), 1)

        def mix_take(eng, dst, m):
            eng.wait_ge(sem("mix_turned"), m + 1)
            op = copy(eng, dst, pa[:, :, :]) if type(eng) is act_engine else nc.vector.tensor_copy(dst, pa[:, :, :])
            op.then_inc(sem("mix_take"), 1)
            eng.wait_ge(sem("mix_take"), m + 1)

        AUX = prods["aux"][0]

        BESIDE_AUX = 6

        def aux_pe(pe):
            pe.wait_ge(consts_ready, 1)
            multiply_normed(pe, AUX, AUX["free"], "mixnorm", width=AUXW)
            first = prods["gdn0"][0]
            wait_pair(pe, first["free"])
            for j in (0, 1):
                multiply_slot(pe, first, j, (xhi, xlo))
            pe.wait_ge(sem(AUX["released"][0]), AUX["released"][1])
            for tt in range(TT):
                tok = slice(tt * P, (tt + 1) * P)
                nc.tensor.transpose(pa[:, 0, tok], nat[:, tt, 0:P], ident[:, :])
                nc.tensor.transpose(pa[:, 1, tok], nat[:, tt, P:2 * P], ident[:, :])
                nc.tensor.transpose(pa[0:32, 2, tok], nat[:, tt, 2 * P:LORA], ident[:, :])
                nc.tensor.transpose(pa[0:GHV, 3, tok], nat[:, tt, LORA:LORA + GHV], ident[:, :])
                mm = nc.tensor.transpose(pb[0:GHV, 0, tok], nat[:, tt, LORA + GHV:AUXW], ident[:, :])
            mm.then_inc(sem("aux_turned"), 1)
            for j in range(2, BESIDE_AUX):
                multiply_slot(pe, first, j, (xhi, xlo))
            pe.wait_ge(sem("gc_ready"), 1)
            for tt in range(TT):
                tok = slice(tt * P, (tt + 1) * P)
                nc.tensor.transpose(pb[:, 2, 8 * tt:8 * tt + 8], gc_t[0:GHV, tok], ident[0:GHV, 0:GHV])
                mm = nc.tensor.transpose(pb[:, 2, 16 + 8 * tt:24 + 8 * tt], beta_t[0:GHV, tok], ident[0:GHV, 0:GHV])
            mm.then_inc(sem("scalars_turned"), 1)

        def aux_dve(dve):
            v_ = nc.vector
            dve.wait_ge(consts_ready, 1)
            link(dve, v_.tensor_scalar(omu, prm[:, PRM["mu_rkv"]:PRM["mu_rkv"] + 24], -1.0, 1.0, ALU.mult, ALU.add))
            for cell, value in ((eps_q, RMS_EPS * GH), (eps_k, RMS_EPS), (eps_gn, RW_GN_EPS), (one_c, 1.0)):
                link(dve, v_.memset(cell, value))
            dve.wait_ge(slot_used, AUX["done"])
            v_.tensor_copy(nat[:, :, 0:AUXW], pair(AUX["par"])[:, :, 0:AUXW]).then_inc(sem(AUX["released"][0]), 1)
            link(dve, v_.memset(auxt[:, :, :], 0.0))
            dve.wait_ge(sem("aux_turned"), 1)
            v_.tensor_copy(auxt[:, 0:2, 1:T + 1], pa[:, 0:2, :])
            link(dve, v_.tensor_copy(auxt[0:32, 2, 1:T + 1], pa[0:32, 2, :]))
            link(dve, v_.tensor_tensor(lora[:, :, :], auxt[:, :, 0:T], auxt[:, :, 1:T + 1], ALU.subtract))
            for m, name in enumerate(("mu_wa", "mu_g0", "mu_g1")):
                op = v_.scalar_tensor_tensor(lora[:, m, :], lora[:, m, :], prm[:, PRM[name]:PRM[name] + 1],
                                             auxt[:, m, 1:T + 1], ALU.mult, ALU.add)
            op.then_inc(sem("lora_mixed"), 1)
            dve.wait_ge(sem("gdn_loaded"), 32)
            v_.tensor_copy(beta_t[0:GHV, :], pa[0:GHV, 3, :]).then_inc(sem("beta_raw"), 1)
            link(dve, v_.tensor_scalar(sp_a[0:GHV, :], pb[0:GHV, 0, :], dtb, None, ALU.add))
            link(dve, v_.tensor_scalar(gc_t[0:GHV, :], sp_a[0:GHV, :], -1.0, None, ALU.mult))
            v_.tensor_tensor(sp_b[0:GHV, :], sp_a[0:GHV, :], gc_t[0:GHV, :], ALU.max).then_inc(sem("abs_ready"), 1)
            for j in range(RING, BESIDE_AUX):
                split_lo(dve, prods["gdn0"][0]["slot"], j)
            dve.wait_ge(sem("ln_ready"), 1)
            link(dve, v_.scalar_tensor_tensor(sp_a[0:GHV, :], sp_a[0:GHV, :], 0.0, sp_b[0:GHV, :], ALU.max, ALU.add))
            link(dve, v_.tensor_scalar(nal, nal, -1.0, None, ALU.mult))
            link(dve, v_.tensor_scalar(sp_a[0:GHV, :], sp_a[0:GHV, :], nal, None, ALU.mult))
            v_.tensor_tensor_scan(gc_t[0:GHV, :], scanmask[0:GHV, :], sp_a[0:GHV, :], 0.0, ALU.mult, ALU.add).then_inc(sem("gc_ready"), 1)
            dve.wait_ge(sem("scalars_turned"), 1)
            v_.tensor_copy(scal[:, 0:32], pb[:, 2, 0:32]).then_inc(sem("scalars_ready"), 1)
            dve.wait_ge(sem("exp_gc"), 1)
            link(dve, v_.scalar_tensor_tensor(scal[:, 32:48], scal[:, 32:48], -1.0, scal[:, 16:32], ALU.mult, ALU.mult))

        def aux_act(act):
            for j in range(RING, BESIDE_AUX):
                split_hi(act, prods["gdn0"][0]["slot"], j)
            act.wait_ge(sem("lora_mixed"), 1)
            nc.scalar.activation(lora[0:LORA_D, 0, :], lora[0:LORA_D, 0, :], ACT.Tanh)
            nc.scalar.activation(lora[:, 1:3, :], lora[:, 1:3, :], ACT.Sigmoid)
            act.wait_ge(sem("beta_raw"), 1)
            link(act, nc.scalar.activation(beta_t[0:GHV, :], beta_t[0:GHV, :], ACT.Sigmoid))
            act.wait_ge(sem("gdn_loaded"), 32)
            link(act, nc.scalar.activation(nal, nal, ACT.Exp))
            act.wait_ge(sem("abs_ready"), 1)
            link(act, nc.scalar.activation(sp_b[0:GHV, :], sp_b[0:GHV, :], ACT.Exp, scale=-1.0))
            nc.scalar.activation(sp_b[0:GHV, :], sp_b[0:GHV, :], ACT.Ln, bias=one_c[0:GHV, :]).then_inc(sem("ln_ready"), 1)
            act.wait_ge(sem("scalars_ready"), 1)
            nc.scalar.activation(scal[:, 32:48], scal[:, 0:16], ACT.Exp).then_inc(sem("exp_gc"), 1)

        def gdn_pe(pe, hf):
            g = prods[f"gdn{hf}"]
            n = hf + 1
            if hf == 0:
                for j in range(BESIDE_AUX, KT // SK):
                    multiply_slot(pe, g[0], j, (xhi, xlo))
                multiply(pe, g[1], g[1]["free"], (xhi, xlo))
                mix_turn(pe, 0, nat, (sem(g[0]["released"][0]), g[0]["released"][1]))
                multiply(pe, g[2], g[2]["free"], (xhi, xlo))
                mix_turn(pe, 1, nat, (sem(g[1]["released"][0]), g[1]["released"][1]))
            else:
                pe.wait_ge(sem("y_ready"), 1)
                mix_turn(pe, 2, gs, (sem("gs_loaded"), 16))
                mix_turn(pe, 3, nat, (sem("nat_loaded"), 16))
            bg_pe(pe, f"gdn{hf}.conv")
            pe.wait_ge(sem("g_sq"), n)
            for kk in range(4):
                mm = nc.tensor.matmul(pb[:, kk, :], ones[:, :], sq_g[:, kk, :], start=True, stop=True)
            mm.then_inc(sem("g_norms"), 1)
            bg_pe(pe, f"gdn{hf}.norms")
            pe.wait_ge(sem("mix_take"), 2 * n)
            pe.wait_ge(sem("g_rooted"), n)
            for hl in range(4):
                hv = 4 * hf + hl
                nc.tensor.matmul(pa[:, hl, :], sel[0:GHV, hv, :], gc_t[0:GHV, :], start=True, stop=True)
                mm = nc.tensor.matmul(pb[:, hl, :], sel[0:GHV, hv, :], beta_t[0:GHV, :], start=True, stop=True)
            mm.then_inc(sem("g_rows"), 1)
            bg_pe(pe, f"gdn{hf}.rows")
            pe.wait_ge(sem("g_qk"), n)
            pe.wait_ge(sem("g_dec"), n)
            pe.wait_ge(sem("g_vact"), n)
            for tt in range(TT):
                tok = slice(tt * P, (tt + 1) * P)
                for kk in range(2):
                    nc.tensor.transpose(bank[2][:, tt, kk * P:(kk + 1) * P], qk[:, 2 + kk, tok], ident[:, :])
                for kk in range(4):
                    mm = nc.tensor.transpose(bank[tt][:, kk // 2, (kk % 2) * P:(kk % 2 + 1) * P], vg[:, kk, tok], ident[:, :])
            mm.then_inc(sem("g_naturals"), 1)
            bg_pe(pe, f"gdn{hf}.naturals")
            pe.wait_ge(sem("g_kb"), n)
            for u in range(8):
                tt, hl = u // 4, u % 4
                for cp in range(2):
                    r = slice(cp * C, (cp + 1) * C)
                    tok = slice(tt * P + cp * C, tt * P + (cp + 1) * C)
                    nc.tensor.matmul(units[2][r, u, :], qk[:, 2 + hl // 2, tok], kb[:, hl, tok], start=True, stop=True)
                    mm = nc.tensor.matmul(units[3][r, u, :], qk[:, 2 + hl // 2, tok], qk[:, hl // 2, tok], start=True, stop=True)
            mm.then_inc(sem("g_mats"), 1)
            bg_pe(pe, f"gdn{hf}.mats")
            invert_pe(pe, hf, inv_g)
            pe.wait_ge(sem("inv_dve"), INV_DVE * n)
            for c in range(NCH):
                tt, cp = c // 2, c % 2
                r = slice(cp * C, (cp + 1) * C)
                tok = slice(c * C, (c + 1) * C)
                m = NCH * hf + c
                pe.wait_ge(sem("g_state"), (NCH + 1) * hf + c + 1)
                for hl in range(4):
                    mm = nc.tensor.matmul(heads4[0][r, hl, :], qk[:, 2 + hl // 2, tok], s_g[:, c % 2, hl, :], start=True, stop=True)
                mm.then_inc(sem("g_ks"), 1)
                bg_pe(pe, f"gdn{hf}.ks{c}")
                pe.wait_ge(sem("g_r"), m + 1)
                for hl in range(4):
                    mm = nc.tensor.matmul(heads4[1][r, hl, :], ut_g[r, 4 * tt + hl, :], r_g[r, hl, :], start=True, stop=True)
                mm.then_inc(sem("g_vnew"), 1)
                bg_pe(pe, f"gdn{hf}.vnew{c}")
                pe.wait_ge(sem("g_vn"), m + 1)
                for hl in range(4):
                    mm = nc.tensor.matmul(heads4[3][:, hl, :], kn[r, tt, (hl // 2) * P:(hl // 2 + 1) * P], vs_g[r, hl, :],
                                          start=True, stop=True)
                mm.then_inc(sem("g_ds"), 1)
                if m > 0:
                    pe.wait_ge(sem("g_o"), m)
                for hl in range(4):
                    nc.tensor.matmul(heads4[2][r, hl, :], qe[:, hl, tok], s_g[:, c % 2, hl, :], start=True, stop=False)
                    mm = nc.tensor.matmul(heads4[2][r, hl, :], att[r, 4 * tt + hl, :], vn_g[r, hl, :], start=False, stop=True)
                mm.then_inc(sem("g_omm"), 1)
                bg_pe(pe, f"gdn{hf}.state{c}")
            bg_pe(pe, f"gdn{hf}.out")
            pe.wait_ge(sem("g_out"), n)
            for kk in range(4):
                for tt in range(TT):
                    mm = nc.tensor.transpose(pa[:, kk, tt * P:(tt + 1) * P], nat[:, tt, kk * P:(kk + 1) * P], ident[:, :])
            mm.then_inc(sem("g_out_turned"), 1)
            bg_pe(pe, f"gdn{hf}.y")

        def qk_tiles(hf):
            return [2 * hf, 2 * hf + 1, 4 + 2 * hf, 5 + 2 * hf]

        def v_tiles(hf):
            return [8 + 4 * hf + k for k in range(4)]

        def tap_weight(tap, tile):
            k = PRM["conv"] + 16 * tap + tile
            return prm[:, k:k + 1]

        def first_tap(act, dst, src, tiles):
            for kk, tile in enumerate(tiles):
                op = nc.scalar.activation(dst[:, kk, :], src[:, kk, 0:T], ACT.Copy, scale=tap_weight(0, tile))
            op.then_inc(sem("g_tap0"), 1)

        def gdn_act(act, hf):
            g = prods[f"gdn{hf}"]
            n = hf + 1

            def bg(name):
                bg_act(act, f"gdn{hf}.{name}", spool_g)

            if hf == 0:
                for m in range(3):
                    for j in range(BESIDE_AUX if m == 0 else 0, KT // SK):
                        split_hi(act, g[m]["slot"], j)
                next_hi(act, "gdn1")
                act.wait_ge(slot_used, g[2]["done"])
                nc.scalar.activation(zg[:, :, :], pair(g[2]["par"]), ACT.Silu).then_inc(sem(g[2]["released"][0]), 1)
            act.wait_ge(sem("pads_clear"), n)
            for m, (dst, src, tiles) in enumerate(((qk, qkp, qk_tiles(hf)), (vg, vp, v_tiles(hf)))):
                if hf == 0:
                    act.wait_ge(sem("mix_take"), m + 1)
                else:
                    mix_take(act, src[:, :, CONV - 1:], 2 + m)
                first_tap(act, dst, src, tiles)
            if hf > 0:
                act.wait_ge(sem("z_loaded"), 16)
                nc.scalar.activation(zg[:, :, :], zg[:, :, :], ACT.Silu).then_inc(sem("z_act"), 1)
            bg("conv")
            act.wait_ge(sem("g_conv"), 2 * hf + 1)
            link(act, nc.scalar.activation(qk[:, :, :], qk[:, :, :], ACT.Silu))
            nc.scalar.activation(sq_g[:, :, :], qk[:, :, :], ACT.Square).then_inc(sem("g_sq"), 1)
            act.wait_ge(sem("g_conv"), 2 * n)
            nc.scalar.activation(vg[:, :, :], vg[:, :, :], ACT.Silu).then_inc(sem("g_vact"), 1)
            act.wait_ge(sem("g_norms"), n)
            nc.scalar.activation(ri_g[:, 0:2, :], pb[:, 0:2, :], ACT.Ln, bias=eps_q, scale=float(GH))
            link(act, nc.scalar.activation(ri_g[:, 2:4, :], pb[:, 2:4, :], ACT.Ln, bias=eps_k))
            nc.scalar.activation(ri_g[:, :, :], ri_g[:, :, :], ACT.Exp, scale=-0.5).then_inc(sem("g_rooted"), 1)
            bg("norms")
            act.wait_ge(sem("g_rows"), n)
            nc.scalar.activation(eg[:, :, :], pa[:, :, :], ACT.Exp)
            copy(act, bb[:, :, :], pb[:, :, :]).then_inc(sem("g_eg"), 1)
            bg("rows")
            act.wait_ge(sem("g_diff"), n)
            nc.scalar.activation(dec[:, :, :], dec[:, :, :], ACT.Exp).then_inc(sem("g_decexp"), 1)
            bg("mats")
            invert_act(act, hf, inv_g, spool_g)
            for c in range(NCH):
                tt, cp = c // 2, c % 2
                r = slice(cp * C, (cp + 1) * C)
                bg(f"vnew{c}")
                act.wait_ge(sem("g_omm"), NCH * hf + c + 1)
                op = copy(act, o_g[r, tt, :], heads4[2][r, :, :].rearrange("p h d -> p (h d)"))
                op.then_inc(sem("g_o"), 1)
                bg(f"state{c}")
            act.wait_ge(sem("g_o"), NCH * n)
            nc.scalar.activation(so_g[:, :, :].rearrange("p a t -> p (a t)"), o_g[:, :, :].rearrange("p t d -> p (t d)"),
                                 ACT.Square).then_inc(sem("g_osq"), 1)
            bg("out")
            act.wait_ge(sem("g_oms"), n)
            nc.scalar.activation(mroot[:, 0:8], msum[:, 0:8], ACT.Sqrt, bias=eps_k, scale=1.0 / GH).then_inc(sem("g_oroot"), 1)
            bg("y")

        def gdn_dve(dve, hf):
            g = prods[f"gdn{hf}"]
            n = hf + 1
            v_ = nc.vector
            v_.memset(qkp[:, :, 0:CONV - 1], 0.0)
            v_.memset(vp[:, :, 0:CONV - 1], 0.0).then_inc(sem("pads_clear"), 1)

            def bg(name):
                bg_dve(dve, f"gdn{hf}.{name}")

            if hf == 0:
                for j in range(BESIDE_AUX, KT // SK):
                    split_lo(dve, g[0]["slot"], j)
                for j in range(KT // SK):
                    split_lo(dve, g[1]["slot"], j)
                    if j == 4:
                        mix_nat(dve, g[0], 0)
                for j in range(KT // SK):
                    split_lo(dve, g[2]["slot"], j)
                    if j == 4:
                        mix_take(dve, qkp[:, :, CONV - 1:], 0)
                        mix_nat(dve, g[1], 1)
                next_lo(dve, "gdn1")
                mix_take(dve, vp[:, :, CONV - 1:], 1)

            def conv(dst, src, tiles):
                for tap in range(1, CONV):
                    for kk, tile in enumerate(tiles):
                        op = v_.scalar_tensor_tensor(dst[:, kk, :], src[:, kk, tap:tap + T], tap_weight(tap, tile), dst[:, kk, :],
                                                     ALU.mult, ALU.add)
                    if tap < CONV - 1:
                        link(dve, op)
                op.then_inc(sem("g_conv"), 1)

            dve.wait_ge(sem("g_tap0"), 2 * hf + 1)
            conv(qk, qkp, qk_tiles(hf))
            bg("conv")
            dve.wait_ge(sem("g_tap0"), 2 * n)
            conv(vg, vp, v_tiles(hf))
            dve.wait_ge(sem("g_conv"), 2 * n)
            dve.wait_ge(sem("g_rooted"), n)
            bg("norms")
            v_.tensor_tensor(qk[:, :, :], qk[:, :, :], ri_g[:, :, :], ALU.mult).then_inc(sem("g_qk"), 1)
            dve.wait_ge(sem("g_eg"), n)
            for tt in range(TT):
                for cp in range(2):
                    r = slice(cp * C, (cp + 1) * C)
                    tok = slice(tt * P + cp * C, tt * P + (cp + 1) * C)
                    own = gc_n[r, tt, 4 * hf:4 * hf + 4].unsqueeze(2).to_broadcast([C, 4, C])
                    op = v_.tensor_tensor(dec[r, 4 * tt:4 * tt + 4, :], pa[r, :, tok], own, ALU.subtract)
            link(dve, op)
            v_.tensor_scalar(dec[:, :, :], dec[:, :, :], 0.0, None, ALU.min).then_inc(sem("g_diff"), 1)
            dve.wait_ge(sem("g_decexp"), n)
            v_.tensor_tensor(dec[:, :, :], dec[:, :, :], over_units(m_inc), ALU.mult).then_inc(sem("g_dec"), 1)
            dve.wait_ge(sem("g_qk"), n)
            for hl in range(4):
                v_.tensor_tensor(kb[:, hl, :], qk[:, 2 + hl // 2, :], bb[:, hl, :], ALU.mult)
                v_.tensor_tensor(qe[:, hl, :], qk[:, hl // 2, :], eg[:, hl, :], ALU.mult)
            bg("rows")
            dve.wait_ge(sem("g_naturals"), n)
            v_.tensor_copy(kn[:, :, :], bank[2])
            for tt in range(TT):
                own = be_n[:, tt, 4 * hf:4 * hf + 4].unsqueeze(2).to_broadcast([P, 4, GH])
                op = v_.tensor_tensor(vb[:, tt, :].rearrange("p (h d) -> p h d", h=4), heads4[tt], own, ALU.mult)
            op.then_inc(sem("g_kb"), 1)
            bg("naturals")
            dve.wait_ge(sem("g_mats"), n)
            dve.wait_ge(sem("g_dec"), n)
            v_.tensor_tensor(att[:, :, :], units[3], dec[:, :, :], ALU.mult)
            link(dve, v_.scalar_tensor_tensor(inv_g[1][:, :, :], units[2], -1.0, dec[:, :, :], ALU.mult, ALU.mult))
            v_.tensor_tensor(inv_g[5][:, :, :], inv_g[1][:, :, :], over_units(m_upo), ALU.mult)
            v_.tensor_tensor(inv_g[0][:, :, :], inv_g[1][:, :, :], over_units(m_upd), ALU.mult).then_inc(sem("inv_in"), 1)
            bg("mats")
            dve.wait_ge(sem("inv_in"), n)
            invert_dve(dve, hf, inv_g, ut_g[:, :, :])
            v_.memset(s_g[:, 0, :, :], 0.0).then_inc(sem("g_state"), 1)
            dve.wait_ge(sem("g_state"), (NCH + 1) * hf + 1)
            for c in range(NCH):
                tt, cp = c // 2, c % 2
                r = slice(cp * C, (cp + 1) * C)
                m = NCH * hf + c
                own = nbe_n[r, tt, 4 * hf:4 * hf + 4].unsqueeze(2).to_broadcast([C, 4, GH])
                dve.wait_ge(sem("g_ks"), m + 1)
                link(dve, v_.tensor_tensor(r_g[r, :, :], heads4[0][r, :, :], own, ALU.mult))
                v_.tensor_tensor(r_g[r, :, :], r_g[r, :, :], vb[r, tt, :].rearrange("p (h d) -> p h d", h=4), ALU.add).then_inc(sem("g_r"), 1)
                bg(f"ks{c}")
                dve.wait_ge(sem("g_vnew"), m + 1)
                v_.tensor_copy(vn_g[r, :, :], heads4[1][r, :, :])
                last = dec[r, 4 * tt:4 * tt + 4, C - 1:C].to_broadcast([C, 4, GH])
                v_.tensor_tensor(vs_g[r, :, :], heads4[1][r, :, :], last, ALU.mult).then_inc(sem("g_vn"), 1)
                bg(f"vnew{c}")
                dve.wait_ge(sem("g_ds"), m + 1)
                if c > 0:
                    dve.wait_ge(sem("g_omm"), m)
                for hl in range(4):
                    end = (c + 1) * C - 1
                    op = v_.scalar_tensor_tensor(s_g[:, (c + 1) % 2, hl, :], s_g[:, c % 2, hl, :], eg[:, hl, end:end + 1],
                                                 heads4[3][:, hl, :], ALU.mult, ALU.add)
                op.then_inc(sem("g_state"), 1)
                bg(f"state{c}")
                dve.wait_ge(sem("g_state"), (NCH + 1) * hf + c + 2)
            dve.wait_ge(sem("g_osq"), n)
            v_.tensor_reduce(msum[:, 0:8], so_g[:, :, :].rearrange("p a (h d) -> p (a h) d", d=GH), AX_X, ALU.add).then_inc(sem("g_oms"), 1)
            bg("out")
            dve.wait_ge(sem("g_oroot"), n)
            link(dve, v_.reciprocal(mroot2[:, 0:8], mroot[:, 0:8]))
            link(dve, v_.tensor_tensor(o_g[:, :, :].rearrange("p t (h d) -> p (t h) d", d=GH),
                                       o_g[:, :, :].rearrange("p t (h d) -> p (t h) d", d=GH),
                                       mroot2[:, 0:8].unsqueeze(2).to_broadcast([P, 8, GH]), ALU.mult))
            if hf == 0:
                dve.wait_ge(sem(g[2]["released"][0]), g[2]["released"][1])
            else:
                dve.wait_ge(sem("z_act"), 1)
            dve.wait_ge(sem("mix_turned"), 2 * n)
            v_.tensor_tensor(nat[:, :, :], o_g[:, :, :], zg[:, :, :], ALU.mult).then_inc(sem("g_out"), 1)
            dve.wait_ge(sem("g_out_turned"), n)
            if hf > 0:
                dve.wait_ge(sem("y_stored"), 16 * hf)
            v_.tensor_scalar(xf[:, :, :], pa[:, :, :], prm[:, PRM["gdn_norm"]:PRM["gdn_norm"] + 1], None, ALU.mult).then_inc(sem("y_ready"), 1)
            bg("y")
            dve.wait_ge(sem("y_ready"), n)

        def rw_pe(pe, hf):
            n = hf + 1
            m0 = 2 * HALVES + 3 * hf
            pe.wait_ge(sem("y_ready"), HALVES + hf)
            pe.wait_ge(sem("lora_loaded"), 64 * n)
            for dt in range(4):
                cols = slice(dt * P, (dt + 1) * P)
                nc.tensor.matmul(pa[:, dt, :], w2z[:, cols], lora[:, 0, :], start=True, stop=True)
                mm = nc.tensor.matmul(pb[:, dt, :], a2z[:, cols], lora[:, 0, :], start=True, stop=True)
            mm.then_inc(sem("r_lora"), 1)
            bg_pe(pe, f"rw{hf}.lora")
            pe.wait_ge(sem("r_sig"), n)
            for dt in range(4):
                cols = slice(dt * P, (dt + 1) * P)
                nc.tensor.matmul(pa[:, dt, :], g2a[:, cols], lora[:, 1, :], start=True, stop=False)
                mm = nc.tensor.matmul(pa[:, dt, :], g2b[0:32, cols], lora[0:32, 2, :], start=False, stop=True)
            mm.then_inc(sem("r_g"), 1)
            bg_pe(pe, f"rw{hf}.g")
            pe.wait_ge(sem("r_gt"), n)
            mix_turn(pe, m0, gs, (sem("gs_loaded"), 16 * (2 + 2 * hf)))
            bg_pe(pe, f"rw{hf}.r")
            mix_turn(pe, m0 + 1, nat, (sem("nat_loaded"), 16 * (2 + hf)))
            bg_pe(pe, f"rw{hf}.k")
            mix_turn(pe, m0 + 2, gs, (sem("gs_loaded"), 16 * (3 + 2 * hf)))
            for name in ("v", "shift"):
                bg_pe(pe, f"rw{hf}.{name}")
            pe.wait_ge(sem("r_kksq"), n)
            for dt in range(4):
                mm = nc.tensor.matmul(pb[:, dt, :], headones[:, :], gs_t[:, dt, :], start=True, stop=True)
            mm.then_inc(sem("r_kknorm"), 1)
            bg_pe(pe, f"rw{hf}.kk")
            pe.wait_ge(sem("r_rkk"), n)
            pe.wait_ge(sem("mix_take"), m0 + 3)
            for dt in range(4):
                mm = nc.tensor.matmul(pa[:, dt, :], headones[:, :], nat_t[:, dt, :], start=True, stop=True)
            mm.then_inc(sem("r_bonus"), 1)
            for name in ("tilde", "bonus"):
                bg_pe(pe, f"rw{hf}.{name}")
            pe.wait_ge(sem("r_rz"), n)
            pe.wait_ge(sem("r_tilde"), n)
            for k, (src, banks, need) in enumerate(((bt, bank[2:4], None), (kt, bank[0:2], "r_bonus_out"), (tmp[2], bank[2:4], "r_nat"))):
                if need is not None:
                    pe.wait_ge(sem(need), n if need == "r_bonus_out" else 3 * hf + 1)
                for tt in range(TT):
                    for dt in range(4):
                        mm = nc.tensor.transpose(banks[tt][:, dt // 2, (dt % 2) * P:(dt % 2 + 1) * P],
                                                 src[:, dt, tt * P:(tt + 1) * P], ident[:, :])
                mm.then_inc(sem("r_nat_turned"), 1)
            bg_pe(pe, f"rw{hf}.nat")
            for tt in range(TT):
                v = HALVES + TT * hf + tt
                if tt == 0:
                    pe.wait_ge(sem("r_nat"), 3 * n)
                else:
                    pe.wait_ge(sem("inv_dve"), INV_DVE * v)
                for u in range(8):
                    for cp in range(2):
                        r = slice(cp * C, (cp + 1) * C)
                        tok = slice(tt * P + cp * C, tt * P + (cp + 1) * C)
                        for k, (left, right) in enumerate(((bt, az), (bt, rz), (kt, az), (kt, rz))):
                            mm = nc.tensor.matmul(units[k][r, u, :], left[:, u // 2, tok], right[:, u // 2, u % 2, tok],
                                                  start=True, stop=True)
                mm.then_inc(sem("r_mats"), 1)
                bg_pe(pe, f"rw{hf}.mats{tt}")
                invert_pe(pe, v, inv_r)
            pe.wait_ge(sem("inv_dve"), INV_DVE * (HALVES + TT * n))
            for c in range(NCH):
                tt, cp = c // 2, c % 2
                r = slice(cp * C, (cp + 1) * C)
                tok = slice(c * C, (c + 1) * C)
                m = NCH * hf + c
                s_in = s_r[:, c % 2, :, :]
                pe.wait_ge(sem("r_state"), m + hf + 1)
                for u in range(8):
                    nc.tensor.matmul(units[0][r, u, :], az[:, u // 2, u % 2, tok], s_in[:, u // 2, :], start=True, stop=False)
                    mm = nc.tensor.matmul(units[0][r, u, :], ak[r, tt, u, :], vn_r[r, tt, u * C:(u + 1) * C], start=False, stop=True)
                mm.then_inc(sem("r_rmm"), 1)
                bg_pe(pe, f"rw{hf}.r{c}")
                pe.wait_ge(sem("r_r"), m + 1)
                for u in range(8):
                    mm = nc.tensor.matmul(units[1][r, u, :], ut_r[r, tt, u, :], r_r[r, u, :], start=True, stop=True)
                mm.then_inc(sem("r_samm"), 1)
                bg_pe(pe, f"rw{hf}.sa{c}")
                pe.wait_ge(sem("r_sa"), m + 1)
                for u in range(8):
                    out = heads_state[(u % 2) * C:(u % 2 + 1) * C, u // 2, :]
                    cols = slice(u * C, (u + 1) * C)
                    nc.tensor.matmul(out, bn[r, tt, cols], sa_r[r, u, :], start=True, stop=False)
                    mm = nc.tensor.matmul(out, kn_r[r, tt, cols], vn_r[r, tt, cols], start=False, stop=True)
                mm.then_inc(sem("r_ds"), 1)
                if m > 0:
                    pe.wait_ge(sem("r_y"), m)
                for u in range(8):
                    cols = slice(u * C, (u + 1) * C)
                    nc.tensor.matmul(units[2][r, u, :], rz[:, u // 2, u % 2, tok], s_in[:, u // 2, :], start=True, stop=False)
                    nc.tensor.matmul(units[2][r, u, :], rb[r, tt, u, :], sa_r[r, u, :], start=False, stop=False)
                    mm = nc.tensor.matmul(units[2][r, u, :], rk[r, tt, u, :], vn_r[r, tt, cols], start=False, stop=True)
                mm.then_inc(sem("r_ymm"), 1)
                bg_pe(pe, f"rw{hf}.y{c}")
            bg_pe(pe, f"rw{hf}.out")
            pe.wait_ge(sem("r_out"), n)
            for kk in range(4):
                for tt in range(TT):
                    mm = nc.tensor.transpose(pa[:, kk, tt * P:(tt + 1) * P], nat[:, tt, kk * P:(kk + 1) * P], ident[:, :])
            mm.then_inc(sem("r_out_turned"), 1)
            bg_pe(pe, f"rw{hf}.y")
            if hf > 0:
                bg_pe(pe, "rest")

        def rw_act(act, hf):
            n = hf + 1
            m0 = 2 * HALVES + 3 * hf

            def col(name, dt):
                k = PRM[name] + 4 * hf + dt
                return prm[:, k:k + 1]

            def bg(name):
                bg_act(act, f"rw{hf}.{name}", spool_r)

            act.wait_ge(sem("r_lora"), n)
            for dt in range(4):
                b = 4 * hf + dt
                nc.scalar.activation(tmp[3][:, dt, :], pa[:, dt, :], ACT.Sigmoid, bias=prm[:, PRM["w0"] + b:PRM["w0"] + b + 1])
            for dt in range(4):
                b = 4 * hf + dt
                op = nc.scalar.activation(tmp[4][:, dt, :], pb[:, dt, :], ACT.Sigmoid, bias=prm[:, PRM["a0"] + b:PRM["a0"] + b + 1])
            op.then_inc(sem("r_sig"), 1)
            act.wait_ge(sem("r_sig"), n)
            nc.scalar.activation(tmp[3][:, :, :], tmp[3][:, :, :], ACT.Copy, scale=-EXP_HALF).then_inc(sem("r_logdecay"), 1)
            bg("lora")
            act.wait_ge(sem("r_g"), n)
            copy(act, gt[:, :, :], pa[:, :, :]).then_inc(sem("r_gt"), 1)
            bg("g")
            act.wait_ge(sem("pads_clear"), HALVES + n)
            for m in range(3):
                mix_take(act, rkv[m][:, :, 1:T + 1], m0 + m)
                for dt in range(4):
                    k = 8 * m + 4 * hf + dt
                    op = nc.scalar.activation(tmp[m][:, dt, :], rkv[m][:, dt, 1:T + 1], ACT.Copy, scale=omu[:, k:k + 1])
                op.then_inc(sem("r_scaled"), 1)
                bg("rkv"[m])
            bg("shift")
            act.wait_ge(sem("r_shifted"), 3 * hf + 2)
            for dt in range(4):
                op = nc.scalar.activation(gs_t[:, dt, :], tmp[1][:, dt, :], ACT.Square, scale=col("k_k", dt))
            op.then_inc(sem("r_kksq"), 1)
            act.wait_ge(sem("y_stored"), 16 * (HALVES + hf))
            for dt in range(4):
                op = nc.scalar.activation(xf[:, dt, :], tmp[1][:, dt, :], ACT.Copy, scale=col("k_k", dt))
            op.then_inc(sem("r_kk0"), 1)
            act.wait_ge(sem("r_cum"), n)
            nc.scalar.activation(tmp[6][:, :, :], tmp[5][:, :, :], ACT.Exp)
            nc.scalar.activation(tmp[7][:, :, :], tmp[5][:, :, :], ACT.Exp, scale=-1.0).then_inc(sem("r_exp"), 1)
            bg("kk")
            act.wait_ge(sem("r_kknorm"), n)
            link(act, nc.scalar.activation(gs_t[:, :, :], pb[:, :, :], ACT.Ln, bias=eps_k))
            nc.scalar.activation(gs_t[:, :, :], gs_t[:, :, :], ACT.Exp, scale=-0.5).then_inc(sem("r_kkroot"), 1)
            act.wait_ge(sem("r_cumx"), n)
            nc.scalar.activation(tmp[5][:, :, :], tmp[5][:, :, :], ACT.Exp).then_inc(sem("r_expx"), 1)
            bg("tilde")
            act.wait_ge(sem("r_rt"), n)
            for e in range(2):
                half = slice(e * C, (e + 1) * C)
                op = copy(act, rz[half, :, e, :], tmp[0][half, :, :])
            op.then_inc(sem("r_rz"), 1)
            for name in ("tilde", "bonus", "nat"):
                bg(name)
            for tt in range(TT):
                bg(f"mats{tt}")
                invert_act(act, HALVES + TT * hf + tt, inv_r, spool_r)
            for c in range(NCH):
                tt, cp = c // 2, c % 2
                r = slice(cp * C, (cp + 1) * C)
                m = NCH * hf + c
                act.wait_ge(sem("r_rmm"), m + 1)
                copy(act, r_r[r, :, :], units[0][r, :, :]).then_inc(sem("r_r"), 1)
                bg(f"r{c}")
                act.wait_ge(sem("r_samm"), m + 1)
                copy(act, sa_r[r, :, :], units[1][r, :, :]).then_inc(sem("r_sa"), 1)
                bg(f"sa{c}")
                act.wait_ge(sem("r_ymm"), m + 1)
                copy(act, y_r[r, tt, :], units[2][r, :, :].rearrange("p u c -> p (u c)")).then_inc(sem("r_y"), 1)
                bg(f"y{c}")
            act.wait_ge(sem("r_cent"), n)
            nc.scalar.activation(gs[:, :, :], y_r[:, :, :], ACT.Square).then_inc(sem("r_centsq"), 1)
            bg("out")
            act.wait_ge(sem("r_var"), n)
            nc.scalar.activation(mroot[:, :], msum[:, :], ACT.Sqrt, bias=eps_gn, scale=1.0 / RH).then_inc(sem("r_std"), 1)
            bg("y")
            if hf > 0:
                bg_act(act, "rest", spool_r)
                for j in (0, 1):
                    split_hi(act, prods["lift"][0]["slot"], j)
                for k, tiles in enumerate((slice(8, 16), slice(0, 4))):
                    act.wait_ge(sem(("deltanet_loaded", "rwkv_loaded")[k]), 16)
                    copy(act, yhi[:, tiles, :], yf[:, tiles, :]).then_inc(sem("y_hi"), 1)
                for j in (2, 3):
                    split_hi(act, prods["lift"][0]["slot"], j)
                spool_out(act, len(BG) - 1, spool_r)

        def rw_dve(dve, hf):
            n = hf + 1
            m0 = 2 * HALVES + 3 * hf
            v_ = nc.vector

            def col(name, dt):
                k = PRM[name] + 4 * hf + dt
                return prm[:, k:k + 1]

            for m in range(3):
                op = v_.memset(rkv[m][:, :, 0:1], 0.0)
            op.then_inc(sem("pads_clear"), 1)

            def bg(name):
                bg_dve(dve, f"rw{hf}.{name}")

            if hf == 0:
                dve.wait_ge(sem("spooled"), 16 * spooled_before)
            bg("lora")
            bg("g")
            for m in range(3):
                dve.wait_ge(sem("r_scaled"), 3 * hf + m + 1)
                bg("rkv"[m])
                for dt in range(4):
                    k = PRM["mu_rkv"] + 8 * m + 4 * hf + dt
                    op = v_.scalar_tensor_tensor(tmp[m][:, dt, :], rkv[m][:, dt, 0:T], prm[:, k:k + 1], tmp[m][:, dt, :],
                                                 ALU.mult, ALU.add)
                op.then_inc(sem("r_shifted"), 1)
                dve.wait_ge(sem("r_shifted"), 3 * hf + m + 1)
            r_, k_, v__, sg, a_, cum, ecum, encum = tmp
            bg("shift")
            dve.wait_ge(sem("r_logdecay"), n)
            for dt in range(4):
                op = v_.tensor_tensor_scan(cum[:, dt, :], scanmask[:, :], sg[:, dt, :], 0.0, ALU.mult, ALU.add)
            op.then_inc(sem("r_cum"), 1)
            bg("kk")
            for dt in range(4):
                op = v_.tensor_scalar(nat_t[:, dt, :], a_[:, dt, :], 1.0, col("k_a", dt), ALU.subtract, ALU.mult)
            link(dve, op)
            dve.wait_ge(sem("r_kk0"), n)
            link(dve, v_.scalar_tensor_tensor(k_[:, :, :], nat_t[:, :, :], 1.0, k_[:, :, :], ALU.add, ALU.mult))
            for dt in range(4):
                op = v_.scalar_tensor_tensor(nat_t[:, dt, :], r_[:, dt, :], col("r_k", dt), k_[:, dt, :], ALU.mult, ALU.mult)
            op.then_inc(sem("r_rkk"), 1)
            dve.wait_ge(sem("r_exp"), n)
            v_.tensor_tensor(cum[:, :, :], cum[:, :, :], sg[:, :, :], ALU.subtract).then_inc(sem("r_cumx"), 1)
            dve.wait_ge(sem("r_cumx"), n)
            bg("tilde")
            dve.wait_ge(sem("rw_clear"), 1)
            dve.wait_ge(sem("r_rkk"), n)
            v_.tensor_copy(pc, ecum[:, :, :].rearrange("p d (c t) -> p d c t", t=C)[:, :, :, C - 1])
            v_.tensor_tensor(kt[:, :, :], k_[:, :, :], encum[:, :, :], ALU.mult)
            v_.tensor_tensor(r_[:, :, :], r_[:, :, :], ecum[:, :, :], ALU.mult).then_inc(sem("r_rt"), 1)
            dve.wait_ge(sem("r_kkroot"), n)
            link(dve, v_.tensor_tensor(xf[:, :, :], xf[:, :, :], gs_t[:, :, :], ALU.mult))
            link(dve, v_.tensor_tensor(gs_t[:, :, :], xf[:, :, :], a_[:, :, :], ALU.mult))
            v_.tensor_tensor(bt[:, :, :], gs_t[:, :, :], encum[:, :, :], ALU.mult)
            dve.wait_ge(sem("r_expx"), n)
            for e in range(2):
                half = slice(e * C, (e + 1) * C)
                op = v_.scalar_tensor_tensor(az[half, :, e, :], xf[half, :, :], -1.0, cum[half, :, :], ALU.mult, ALU.mult)
            op.then_inc(sem("r_tilde"), 1)
            dve.wait_ge(sem("r_bonus"), n)
            v_.tensor_tensor(bonus[:, :, :], pa[:, :, :], v__[:, :, :], ALU.mult).then_inc(sem("r_bonus_out"), 1)
            bg("bonus")
            dve.wait_ge(sem("r_tilde"), n)
            for k, (dst, lo, hi) in enumerate(((bn, 2, 4), (kn_r, 0, 2), (vn_r, 2, 4))):
                dve.wait_ge(sem("r_nat_turned"), 3 * hf + k + 1)
                src = (pa, pb)[lo // 2][:, :, :].rearrange("p a t -> p (a t)")
                v_.tensor_copy(dst[:, :, :].rearrange("p t d -> p (t d)"), src).then_inc(sem("r_nat"), 1)
            bg("nat")
            for tt in range(TT):
                v = HALVES + TT * hf + tt
                dve.wait_ge(sem("r_mats"), TT * hf + tt + 1)
                for dst, k, mask in ((inv_r[5][:, :, :], 0, m_upo), (rb[:, tt, :, :], 1, m_inc), (ak[:, tt, :, :], 2, m_up),
                                     (rk[:, tt, :, :], 3, m_inc)):
                    v_.tensor_tensor(dst, units[k], over_units(mask), ALU.mult)
                v_.tensor_tensor(inv_r[0][:, :, :], units[0], over_units(m_upd), ALU.mult).then_inc(sem("inv_in"), 1)
                bg(f"mats{tt}")
                dve.wait_ge(sem("inv_in"), v + 1)
                invert_dve(dve, v, inv_r, ut_r[:, tt, :, :])
            v_.memset(s_r[:, 0, :, :], 0.0).then_inc(sem("r_state"), 1)
            dve.wait_ge(sem("r_state"), (NCH + 1) * hf + 1)
            for c in range(NCH):
                m = NCH * hf + c
                bg(f"sa{c}")
                dve.wait_ge(sem("r_ds"), m + 1)
                if m > 0 and c > 0:
                    dve.wait_ge(sem("r_ymm"), m)
                s_in, s_out = s_r[:, c % 2, :, :], s_r[:, (c + 1) % 2, :, :]
                link(dve, v_.tensor_tensor(s_out, s_in, heads_state, ALU.add))
                v_.tensor_tensor(s_out, s_out, pc[:, :, c:c + 1].to_broadcast([P, 4, C]), ALU.mult).then_inc(sem("r_state"), 1)
                bg(f"y{c}")
                dve.wait_ge(sem("r_state"), m + hf + 2)
            dve.wait_ge(sem("r_y"), NCH * n)
            yv = y_r[:, :, :].rearrange("p t (h c) -> p (t h) c", c=RH)
            link(dve, v_.tensor_reduce(msum2[:, :], yv, AX_X, ALU.add))
            link(dve, v_.tensor_scalar(mroot2[:, :], msum2[:, :], 1.0 / RH, None, ALU.mult))
            v_.tensor_tensor(yv, yv, mroot2[:, :].unsqueeze(2).to_broadcast([P, 16, RH]), ALU.subtract).then_inc(sem("r_cent"), 1)
            bg("out")
            dve.wait_ge(sem("r_centsq"), n)
            v_.tensor_reduce(msum[:, :], gs[:, :, :].rearrange("p t (h c) -> p (t h) c", c=RH), AX_X, ALU.add).then_inc(sem("r_var"), 1)
            dve.wait_ge(sem("r_std"), n)
            link(dve, v_.reciprocal(msum2[:, :], mroot[:, :]))
            v_.tensor_tensor(nat[:, :, :].rearrange("p t (h c) -> p (t h) c", c=RH), yv,
                             msum2[:, :].unsqueeze(2).to_broadcast([P, 16, RH]), ALU.mult).then_inc(sem("r_out"), 1)
            bg("y")
            if hf > 0:
                bg_dve(dve, "rest")
                for j in (0, 1):
                    split_lo(dve, prods["lift"][0]["slot"], j)
                y_lo(dve, 1, yf[:, 8:16, :], slice(8, 16))
            dve.wait_ge(sem("r_out_turned"), n)
            for dt in range(4):
                op = v_.tensor_scalar(xf[:, dt, :], pa[:, dt, :], col("ln_w", dt), col("ln_b", dt), ALU.mult, ALU.add)
            link(dve, op)
            link(dve, v_.tensor_tensor(xf[:, :, :], xf[:, :, :], bonus[:, :, :], ALU.add))
            v_.tensor_tensor(xf[:, :, :], xf[:, :, :], gt[:, :, :], ALU.mult).then_inc(sem("y_ready"), 1)
            dve.wait_ge(sem("y_ready"), HALVES + n)
            if hf > 0:
                for j in (2, 3):
                    split_lo(dve, prods["lift"][0]["slot"], j)

        gs_t = gs[:, :, :].rearrange("p a (b t) -> p (a b) t", t=T)
        nat_t = nat[:, :, :].rearrange("p a (b t) -> p (a b) t", t=T)
        heads_state = bank[3].rearrange("p a (u c) -> p (a u) c", c=C)[:, 0:4, :]

        def lift_pe(pe):
            L = prods["lift"]
            t0, s0 = turns["merged"]
            pe.wait_ge(sem("y_split"), 1)
            for c in range(NDC):
                multiply(pe, L[2 * c], L[2 * c]["free"], (yhi, ylo), k0=8)
                if c > 0:
                    turn(pe, t0 + c - 1)
                if c == 0:
                    pe.wait_ge(sem("y_split"), 3)
                multiply(pe, L[2 * c + 1], L[2 * c + 1]["free"], (yhi, ylo))
            pe.wait_ge(x_ready, s0 + 2)

        def gates_act(act, c):
            act.wait_ge(sem("ga_loaded"), 16 * (c + 1))
            nc.scalar.activation(ga[:, :, :], ga[:, :, :], ACT.Sigmoid)
            act.wait_ge(sem("gb_loaded"), 16 * (c + 1))
            nc.scalar.activation(gb[:, :, :], gb[:, :, :], ACT.Sigmoid).then_inc(sem("gates_ready"), 1)

        def lift_act(act):
            L = prods["lift"]
            t0, s0 = turns["merged"]
            act.wait_ge(sem("y_ready"), 2 * HALVES)
            copy(act, yhi[:, 4:8, :], xf[:, :, :]).then_inc(sem("y_hi"), 1)
            for c in range(NDC):
                la, lb = L[2 * c:2 * c + 2]
                for j in range(RING if c == 0 else 0, la["ns"]):
                    split_hi(act, la["slot"], j)
                if c == 0:
                    gates_act(act, 0)
                for j in range(lb["ns"]):
                    split_hi(act, lb["slot"], j)
                if c > 0:
                    x_hi(act, t0 + c - 1, mhi[:, 4 * c - 4:4 * c, :])
                    gates_act(act, c)
                    if c == 1:
                        act.wait_ge(sem("mem_loaded"), 16 * TT)
                        sumsq(act, msb, 2, 0)
                    sumsq(act, msb, 2, c)
            for j in range(6):
                split_hi(act, prods["out"][0]["slot"], j)
            x_hi(act, t0 + NDC - 1, mhi[:, 12:16, :])

        def y_lo(dve, n, src, tiles):
            dve.wait_ge(sem("y_hi"), n)
            nc.vector.tensor_tensor(ylo[:, tiles, :], src, yhi[:, tiles, :].bitcast(F32), ALU.subtract).then_inc(sem("y_split"), 1)

        def lift_dve(dve):
            L = prods["lift"]
            t0, s0 = turns["merged"]
            v_ = nc.vector

            def branch(c, m, gate):
                pr = L[2 * c + m]
                dve.wait_ge(slot_used, pr["done"])
                dve.wait_ge(sem("gates_ready"), c + 1)
                v_.tensor_tensor(gate[:, :, :], gate[:, :, :], pair(pr["par"]), ALU.mult).then_inc(sem(pr["released"][0]), 1)
                dve.wait_ge(sem(pr["released"][0]), pr["released"][1])

            def merge(c):
                if c > 0:
                    dve.wait_ge(turned, t0 + c)
                else:
                    dve.wait_ge(sem("r_out_turned"), HALVES)
                v_.tensor_tensor(nat[:, :, :], ga[:, :, :], gb[:, :, :], ALU.add).then_inc(nat_ready, 1)

            y_lo(dve, 2, yf[:, 0:4, :], slice(0, 4))
            y_lo(dve, 3, xf[:, :, :], slice(4, 8))
            dve.wait_ge(sem("y_split"), 3)
            for c in range(NDC):
                la, lb = L[2 * c:2 * c + 2]
                for j in range(RING if c == 0 else 0, la["ns"]):
                    split_lo(dve, la["slot"], j)
                if c > 0:
                    branch(c - 1, 1, ga)
                    merge(c - 1)
                for j in range(lb["ns"]):
                    split_lo(dve, lb["slot"], j)
                if c > 0:
                    take(dve, t0 + c - 1, s0 + c - 1)
                branch(c, 0, gb)
                if c > 0:
                    x_lo(dve, s0 + c - 1, mhi[:, 4 * c - 4:4 * c, :], mlo[:, 4 * c - 4:4 * c, :])
            for j in range(RING):
                split_lo(dve, prods["out"][0]["slot"], j)
            branch(NDC - 1, 1, ga)
            merge(NDC - 1)
            for j in (4, 5):
                split_lo(dve, prods["out"][0]["slot"], j)
            take(dve, t0 + NDC - 1, s0 + NDC - 1)
            x_lo(dve, s0 + NDC - 1, mhi[:, 12:16, :], mlo[:, 12:16, :])

        def out_pair(e):
            return pair((prods["mo"][0]["par"] + MH - e) % 2)

        def attn_pe(pe):
            O, KV, Q, MO = prods["out"], prods["mkv"], prods["mq"], prods["mo"]
            tm, tk, tq, th = (turns[k][0] for k in ("memnorm", "mk", "qnorm", "mq"))
            tg, sg = turns["merged"]

            def chunks(s, *which):
                return tuple((2 * c, lambda c=c: pe.wait_ge(x_ready, s + c + 1)) for c in which)

            for c in range(NDC):
                late = ((RING, lambda: turn(pe, tg + NDC - 1)),) + chunks(sg, 2, 3) if c == 0 else ()
                multiply(pe, O[c], O[c]["free"], (mhi, mlo), ahead_of=late)
                turn(pe, tm + c)
            for c in range(2 * NDC):
                late = chunks(turns["memnorm"][1], 0, 1, 2, 3) if c == 0 else ()
                multiply(pe, KV[c], KV[c]["free"], (xhi, xlo), ahead_of=late)
                if 1 <= c <= NDC:
                    turn(pe, tk + c - 1)
                if c > NDC:
                    turn(pe, tq + c - NDC - 1)
            for c in range(NDC):
                late = ((2, lambda: turn(pe, tq + NDC - 1)),) + chunks(turns["qnorm"][1], 0, 1, 2, 3) if c == 0 else ()
                multiply(pe, Q[c], Q[c]["free"], (qhi, qlo), ahead_of=late)
                if c > 0:
                    turn(pe, th + c - 1)
            turn(pe, th + NDC - 1)
            pe.wait_ge(xf_ready, th + NDC)
            pe.wait_ge(sem(Q[NDC - 1]["released"][0]), Q[NDC - 1]["released"][1])
            for g in range(MH + 1):
                if g < MH:
                    if g >= 2:
                        pe.wait_ge(sem("p_exp"), g - 1)
                    sc = bank[2 + g % 2]
                    for tt in range(TT):
                        for kk in range(MHK):
                            mm = nc.tensor.matmul(sc[:, tt, :], qt[:, MHK * g + kk, tt * P:(tt + 1) * P], kt_m[:, MHK * g + kk, :],
                                                  start=(kk == 0), stop=(kk == MHK - 1))
                    mm.then_inc(sem("p_scores"), 1)
                if g > 0:
                    e = g - 1
                    if e < MH - 1:
                        pe.wait_ge(sem("p_norm"), e + 1)
                    if e == MH - 1:
                        pe.wait_ge(sem("o_take"), MH - 1)
                        pe.wait_ge(sem("o_ready"), MH - 2)
                        for j in range(RING):
                            multiply_slot(pe, MO[0], j, (xhi, xlo))
                        pe.wait_ge(sem("p_norm"), e + 1)
                    for mt in range(TT):
                        for tt in range(TT):
                            mm = nc.tensor.transpose(bank[e % 2][:, mt, tt * P:(tt + 1) * P], pr_m[:, e % 2, tt, mt * P:(mt + 1) * P],
                                                     ident[:, :])
                    mm.then_inc(sem("p_turned"), 1)
                    pe.wait_ge(sem("p_t"), e + 1)
                    if e >= 2:
                        pe.wait_ge(sem("o_take"), e - 1)
                    out = out_pair(e).rearrange("p a (b t) -> p (a b) t", t=T)
                    for kk in range(MHK):
                        for mt in range(TT):
                            mm = nc.tensor.matmul(out[:, kk, :], v_m[:, mt, e * MHD + kk * P:e * MHD + (kk + 1) * P],
                                                  pt_m[:, e % 2, mt, :], start=(mt == 0), stop=(mt == TT - 1))
                    mm.then_inc(sem("o_mm"), 1)
            for j in range(RING, KT // SK):
                if j % 2 == 0:
                    pe.wait_ge(sem("o_ready"), j // 2 + 1)
                multiply_slot(pe, MO[0], j, (xhi, xlo))
            for c in range(1, NDC):
                multiply(pe, MO[c], MO[c]["free"], (xhi, xlo))

        def attn_act(act):
            O, KV, Q, MO = prods["out"], prods["mkv"], prods["mq"], prods["mo"]
            tm, tk, tq, th = (turns[k][0] for k in ("memnorm", "mk", "qnorm", "mq"))
            split_hi(act, O[0]["slot"], 6)
            split_hi(act, O[0]["slot"], 7)
            norm_root(act, 2)
            for c in range(NDC):
                for j in range(KT // SK if c == 0 else 0, KT // SK):
                    split_hi(act, O[c]["slot"], j)
                    if c > 0 and j == 5:
                        act.wait_ge(sem(O[c - 1]["released"][0]), O[c - 1]["released"][1])
                        sumsq(act, h, 3, c - 1)
                        x_hi(act, tm + c - 1, xhi[:, 4 * c - 4:4 * c, :])
            for j in range(RING):
                split_hi(act, KV[0]["slot"], j)
            act.wait_ge(sem(O[3]["released"][0]), O[3]["released"][1])
            sumsq(act, h, 3, 3)
            x_hi(act, tm + 3, xhi[:, 12:16, :])
            for c in range(2 * NDC):
                for j in range(RING if c == 0 else 0, KT // SK):
                    split_hi(act, KV[c]["slot"], j)
                    if c == NDC and j == 5:
                        norm_root(act, 3)
                if c > NDC + 1:
                    x_hi(act, tq + c - NDC - 2, qhi[:, 4 * (c - NDC - 2):4 * (c - NDC - 1), :])
            for j in range(RING):
                split_hi(act, Q[0]["slot"], j)
            x_hi(act, tq + 2, qhi[:, 8:12, :])
            for j in range(RING, EARLY):
                split_hi(act, Q[0]["slot"], j)
            x_hi(act, tq + 3, qhi[:, 12:16, :])
            for c in range(NDC):
                for j in range(EARLY if c == 0 else 0, KT // SK):
                    split_hi(act, Q[c]["slot"], j)
            for j in range(RING):
                split_hi(act, MO[0]["slot"], j)
            for g in range(MH + 1):
                if g < MH:
                    act.wait_ge(sem("p_max"), g + 1)
                    for tt in range(TT):
                        op = nc.scalar.activation(pr_m[:, g % 2, tt, :], bank[2 + g % 2][:, tt, :], ACT.Exp, bias=nmx[:, g, tt:tt + 1],
                                                  scale=MHD ** -0.5, accum_out=den[:, g, tt:tt + 1])
                    op.then_inc(sem("p_exp"), 1)
                if g == MH:
                    for j in range(RING, EARLY):
                        split_hi(act, MO[0]["slot"], j)
                if g > 0:
                    act.wait_ge(sem("o_take"), g)
                    e = g - 1
                    copy(act, xhi[:, MHK * e:MHK * (e + 1), :], xf[:, :, :]).then_inc(sem("o_hi"), 1)
            for c in range(NDC):
                for j in range(EARLY if c == 0 else 0, KT // SK):
                    split_hi(act, MO[c]["slot"], j)
                    if c > 0 and j == 5:
                        act.wait_ge(sem(MO[c - 1]["released"][0]), MO[c - 1]["released"][1])
                        sumsq(act, h, 4, c - 1)

        def attn_dve(dve):
            O, KV, Q, MO = prods["out"], prods["mkv"], prods["mq"], prods["mo"]
            (tm, sm), (tk, _), (tq, sq), (th, _) = (turns[k] for k in ("memnorm", "mk", "qnorm", "mq"))
            v_ = nc.vector
            split_lo(dve, O[0]["slot"], 6)
            split_lo(dve, O[0]["slot"], 7)
            norm_scale(dve, 2)
            norm_chunk(dve, msb, 0, tm)
            for c in range(NDC):
                for j in range(KT // SK if c == 0 else 0, KT // SK):
                    split_lo(dve, O[c]["slot"], j)
                    if c > 0 and j == 4:
                        residual(dve, O[c - 1], c - 1, 1.0)
                        take(dve, tm + c - 1, sm + c - 1, PRM["mem_kv_norm"] + 4 * (c - 1))
                        norm_chunk(dve, msb, c, tm + c)
                    if c > 0 and j == 7:
                        x_lo(dve, sm + c - 1, xhi[:, 4 * c - 4:4 * c, :], xlo[:, 4 * c - 4:4 * c, :])
            for j in range(RING):
                split_lo(dve, KV[0]["slot"], j)
            residual(dve, O[3], 3, 1.0)
            take(dve, tm + 3, sm + 3, PRM["mem_kv_norm"] + 12)
            x_lo(dve, sm + 3, xhi[:, 12:16, :], xlo[:, 12:16, :])

            def k_nat(c):
                dve.wait_ge(slot_used, KV[c]["done"])
                dve.wait_ge(turned, tk + c)
                v_.tensor_copy(nat[:, :, :], pair(KV[c]["par"])).then_inc(nat_ready, 1)
                dve.wait_ge(nat_ready, tk + c + 1)
                dve.sem_inc(sem(KV[c]["released"][0]), 1)

            def plain(dst, t):
                dve.wait_ge(turned, t + 1)
                v_.tensor_copy(dst, pa[:, :, :]).then_inc(xf_ready, 1)

            def v_nat(c):
                dve.wait_ge(slot_used, KV[NDC + c]["done"])
                v_.tensor_copy(v_m[:, :, c * CW:(c + 1) * CW], pair(KV[NDC + c]["par"])).then_inc(sem(KV[NDC + c]["released"][0]), 1)

            for c in range(2 * NDC):
                for j in range(RING if c == 0 else 0, KT // SK):
                    split_lo(dve, KV[c]["slot"], j)
                    if j == 4 and 1 <= c <= NDC:
                        k_nat(c - 1)
                    if j == 4 and c > NDC:
                        v_nat(c - 1 - NDC)
                    if j == 1 and 2 <= c <= NDC + 1:
                        plain(kt_m[:, MHK * (c - 2):MHK * (c - 1), :], tk + c - 2)
                    if j == 5 and c == NDC:
                        norm_scale(dve, 3)
                    if j == 5 and c > NDC:
                        norm_chunk(dve, h, c - NDC - 1, tq + c - NDC - 1)
                    if j == 1 and c > NDC + 1:
                        take(dve, tq + c - NDC - 2, sq + c - NDC - 2, PRM["mem_q_norm"] + 4 * (c - NDC - 2))
                if c > NDC + 1:
                    e = c - NDC - 2
                    x_lo(dve, sq + e, qhi[:, 4 * e:4 * e + 4, :], qlo[:, 4 * e:4 * e + 4, :])
            for j in range(RING):
                split_lo(dve, Q[0]["slot"], j)
            v_nat(NDC - 1)
            take(dve, tq + 2, sq + 2, PRM["mem_q_norm"] + 8)
            norm_chunk(dve, h, 3, tq + 3)
            x_lo(dve, sq + 2, qhi[:, 8:12, :], qlo[:, 8:12, :])
            for j in range(RING, EARLY):
                split_lo(dve, Q[0]["slot"], j)
            take(dve, tq + 3, sq + 3, PRM["mem_q_norm"] + 12)
            x_lo(dve, sq + 3, qhi[:, 12:16, :], qlo[:, 12:16, :])

            def q_nat(c):
                dve.wait_ge(slot_used, Q[c]["done"])
                dve.wait_ge(turned, th + c)
                v_.tensor_copy(nat[:, :, :], pair(Q[c]["par"])).then_inc(nat_ready, 1)
                dve.wait_ge(nat_ready, th + c + 1)
                dve.sem_inc(sem(Q[c]["released"][0]), 1)

            for c in range(NDC):
                for j in range(EARLY if c == 0 else 0, KT // SK):
                    split_lo(dve, Q[c]["slot"], j)
                    if j == 4 and c > 0:
                        q_nat(c - 1)
                    if j == 1 and c > 1:
                        plain(qt[:, MHK * (c - 2):MHK * (c - 1), :], th + c - 2)
            for j in range(RING):
                split_lo(dve, MO[0]["slot"], j)
            plain(qt[:, 8:12, :], th + 2)
            q_nat(3)
            plain(qt[:, 12:16, :], th + 3)
            def turned_probabilities(g):
                dve.wait_ge(sem("p_turned"), g + 1)
                v_.tensor_copy(pt_m[:, g % 2, :, :], bank[g % 2]).then_inc(sem("p_t"), 1)

            def head_output(e):
                dve.wait_ge(sem("o_mm"), e + 1)
                if e > 0:
                    dve.wait_ge(sem("o_hi"), e)
                    dve.wait_ge(sem("o_ready"), e)
                v_.tensor_copy(xf[:, :, :], out_pair(e).rearrange("p a (b t) -> p (a b) t", t=T)).then_inc(sem("o_take"), 1)
                dve.wait_ge(sem("o_hi"), e + 1)
                v_.tensor_tensor(xlo[:, MHK * e:MHK * (e + 1), :], xf[:, :, :], xhi[:, MHK * e:MHK * (e + 1), :].bitcast(F32),
                                 ALU.subtract).then_inc(sem("o_ready"), 1)

            for g in range(MH + 1):
                if g < MH:
                    dve.wait_ge(sem("p_scores"), g + 1)
                    link(dve, v_.tensor_reduce(mx[:, g, :], bank[2 + g % 2], AX_X, ALU.max))
                    v_.tensor_scalar(nmx[:, g, :], mx[:, g, :], -MHD ** -0.5, None, ALU.mult).then_inc(sem("p_max"), 1)
                    dve.wait_ge(sem("p_exp"), g + 1)
                    link(dve, v_.reciprocal(rden[:, g, :], den[:, g, :]))
                    for tt in range(TT):
                        op = v_.tensor_scalar(pr_m[:, g % 2, tt, :], pr_m[:, g % 2, tt, :], rden[:, g, tt:tt + 1], None, ALU.mult)
                    op.then_inc(sem("p_norm"), 1)
                    if g < MH - 1:
                        turned_probabilities(g)
                if g == MH:
                    for j in range(RING, EARLY):
                        split_lo(dve, MO[0]["slot"], j)
                if g > 0:
                    head_output(g - 1)
                if g == MH - 1:
                    turned_probabilities(g)
            for c in range(NDC):
                for j in range(EARLY if c == 0 else 0, KT // SK):
                    split_lo(dve, MO[c]["slot"], j)
                    if c > 0 and j == 4:
                        residual(dve, MO[c - 1], c - 1, 1.0)

        fgain = at("fgain", 64, [D])

        def next_hi(act, phase):
            for j in range(RING):
                split_hi(act, prods[phase][0]["slot"], j)

        def next_lo(dve, phase):
            for j in range(RING):
                split_lo(dve, prods[phase][0]["slot"], j)

        def store_y(sp, tile, n):
            sp.wait_ge(sem("y_ready"), n)
            sp.dma_start(y_turned[tile:tile + 4].rearrange("k p t -> p k t"), xf[:, :, :]).then_inc(sem("y_stored"), 16)

        def last_sumsq(act, pr, q):
            act.wait_ge(sem(pr["released"][0]), pr["released"][1])
            sumsq(act, h, q, NDC - 1)

        block = ctx.enter_context(nc.Block())

        @block.gpsimd
        def _(pool):
            g = nc.gpsimd
            g.memset(nat[:, :, :], 0.0).then_inc(prm_clear, 1)
            pool.wait_ge(prm_clear, 1)
            link(pool, g.memset(epsn[:, :], RMS_EPS))
            link(pool, g.memset(ident[:, :], 0.0))
            g.affine_select(out=ident[:, :], in_=ident[:, :], compare_op=ALU.not_equal, fill=1.0, base=0,
                            pattern=[[-1, P]], channel_multiplier=1).then_inc(ident_ready, 1)
            pool.wait_ge(ident_ready, 1)
            link(pool, g.memset(ones[:, :], 1.0))
            link(pool, g.memset(headones[:, :], 0.0))
            link(pool, g.memset(eye[:, :], 0.0))
            for c in range(2):
                rows = slice(c * C, (c + 1) * C)
                link(pool, g.memset(headones[rows, rows], 1.0))
                link(pool, g.affine_select(out=eye[rows, :], in_=eye[rows, :], compare_op=ALU.not_equal, fill=1.0, base=0,
                                           pattern=[[-1, C]], channel_multiplier=1))
                for mask, op, pattern in ((m_inc, ALU.is_ge, [[1, C]]), (m_up, ALU.is_gt, [[1, C]]),
                                          (m_upo, ALU.is_gt, [[16, C // 16], [0, 16]])):
                    link(pool, g.affine_select(out=mask[rows, :], in_=ones[rows, 0:C], compare_op=op, fill=0.0, base=0,
                                               pattern=pattern, channel_multiplier=-1))
            link(pool, g.tensor_tensor(m_upd[:, :], m_up[:, :], m_upo[:, :], ALU.subtract))
            link(pool, g.memset(scanmask[:, :], 1.0))
            link(pool, g.memset(scanmask[:, :].rearrange("p (c t) -> p c t", t=C)[:, :, 0:1], 0.0))
            link(pool, g.memset(sel[0:GHV, :, :], 1.0))
            g.affine_select(out=sel[0:GHV, :, :], in_=sel[0:GHV, :, :], compare_op=ALU.is_equal, fill=0.0, base=0,
                            pattern=[[-1, GHV], [0, P]], channel_multiplier=1).then_inc(consts_ready, 1)

            def fetch(q, dst, loaded, *free):
                pool.wait_ge(sem("spooled"), 16 * (q + 1))
                for name, value in free:
                    pool.wait_ge(sem(name), value)
                g.dma_start(dst[:, :, :], proj[q].rearrange("(t p) c -> p t c", p=P)).then_inc(sem(loaded), 16)

            fetch(0, gs, "gs_loaded")
            fetch(2, zg, "z_loaded", ("g_out", 1))
            fetch(1, nat, "nat_loaded", ("g_out_turned", 1))
            store_y(pool, 8, 1)
            fetch(3, gs, "gs_loaded", ("mix_turned", 3))
            for hf in range(HALVES):
                cols = slice(hf * CW, (hf + 1) * CW)
                if hf == 0:
                    pool.wait_ge(sem("g_eg"), HALVES)
                    pool.wait_ge(sem("inv_dve"), INV_DVE * HALVES)
                else:
                    pool.wait_ge(sem("inv_dve"), INV_DVE * (HALVES + TT))
                g.memset(w2z[:, :], 0.0)
                g.memset(a2z[:, :], 0.0).then_inc(sem("lora_clear"), 1)
                pool.wait_ge(sem("lora_clear"), hf + 1)
                g.dma_start(w2z[0:LORA_D, :], A["rw_w2"][0][:, cols]).then_inc(sem("lora_loaded"), 16)
                g.dma_start(a2z[LORA_D:P, :], A["rw_a2"][0][:, cols]).then_inc(sem("lora_loaded"), 16)
                g.dma_start(g2a[:, :], A["rw_g2"][0][0:P, cols]).then_inc(sem("lora_loaded"), 16)
                g.dma_start(g2b[0:32, :], A["rw_g2"][0][P:LORA_G, cols]).then_inc(sem("lora_loaded"), 16)
                if hf == 0:
                    pool.wait_ge(sem("g_omm"), NCH * HALVES)
                    pool.wait_ge(sem("g_state"), (NCH + 1) * HALVES)
                    g.memset(az[:, :, :, :], 0.0)
                    g.memset(rz[:, :, :, :], 0.0).then_inc(sem("rw_clear"), 1)
                fetch(4 + 3 * hf, nat, "nat_loaded", ("g_out_turned", HALVES) if hf == 0 else ("r_out_turned", 1))
                store_y(pool, 12 if hf == 0 else 0, HALVES + hf)
                fetch(5 + 3 * hf, gs, "gs_loaded", ("mix_turned", 5 + 3 * hf))
                if hf == 0:
                    fetch(6, gs, "gs_loaded", ("r_var", 1))
            pool.wait_ge(sem("r_y"), NCH * HALVES)
            pool.wait_ge(sem("r_state"), (NCH + 1) * HALVES)
            pool.wait_ge(sem("y_stored"), 16 * (HALVES + 1))
            for tiles, loaded in ((slice(8, 16), "deltanet_loaded"), (slice(0, 4), "rwkv_loaded")):
                g.dma_start(yf[:, tiles, :], y_turned[tiles].rearrange("k p t -> p k t")).then_inc(sem(loaded), 16)
            for c in range(NDC):
                free = () if c == 0 else (("nat_ready", turns["merged"][0] + c),)
                if c == 0:
                    free = (("y_ready", 2 * HALVES),)
                fetch(9 + c, ga, "ga_loaded", *free)
                fetch(9 + NDC + c, gb, "gb_loaded", *free)
            pool.wait_ge(slot_used, prods["f2dn"][0]["slot"])
            g.dma_start(fgain[:, :], A["final_norm"].rearrange("(m d) -> m d", m=1).to_broadcast([P, D])).then_inc(sem("fgain_loaded"), 16)


        @block.sync
        def _(sp):
            for tt in range(TT):
                sp.dma_start(h[:, tt, :], A["x"][0, tt * P:(tt + 1) * P, :]).then_inc(x_loaded, 16)
            sp.wait_ge(prm_clear, 1)
            for name, src, m in prm_sources(A):
                r = PRM[name]
                sp.dma_start(nat[r % P:r % P + m, r // P, 0:src.shape[-1]], src).then_inc(prm_loaded, 16)
            for cell, name in ((dtb, "gdn_dt_bias"), (nal, "gdn_a_log")):
                sp.dma_start(cell, A[name][0].rearrange("(g m) -> g m", m=1)).then_inc(sem("gdn_loaded"), 16)
            ffn_load(sp, "f1", A["ffn1_w_gate"][0], A["ffn1_w_up"][0], A["ffn1_w_down"][0])

            def weights(w, cols, pr, rows0=0):
                for j in range(pr["ns"]):
                    rows = slice(rows0 + j * SK * P, rows0 + (j + 1) * SK * P)
                    load_slot(sp, w[rows, cols].rearrange("(k p) n -> p k n", p=P), pr["slot"], j)

            w_in = A["w_in"][0]
            for j in range(KT // SK):
                rows = slice(j * SK * P, (j + 1) * SK * P)
                s, n, _ = slot_of(AUX["slot"], j)
                sp.wait_ge(wlo_ready, n - RING + 1)
                for at_, c0, c1 in ((0, 3 * RW, RW_COLS), (LORA, BA0, GATE0)):
                    sp.dma_start(raw[:, s, :, at_:at_ + c1 - c0], w_in[rows, c0:c1].rearrange("(k p) n -> p k n", p=P)).then_inc(LOADED[s], 16)
            for hf in range(HALVES):
                g = prods[f"gdn{hf}"]
                for j in range(KT // SK):
                    rows = slice(j * SK * P, (j + 1) * SK * P)
                    s, n, _ = slot_of(g[0]["slot"], j)
                    sp.wait_ge(wlo_ready, n - RING + 1)
                    for at_, c0 in ((0, GDN0 + hf * 256), (256, GDN0 + GQ + hf * 256)):
                        sp.dma_start(raw[:, s, :, at_:at_ + 256], w_in[rows, c0:c0 + 256].rearrange("(k p) n -> p k n", p=P)).then_inc(LOADED[s], 16)
                for m, c0 in ((1, GDN0 + 2 * GQ), (2, Z0)):
                    weights(w_in, slice(c0 + hf * CW, c0 + (hf + 1) * CW), g[m])
            for hf in range(HALVES):
                for m in range(3):
                    weights(w_in, slice(m * RW + hf * CW, m * RW + (hf + 1) * CW), prods[f"rw{hf}"][m])
            for c in range(2 * NDC):
                weights(w_in, slice(GATE0 + c * CW, GATE0 + (c + 1) * CW), prods["gates"][c])
            for c in range(NDC):
                for m in range(2):
                    weights(A["w_lift"][0, 1 - m], slice(c * CW, (c + 1) * CW), prods["lift"][2 * c + m])
                if c == 0:
                    sp.wait_ge(sem("y_split"), 2)
                    for tt in range(TT):
                        sp.dma_start(msb[:, tt, :], A["mem"][0, tt * P:(tt + 1) * P, :]).then_inc(sem("mem_loaded"), 16)
            for phase, ws in (("out", ("w_out",)), ("mkv", ("w_mk", "w_mv")), ("mq", ("w_mq",)), ("mo", ("w_mo",))):
                for m, w in enumerate(ws):
                    for c in range(NDC):
                        weights(A[w][0], slice(c * CW, (c + 1) * CW), prods[phase][NDC * m + c])
            ffn_load(sp, "f2", A["ffn2_w_gate"][0], A["ffn2_w_up"][0], A["ffn2_w_down"][0])
            for c in range(NDC):
                sp.wait_ge(sem("out_ready"), c + 1)
                sp.dma_start(A["out"][0].rearrange("(t p) d -> p t d", p=P)[:, :, c * CW:(c + 1) * CW],
                             h[:, :, c * CW:(c + 1) * CW]).then_inc(stored, 16)
            sp.wait_ge(stored, 16 * NDC)

        @block.scalar
        def _(act):
            act.wait_ge(x_loaded, 16 * TT)
            for c in range(NDC):
                sumsq(act, h, 0, c)
            next_hi(act, "f1gu")
            act.wait_ge(ident_ready, 1)
            act.wait_ge(prm_turned, 1)
            norm_act(act, 0, h, "f1norm", prods["f1gu"][0])
            ffn_act(act, "f1")
            for j in range(RING):
                split_hi(act, AUX["slot"], j, width=AUXW)
            last_sumsq(act, prods["f1dn"][3], 1)
            norm_act(act, 1, h, "mixnorm", AUX, AUXW)
            for j in range(EARLY, KT // SK):
                split_hi(act, AUX["slot"], j, width=AUXW)
            next_hi(act, "gdn0")
            aux_act(act)
            for hf in range(HALVES):
                gdn_act(act, hf)
            for hf in range(HALVES):
                rw_act(act, hf)
            lift_act(act)
            attn_act(act)
            next_hi(act, "f2gu")
            last_sumsq(act, prods["mo"][3], 4)
            norm_act(act, 4, h, "f2norm", prods["f2gu"][0])
            ffn_act(act, "f2")
            last_sumsq(act, prods["f2dn"][3], 5)
            norm_root(act, 5)

        @block.vector
        def _(dve):
            dve.wait_ge(prm_turned, 1)
            nc.vector.tensor_copy(prm[:, 0:NPRM], pb[:, :, :].rearrange("p a b -> p (a b)")[:, 0:NPRM]).then_inc(prm_ready, 1)
            dve.wait_ge(prm_ready, 1)
            next_lo(dve, "f1gu")
            norm_dve(dve, 0, "f1norm", "ffn1_norm", prods["f1gu"][0])
            ffn_dve(dve, "f1")
            for j in range(RING):
                split_lo(dve, AUX["slot"], j, width=AUXW)
            residual(dve, prods["f1dn"][3], 3, 0.5)
            norm_dve(dve, 1, "mixnorm", "mix_norm", AUX, AUXW)
            for j in range(EARLY, KT // SK):
                split_lo(dve, AUX["slot"], j, width=AUXW)
            next_lo(dve, "gdn0")
            aux_dve(dve)
            for hf in range(HALVES):
                gdn_dve(dve, hf)
            for hf in range(HALVES):
                rw_dve(dve, hf)
            lift_dve(dve)
            attn_dve(dve)
            next_lo(dve, "f2gu")
            residual(dve, prods["mo"][3], 3, 1.0)
            norm_dve(dve, 4, "f2norm", "ffn2_norm", prods["f2gu"][0])
            ffn_dve(dve, "f2")
            residual(dve, prods["f2dn"][3], 3, 0.5)
            norm_scale(dve, 5)
            dve.wait_ge(sem("fgain_loaded"), 16)
            for c in range(NDC):
                cols = slice(c * CW, (c + 1) * CW)
                for tt in range(TT):
                    op = nc.vector.scalar_tensor_tensor(h[:, tt, cols], h[:, tt, cols], rstd[:, tt:tt + 1], fgain[:, cols], ALU.mult, ALU.mult)
                op.then_inc(sem("out_ready"), 1)

        @block.tensor
        def _(pe):
            pe.wait_ge(ident_ready, 1)
            pe.wait_ge(prm_loaded, 16 * len(PRM))
            for g in range(2):
                mm = nc.tensor.transpose(pb[:, g // 2, g * P:(g + 1) * P], nat[:, g, 0:P], ident[:, :])
            mm.then_inc(prm_turned, 1)
            ffn_pe(pe, "f1")
            aux_pe(pe)
            for hf in range(HALVES):
                gdn_pe(pe, hf)
            for hf in range(HALVES):
                rw_pe(pe, hf)
            lift_pe(pe)
            attn_pe(pe)
            ffn_pe(pe, "f2")


def prm_sources(A):
    def rows(v):
        return v.rearrange("(m p) -> m p", p=P)

    mu = A["rw_shift_mu"][0]
    wide = 3 * RW
    out = [("ffn1_norm", rows(A["ffn1_norm"][0]), KT), ("mix_norm", rows(A["mix_norm"][0]), KT),
           ("mem_q_norm", rows(A["mem_q_norm"][0]), KT), ("mem_kv_norm", rows(A["mem_kv_norm"][0]), KT),
           ("ffn2_norm", rows(A["ffn2_norm"][0]), KT), ("mu_rkv", rows(mu[0:wide]), wide // P),
           ("mu_wa", rows(mu[wide:wide + P]), 1), ("mu_g0", rows(mu[wide + P:wide + 2 * P]), 1),
           ("mu_g1", mu[wide + 2 * P:RW_COLS].rearrange("(m p) -> m p", m=1), 1)]
    for name in ("w0", "a0", "k_k", "k_a", "ln_w", "ln_b"):
        out.append((name, rows(A["rw_" + name][0]), RW // P))
    out.append(("r_k", A["rw_r_k"][0].rearrange("(m a) n -> m (a n)", a=2), RW // P))
    out.append(("conv", A["gdn_conv_w"][0].rearrange("k (m p) -> (k m) p", p=P), CONV * 16))
    out.append(("gdn_norm", A["gdn_norm_w"][0].rearrange("(m p) -> m p", m=1), 1))
    return out


_INS = ['x', 'mem', 'ffn1_norm', 'ffn1_w_gate', 'ffn1_w_up', 'ffn1_w_down', 'mix_norm', 'w_in', 'rw_shift_mu', 'rw_w0',
        'rw_w2', 'rw_a0', 'rw_a2', 'rw_g2', 'rw_k_k', 'rw_k_a', 'rw_r_k', 'rw_ln_w', 'rw_ln_b', 'gdn_conv_w',
        'gdn_a_log', 'gdn_dt_bias', 'gdn_norm_w', 'w_lift', 'w_out', 'mem_q_norm', 'mem_kv_norm', 'w_mq', 'w_mk',
        'w_mv', 'w_mo', 'ffn2_norm', 'ffn2_w_gate', 'ffn2_w_up', 'ffn2_w_down', 'final_norm']


def kernel(**inputs):
    import numpy as np
    import concourse.bacc as bacc
    from concourse.bass_utils import run_bass_kernel_spmd

    nc = bacc.Bacc("TRN2", target_bir_lowering=False, num_devices=1)
    arrays, aps = {}, {}
    for name in _INS:
        a = np.ascontiguousarray(inputs[name])
        arrays[f"in_{name}"] = a
        aps[name] = nc.dram_tensor(f"in_{name}", a.shape, mybir.dt.from_np(a.dtype), kind="ExternalInput").ap()
    aps["out"] = nc.dram_tensor("out", (1, T, D), F32, kind="ExternalOutput").ap()
    build(nc, aps)
    r = run_bass_kernel_spmd(nc, [arrays], core_ids=[0])
    return np.asarray(r.results[0]["out"])
```
